# Optimizing a Trainium2 kernel written in Bass

```python
import math
import jax, jax.numpy as jnp
from jax import lax
import numpy as np

D_MODEL = 1024
BATCH = 1
SEQ = 256
DEPTH = 1

MIX_WIDTH = D_MODEL
SGU_GROUPS = 4
SGU_CH = D_MODEL // 8
SGU_WIDTH = SGU_GROUPS * SGU_CH
CHUNK = 128
DIFF_HEADS = 4
DIFF_QK_DIM = D_MODEL // 16
DIFF_V_DIM = 2 * DIFF_QK_DIM
DIFF_QK_WIDTH = DIFF_HEADS * 2 * DIFF_QK_DIM
DIFF_WIDTH = DIFF_HEADS * DIFF_V_DIM
Q_BLOCK = 128
IN_WIDTH = 2 * SGU_WIDTH + 2 * DIFF_QK_WIDTH + DIFF_WIDTH
MEM_LEN = 256
MEM_HEADS = 4
MEM_HEAD_DIM = D_MODEL // MEM_HEADS
MEM_WIDTH = MEM_HEADS * MEM_HEAD_DIM
N_GROUPS = 4
EXPERTS_PER_GROUP = 8
N_EXPERTS = N_GROUPS * EXPERTS_PER_GROUP
TOP_K = 2
D_EXPERT = D_MODEL // 2
EXPERT_BLOCK = 128
RMS_EPS = 1e-6
LN_EPS = 1e-5


def rms_norm(x, g, eps=RMS_EPS):
    xf = x.astype(jnp.float32)
    y = xf * lax.rsqrt(jnp.mean(xf * xf, axis=-1, keepdims=True) + eps)
    return (y * g.astype(jnp.float32)).astype(x.dtype)

def layer_norm(x, g, b, eps=LN_EPS):
    xf = x.astype(jnp.float32)
    mu = jnp.mean(xf, axis=-1, keepdims=True)
    var = jnp.mean(jnp.square(xf - mu), axis=-1, keepdims=True)
    y = (xf - mu) * lax.rsqrt(var + eps)
    return (y * g.astype(jnp.float32) + b.astype(jnp.float32)).astype(x.dtype)

def chunked_sgu(u, v, ln_g, ln_b, w_s, b_s):
    Bn, Sn, G, C = v.shape
    vn = layer_norm(v, ln_g, ln_b)
    vc = vn.reshape(Bn, Sn // CHUNK, CHUNK, G, C)
    ws = jnp.tril(w_s).astype(vc.dtype)
    sp = jnp.einsum('gts,bnsgc->bntgc', ws, vc) + b_s.T.astype(vc.dtype)[:, :, None]
    return u * sp.reshape(Bn, Sn, G, C)

def diff_attention(q, k, v, lam):
    Bn, H, _, Sn, Dq = q.shape
    n_qb = Sn // Q_BLOCK
    slopes = 2.0 ** (-8.0 * jnp.arange(1, H + 1, dtype=jnp.float32) / H)
    q_blocks = jnp.moveaxis(q.reshape(Bn, H, 2, n_qb, Q_BLOCK, Dq), 3, 0)
    kpos = jnp.arange(Sn, dtype=jnp.int32)

    def attend(args):
        qb, i = args
        s = jnp.einsum('bhiqd,bhikd->bhiqk', qb, k).astype(jnp.float32)
        qpos = i * Q_BLOCK + jnp.arange(Q_BLOCK, dtype=jnp.int32)
        dist = (qpos[:, None] - kpos[None, :]).astype(jnp.float32)
        s = s - (slopes[:, None, None] * dist)[None, :, None]
        s = jnp.where(dist >= 0, s, -jnp.inf)
        p = jax.nn.softmax(s, axis=-1)
        a = p[:, :, 0] - lam * p[:, :, 1]
        return jnp.einsum('bhqk,bhkd->bqhd', a.astype(v.dtype), v)

    o = lax.map(attend, (q_blocks, jnp.arange(n_qb, dtype=jnp.int32)))
    return jnp.moveaxis(o, 0, 1).reshape(Bn, Sn, H, v.shape[-1])

def memory_attention(hq, mem_n, w_q, w_kv, w_o):
    Bn, Sn, _ = hq.shape
    Mn = mem_n.shape[1]
    q = (hq @ w_q).reshape(Bn, Sn, MEM_HEADS, MEM_HEAD_DIM) * (MEM_HEAD_DIM ** -0.5)
    kv = (mem_n @ w_kv).reshape(Bn, Mn, 2, MEM_HEADS, MEM_HEAD_DIM)
    k, v = kv[:, :, 0], kv[:, :, 1]
    s = jnp.einsum('bqhd,bkhd->bhqk', q, k).astype(jnp.float32)
    p = jax.nn.softmax(s, axis=-1)
    o = jnp.einsum('bhqk,bkhd->bqhd', p.astype(v.dtype), v).reshape(Bn, Sn, MEM_WIDTH)
    return o @ w_o

def hierarchical_moe(h, w_rg, b_rg, w_re, b_re, w_gate, w_up, w_down):
    Bn, Sn, D = h.shape
    t = h.reshape(-1, D)
    N = t.shape[0]
    pg = jax.nn.softmax((t @ w_rg + b_rg).astype(jnp.float32), axis=-1)
    gate_g, gidx = lax.top_k(pg, 1)
    el = (t @ w_re + b_re).astype(jnp.float32).reshape(N, N_GROUPS, EXPERTS_PER_GROUP)
    el = el[jnp.arange(N), gidx[:, 0]]
    pe = jax.nn.softmax(el, axis=-1)
    pe_top, eloc = lax.top_k(pe, TOP_K)
    wts = gate_g * pe_top / jnp.sum(pe_top, axis=-1, keepdims=True)
    eid = (gidx * EXPERTS_PER_GROUP + eloc).reshape(-1)
    A = N * TOP_K
    tok = jnp.repeat(jnp.arange(N, dtype=jnp.int32), TOP_K)
    order = jnp.argsort(eid)
    e_sorted = eid[order]
    counts = jnp.bincount(eid, length=N_EXPERTS)
    starts = jnp.cumsum(counts) - counts
    padded = (counts + EXPERT_BLOCK - 1) // EXPERT_BLOCK * EXPERT_BLOCK
    pend = jnp.cumsum(padded)
    pstarts = pend - padded
    pos_sorted = (pstarts[e_sorted] + jnp.arange(A, dtype=jnp.int32) - starts[e_sorted]).astype(jnp.int32)
    P = -(-A // EXPERT_BLOCK) * EXPERT_BLOCK + N_EXPERTS * EXPERT_BLOCK
    n_blocks = P // EXPERT_BLOCK
    row_tok = jnp.zeros((P,), jnp.int32).at[pos_sorted].set(tok[order])
    block_expert = jnp.clip(jnp.searchsorted(pend, jnp.arange(n_blocks, dtype=jnp.int32) * EXPERT_BLOCK,
                                             side='right'), 0, N_EXPERTS - 1).astype(jnp.int32)
    x_rows = t[row_tok].reshape(n_blocks, EXPERT_BLOCK, D)

    def expert_rows(args):
        xb, e = args
        g = xb @ w_gate[e]
        u = xb @ w_up[e]
        return (jax.nn.silu(g) * u) @ w_down[e]

    y_rows = lax.map(expert_rows, (x_rows, block_expert)).reshape(P, D)
    pos = jnp.zeros((A,), jnp.int32).at[order].set(pos_sorted)
    y = y_rows[pos].reshape(N, TOP_K, D)
    out = jnp.einsum('nk,nkd->nd', wts.astype(y.dtype), y)
    return out.reshape(Bn, Sn, D)

def first_inputs(seed: int = 0) -> dict:
    key = jax.random.key(seed)
    ks = jax.random.split(key, 32)
    L, D = DEPTH, D_MODEL
    f32 = jnp.float32

    def nrm(k, shape, scale):
        return jax.random.normal(k, shape, f32) * scale

    def gain(k, shape):
        return 1.0 + 0.05 * jax.random.normal(k, shape, f32)

    return {
        "x": jax.random.normal(ks[0], (BATCH, SEQ, D), f32),
        "mem": jax.random.normal(ks[1], (BATCH, MEM_LEN, D), f32),
        "norm_mix": gain(ks[2], (L, D)),
        "w_in": nrm(ks[3], (L, D, IN_WIDTH), D ** -0.5),
        "sgu_ln_g": gain(ks[4], (L, SGU_GROUPS, SGU_CH)),
        "sgu_ln_b": nrm(ks[5], (L, SGU_GROUPS, SGU_CH), 0.02),
        "sgu_w": nrm(ks[6], (L, SGU_GROUPS, CHUNK, CHUNK), CHUNK ** -0.5),
        "sgu_b": gain(ks[7], (L, SGU_GROUPS, CHUNK)),
        "lambda_q1": nrm(ks[8], (L, DIFF_QK_DIM), 0.1),
        "lambda_k1": nrm(ks[9], (L, DIFF_QK_DIM), 0.1),
        "lambda_q2": nrm(ks[10], (L, DIFF_QK_DIM), 0.1),
        "lambda_k2": nrm(ks[11], (L, DIFF_QK_DIM), 0.1),
        "diff_subln": gain(ks[12], (L, DIFF_V_DIM)),
        "w_out": nrm(ks[13], (L, MIX_WIDTH, D), MIX_WIDTH ** -0.5),
        "norm_xq": gain(ks[14], (L, D)),
        "norm_mem": gain(ks[15], (L, D)),
        "w_q_mem": nrm(ks[16], (L, D, MEM_WIDTH), D ** -0.5),
        "w_kv_mem": nrm(ks[17], (L, D, 2 * MEM_WIDTH), D ** -0.5),
        "w_o_mem": nrm(ks[18], (L, MEM_WIDTH, D), MEM_WIDTH ** -0.5),
        "norm_ffn": gain(ks[19], (L, D)),
        "w_router_group": nrm(ks[20], (L, D, N_GROUPS), D ** -0.5),
        "b_router_group": nrm(ks[21], (L, N_GROUPS), 0.01),
        "w_router_expert": nrm(ks[22], (L, D, N_EXPERTS), D ** -0.5),
        "b_router_expert": nrm(ks[23], (L, N_EXPERTS), 0.01),
        "w_gate": nrm(ks[24], (L, N_EXPERTS, D, D_EXPERT), D ** -0.5),
        "w_up": nrm(ks[25], (L, N_EXPERTS, D, D_EXPERT), D ** -0.5),
        "w_down": nrm(ks[26], (L, N_EXPERTS, D_EXPERT, D), D_EXPERT ** -0.5),
        "norm_final": gain(ks[27], (D,)),
    }

def first_block(x, mem, norm_mix, w_in, sgu_ln_g, sgu_ln_b, sgu_w, sgu_b, lambda_q1, lambda_k1, lambda_q2,
              lambda_k2, diff_subln, w_out, norm_xq, norm_mem, w_q_mem, w_kv_mem, w_o_mem, norm_ffn,
              w_router_group, b_router_group, w_router_expert, b_router_expert, w_gate, w_up, w_down,
              norm_final):
    Bn, Sn, _ = x.shape
    cuts = [SGU_WIDTH, 2 * SGU_WIDTH, 2 * SGU_WIDTH + DIFF_QK_WIDTH, 2 * SGU_WIDTH + 2 * DIFF_QK_WIDTH]
    for l in range(DEPTH):
        lambda_init = 0.8 - 0.6 * math.exp(-0.3 * l)
        h = rms_norm(x, norm_mix[l])
        z = h @ w_in[l]
        zu, zv, zq, zk, zval = jnp.split(z, cuts, axis=-1)
        u = jax.nn.gelu(zu, approximate=False).reshape(Bn, Sn, SGU_GROUPS, SGU_CH)
        v = jax.nn.gelu(zv, approximate=False).reshape(Bn, Sn, SGU_GROUPS, SGU_CH)
        a_out = chunked_sgu(u, v, sgu_ln_g[l], sgu_ln_b[l], sgu_w[l], sgu_b[l]).reshape(Bn, Sn, SGU_WIDTH)
        q = zq.reshape(Bn, Sn, DIFF_HEADS, 2, DIFF_QK_DIM).transpose(0, 2, 3, 1, 4) * (DIFF_QK_DIM ** -0.5)
        k = zk.reshape(Bn, Sn, DIFF_HEADS, 2, DIFF_QK_DIM).transpose(0, 2, 3, 1, 4)
        vv = zval.reshape(Bn, Sn, DIFF_HEADS, DIFF_V_DIM).transpose(0, 2, 1, 3)
        lam = (jnp.exp(jnp.sum(lambda_q1[l].astype(jnp.float32) * lambda_k1[l].astype(jnp.float32)))
               - jnp.exp(jnp.sum(lambda_q2[l].astype(jnp.float32) * lambda_k2[l].astype(jnp.float32)))
               + lambda_init)
        o = diff_attention(q, k, vv, lam)
        o = rms_norm(o, diff_subln[l]) * (1.0 - lambda_init)
        mixed = jnp.concatenate([a_out, o.reshape(Bn, Sn, DIFF_WIDTH)], axis=-1) @ w_out[l]
        x = x + mixed
        x = x + memory_attention(rms_norm(x, norm_xq[l]), rms_norm(mem, norm_mem[l]),
                                 w_q_mem[l], w_kv_mem[l], w_o_mem[l])
        x = x + hierarchical_moe(rms_norm(x, norm_ffn[l]), w_router_group[l], b_router_group[l],
                                 w_router_expert[l], b_router_expert[l], w_gate[l], w_up[l], w_down[l])
    return rms_norm(x, norm_final)


DEPTH_2 = 2

N_A_LAYERS = (DEPTH_2 + 1) // 2
N_B_LAYERS = DEPTH_2 - N_A_LAYERS
HEAD_DIM = 64
MEM_WIDTH_2 = MEM_HEADS * HEAD_DIM
PRIMARY_WIDTH = D_MODEL - MEM_WIDTH_2
B_HEADS = PRIMARY_WIDTH // HEAD_DIM
CONV_CH = PRIMARY_WIDTH
CONV_WIDTH = 31
D_FF = 256 * ((8 * D_MODEL // 3 + 255) // 256)
MOBA_BLOCK = 256
MOBA_TOPK = 3
Q_CHUNK = 16
ROPE_THETA = 500000.0
ROPE_DIM = HEAD_DIM // 4
EPS = 1e-6


def rms_norm_2(x, g):
    xf = x.astype(jnp.float32)
    y = xf * lax.rsqrt(jnp.mean(xf * xf, axis=-1, keepdims=True) + EPS)
    return (y * g.astype(jnp.float32)).astype(x.dtype)

def layer_norm_2(x, g, b):
    xf = x.astype(jnp.float32)
    xc = xf - jnp.mean(xf, axis=-1, keepdims=True)
    y = xc * lax.rsqrt(jnp.mean(xc * xc, axis=-1, keepdims=True) + EPS)
    return (y * g.astype(jnp.float32) + b.astype(jnp.float32)).astype(x.dtype)

def swiglu(x, w_gate, w_up, w_down):
    return (jax.nn.silu(x @ w_gate) * (x @ w_up)) @ w_down

def partial_rope(x, positions):
    half = ROPE_DIM // 2
    inv_freq = 1.0 / (ROPE_THETA ** (jnp.arange(0, ROPE_DIM, 2, dtype=jnp.float32) / ROPE_DIM))
    ang = positions.astype(jnp.float32)[..., None] * inv_freq
    cos = jnp.cos(ang)[:, :, None, :]
    sin = jnp.sin(ang)[:, :, None, :]
    xr = x[..., :ROPE_DIM].astype(jnp.float32)
    x1, x2 = xr[..., :half], xr[..., half:]
    rot = jnp.concatenate([x1 * cos - x2 * sin, x2 * cos + x1 * sin], axis=-1)
    return jnp.concatenate([rot.astype(x.dtype), x[..., ROPE_DIM:]], axis=-1)

def conformer_conv(u, dw_kernel, dw_bias, ln_g, ln_b):
    a, gate = jnp.split(u, 2, axis=-1)
    h = a * jax.nn.sigmoid(gate)
    h = lax.conv_general_dilated(h, dw_kernel.astype(h.dtype), window_strides=(1,),
                                 padding=[(CONV_WIDTH - 1, 0)],
                                 dimension_numbers=('NWC', 'WIO', 'NWC'),
                                 feature_group_count=CONV_CH) + dw_bias
    return jax.nn.silu(layer_norm_2(h, ln_g, ln_b))

def memory_attention_2(q, mem_n, w_mem_kv, q_g, k_g):
    B, S = q.shape[:2]
    M = mem_n.shape[1]
    k, v = jnp.split(mem_n @ w_mem_kv, 2, axis=-1)
    k = rms_norm_2(k.reshape(B, M, MEM_HEADS, HEAD_DIM), k_g)
    v = v.reshape(B, M, MEM_HEADS, HEAD_DIM)
    q = rms_norm_2(q.reshape(B, S, MEM_HEADS, HEAD_DIM), q_g)
    logits = jnp.einsum('bshd,bmhd->bhsm', q, k).astype(jnp.float32) * (HEAD_DIM ** -0.5)
    p = jax.nn.softmax(logits, axis=-1).astype(v.dtype)
    return jnp.einsum('bhsm,bmhd->bshd', p, v).reshape(B, S, MEM_WIDTH_2)

def shared_moba_kv(h, positions, kv_norm_g, w_kv, k_norm_g):
    B, S, _ = h.shape
    k, v = jnp.split(rms_norm_2(h, kv_norm_g) @ w_kv, 2, axis=-1)
    k = partial_rope(rms_norm_2(k.reshape(B, S, B_HEADS, HEAD_DIM), k_norm_g), positions)
    v = v.reshape(B, S, B_HEADS, HEAD_DIM)
    n_blocks = -(-S // MOBA_BLOCK)
    pad = n_blocks * MOBA_BLOCK - S

    def to_blocks(t):
        t = jnp.pad(t, ((0, 0), (0, pad), (0, 0), (0, 0)))
        return t.reshape(B, n_blocks, MOBA_BLOCK, B_HEADS, HEAD_DIM).transpose(0, 3, 1, 2, 4)

    k_blocks = to_blocks(k)
    v_blocks = to_blocks(v)
    k_mean = jnp.mean(k_blocks.astype(jnp.float32), axis=3).astype(k_blocks.dtype)
    return k_blocks, v_blocks, k_mean

def moba_attention(q, k_blocks, v_blocks, k_mean):
    B, S, H, Dh = q.shape
    n_blocks = k_blocks.shape[2]
    topk = min(MOBA_TOPK, n_blocks)
    n_chunks = S // Q_CHUNK
    scale = Dh ** -0.5
    q_chunks = q.reshape(B, n_chunks, Q_CHUNK, H, Dh).transpose(1, 0, 3, 2, 4)
    b_idx = jnp.arange(B)[:, None, None, None]
    h_idx = jnp.arange(H)[None, :, None, None]

    def chunk_attend(args):
        q_c, c = args
        start = c * Q_CHUNK
        own = start // MOBA_BLOCK
        gate = jnp.einsum('bhqd,bhnd->bhqn', q_c, k_mean).astype(jnp.float32)
        gate = jnp.where(jnp.arange(n_blocks) < own, gate, -jnp.inf)
        _, sel = lax.top_k(gate, topk)
        valid = jnp.arange(topk) < own
        k_sel = k_blocks[b_idx, h_idx, sel]
        v_sel = v_blocks[b_idx, h_idx, sel]
        k_own = lax.dynamic_index_in_dim(k_blocks, own, axis=2, keepdims=False)
        v_own = lax.dynamic_index_in_dim(v_blocks, own, axis=2, keepdims=False)
        s_sel = jnp.einsum('bhqd,bhqnjd->bhqnj', q_c, k_sel).astype(jnp.float32) * scale
        s_sel = jnp.where(valid[:, None], s_sel, -jnp.inf)
        s_own = jnp.einsum('bhqd,bhjd->bhqj', q_c, k_own).astype(jnp.float32) * scale
        q_pos = start + jnp.arange(Q_CHUNK)
        k_pos = own * MOBA_BLOCK + jnp.arange(MOBA_BLOCK)
        s_own = jnp.where(k_pos[None, :] <= q_pos[:, None], s_own, -jnp.inf)
        logits = jnp.concatenate([s_sel.reshape(B, H, Q_CHUNK, topk * MOBA_BLOCK), s_own], axis=-1)
        p = jax.nn.softmax(logits, axis=-1).astype(v_blocks.dtype)
        p_sel = p[..., :topk * MOBA_BLOCK].reshape(B, H, Q_CHUNK, topk, MOBA_BLOCK)
        p_own = p[..., topk * MOBA_BLOCK:]
        return (jnp.einsum('bhqnj,bhqnjd->bhqd', p_sel, v_sel)
                + jnp.einsum('bhqj,bhjd->bhqd', p_own, v_own))

    out = lax.map(chunk_attend, (q_chunks, jnp.arange(n_chunks)))
    return out.transpose(1, 0, 3, 2, 4).reshape(B, S, H * Dh)

def second_inputs(seed: int = 0) -> dict:
    key = jax.random.key(seed)
    it = iter(jax.random.split(key, 64))

    def w(shape, fan_in):
        return jax.random.normal(next(it), shape, jnp.float32) * fan_in ** -0.5

    def gain(shape):
        return 1.0 + 0.01 * jax.random.normal(next(it), shape, jnp.float32)

    def bias(shape):
        return 0.01 * jax.random.normal(next(it), shape, jnp.float32)

    x = jax.random.normal(next(it), (BATCH, SEQ, D_MODEL), jnp.float32)
    mem = jax.random.normal(next(it), (BATCH, 256, D_MODEL), jnp.float32)
    offsets = jax.random.randint(next(it), (BATCH, 1), 0, 8192, dtype=jnp.int32)
    positions = (offsets + jnp.arange(SEQ, dtype=jnp.int32)[None, :]).astype(jnp.int32)
    return {
        'x': x, 'mem': mem, 'positions': positions,
        'ffn1_norm_g': gain((DEPTH_2, D_MODEL)),
        'ffn1_w_gate': w((DEPTH_2, D_MODEL, D_FF), D_MODEL),
        'ffn1_w_up': w((DEPTH_2, D_MODEL, D_FF), D_MODEL),
        'ffn1_w_down': w((DEPTH_2, D_FF, D_MODEL), D_FF),
        'mix_norm_g': gain((DEPTH_2, D_MODEL)),
        'mem_norm_g': gain((DEPTH_2, D_MODEL)),
        'w_mem_kv': w((DEPTH_2, D_MODEL, 2 * MEM_WIDTH_2), D_MODEL),
        'mem_q_norm_g': gain((DEPTH_2, HEAD_DIM)),
        'mem_k_norm_g': gain((DEPTH_2, HEAD_DIM)),
        'w_o': w((DEPTH_2, PRIMARY_WIDTH + MEM_WIDTH_2, D_MODEL), PRIMARY_WIDTH + MEM_WIDTH_2),
        'ffn2_norm_g': gain((DEPTH_2, D_MODEL)),
        'ffn2_w_gate': w((DEPTH_2, D_MODEL, D_FF), D_MODEL),
        'ffn2_w_up': w((DEPTH_2, D_MODEL, D_FF), D_MODEL),
        'ffn2_w_down': w((DEPTH_2, D_FF, D_MODEL), D_FF),
        'a_w_in': w((N_A_LAYERS, D_MODEL, 2 * CONV_CH + MEM_WIDTH_2), D_MODEL),
        'a_dw_kernel': w((N_A_LAYERS, CONV_WIDTH, 1, CONV_CH), CONV_WIDTH),
        'a_dw_bias': bias((N_A_LAYERS, CONV_CH)),
        'a_ln_g': gain((N_A_LAYERS, CONV_CH)),
        'a_ln_b': bias((N_A_LAYERS, CONV_CH)),
        'kv_norm_g': gain((D_MODEL,)),
        'w_kv': w((D_MODEL, 2 * PRIMARY_WIDTH), D_MODEL),
        'k_norm_g': gain((HEAD_DIM,)),
        'b_w_in': w((N_B_LAYERS, D_MODEL, PRIMARY_WIDTH + MEM_WIDTH_2), D_MODEL),
        'b_q_norm_g': gain((N_B_LAYERS, HEAD_DIM)),
    }

def second_block(x, mem, positions, ffn1_norm_g, ffn1_w_gate, ffn1_w_up, ffn1_w_down,
              mix_norm_g, mem_norm_g, w_mem_kv, mem_q_norm_g, mem_k_norm_g, w_o,
              ffn2_norm_g, ffn2_w_gate, ffn2_w_up, ffn2_w_down,
              a_w_in, a_dw_kernel, a_dw_bias, a_ln_g, a_ln_b,
              kv_norm_g, w_kv, k_norm_g, b_w_in, b_q_norm_g):
    B, S, _ = x.shape
    h = x
    shared_kv = None
    for layer in range(DEPTH_2):
        if layer == N_A_LAYERS:
            shared_kv = shared_moba_kv(h, positions, kv_norm_g, w_kv, k_norm_g)
        h = h + 0.5 * swiglu(rms_norm_2(h, ffn1_norm_g[layer]), ffn1_w_gate[layer],
                             ffn1_w_up[layer], ffn1_w_down[layer])
        hn = rms_norm_2(h, mix_norm_g[layer])
        if layer < N_A_LAYERS:
            u = hn @ a_w_in[layer]
            primary = conformer_conv(u[..., :2 * CONV_CH], a_dw_kernel[layer], a_dw_bias[layer],
                                     a_ln_g[layer], a_ln_b[layer])
            q_mem = u[..., 2 * CONV_CH:]
        else:
            j = layer - N_A_LAYERS
            u = hn @ b_w_in[j]
            q = rms_norm_2(u[..., :PRIMARY_WIDTH].reshape(B, S, B_HEADS, HEAD_DIM), b_q_norm_g[j])
            k_blocks, v_blocks, k_mean = shared_kv
            primary = moba_attention(partial_rope(q, positions), k_blocks, v_blocks, k_mean)
            q_mem = u[..., PRIMARY_WIDTH:]
        mem_out = memory_attention_2(q_mem, rms_norm_2(mem, mem_norm_g[layer]), w_mem_kv[layer],
                                   mem_q_norm_g[layer], mem_k_norm_g[layer])
        h = h + jnp.concatenate([primary, mem_out], axis=-1) @ w_o[layer]
        h = h + 0.5 * swiglu(rms_norm_2(h, ffn2_norm_g[layer]), ffn2_w_gate[layer],
                             ffn2_w_up[layer], ffn2_w_down[layer])
    return h


def setup_inputs(seed=0):
    out = dict(first_inputs(seed))
    for name, value in second_inputs(seed + 1).items():
        if name != "x":
            out[name + "_2"] = value
    return out


def reference(
    x, mem, norm_mix, w_in, sgu_ln_g, sgu_ln_b, sgu_w, sgu_b, lambda_q1, lambda_k1, lambda_q2,
    lambda_k2, diff_subln, w_out, norm_xq, norm_mem, w_q_mem, w_kv_mem, w_o_mem, norm_ffn,
    w_router_group, b_router_group, w_router_expert, b_router_expert, w_gate, w_up, w_down,
    norm_final, mem_2, positions_2, ffn1_norm_g_2, ffn1_w_gate_2, ffn1_w_up_2, ffn1_w_down_2,
    mix_norm_g_2, mem_norm_g_2, w_mem_kv_2, mem_q_norm_g_2, mem_k_norm_g_2, w_o_2,
    ffn2_norm_g_2, ffn2_w_gate_2, ffn2_w_up_2, ffn2_w_down_2, a_w_in_2, a_dw_kernel_2,
    a_dw_bias_2, a_ln_g_2, a_ln_b_2, kv_norm_g_2, w_kv_2, k_norm_g_2, b_w_in_2, b_q_norm_g_2,
):
    x = first_block(
        x, mem, norm_mix, w_in, sgu_ln_g, sgu_ln_b, sgu_w, sgu_b, lambda_q1, lambda_k1,
        lambda_q2, lambda_k2, diff_subln, w_out, norm_xq, norm_mem, w_q_mem, w_kv_mem, w_o_mem,
        norm_ffn, w_router_group, b_router_group, w_router_expert, b_router_expert, w_gate,
        w_up, w_down, norm_final,
    )
    return second_block(
        x, mem_2, positions_2, ffn1_norm_g_2, ffn1_w_gate_2, ffn1_w_up_2, ffn1_w_down_2,
        mix_norm_g_2, mem_norm_g_2, w_mem_kv_2, mem_q_norm_g_2, mem_k_norm_g_2, w_o_2,
        ffn2_norm_g_2, ffn2_w_gate_2, ffn2_w_up_2, ffn2_w_down_2, a_w_in_2, a_dw_kernel_2,
        a_dw_bias_2, a_ln_g_2, a_ln_b_2, kv_norm_g_2, w_kv_2, k_norm_g_2, b_w_in_2,
        b_q_norm_g_2,
    )


_drawn_inputs = setup_inputs


def setup_inputs(seed=0):
    import zlib

    import numpy as np

    out = dict(_drawn_inputs(seed))
    spreads = {}
    factors = {'sgu_ln_b': 4.055,
     'lambda_k1': 4.47,
     'lambda_q2': 4.519,
     'norm_xq': 2.751,
     'norm_mem': 3.775,
     'b_router_group': 18.62,
     'b_router_expert': 7.278,
     'ffn1_norm_g_2': 8.0,
     'mix_norm_g_2': 8.0,
     'mem_norm_g_2': 8.0,
     'mem_q_norm_g_2': 8.0,
     'mem_k_norm_g_2': 8.0,
     'ffn2_norm_g_2': 8.0,
     'a_dw_bias_2': 33.752,
     'a_ln_g_2': 64.0,
     'a_ln_b_2': 64.0,
     'kv_norm_g_2': 36.081,
     'k_norm_g_2': 33.023,
     'b_q_norm_g_2': 40.185}
    for name, (base, spread) in spreads.items():
        noise = np.random.default_rng([zlib.crc32(name.encode()), seed]).standard_normal(out[name].shape)
        drawn = base * np.exp(spread * noise) if base else spread * noise
        out[name] = __import__('jax').numpy.asarray(drawn.astype(out[name].dtype))
    for name, factor in factors.items():
        out[name] = (out[name] * factor).astype(out[name].dtype)
    return out
```

```python
from contextlib import ExitStack

import concourse.bass as bass
import numpy as np
from concourse import mybir

P = 128
F32 = mybir.dt.float32
F32R = mybir.dt.float32r
BF16 = mybir.dt.bfloat16
I32 = mybir.dt.int32
U32 = mybir.dt.uint32
ALU = mybir.AluOpType
ACT = mybir.ActivationFunctionType
AX = mybir.AxisListType.X

TOK = 256
TT = TOK // P
D = 1024
KT = D // P
CW = 256
RAW = 6
SPLIT = 3
CH = KT * CW
D_FF = 2816
PAIRS = D_FF // CW
FT = D_FF // P
EXPERTS, GROUPS, D_EXPERT = 32, 4, 512
SLOTS = 32
EG = 4
MAX_ROUNDS = TOK // SLOTS
RMS_EPS, LN_EPS = 1e-6, 1e-5
LAMBDA_INIT = 0.8 - 0.6
NEG = -1e30
MAGIC = 1.5 * 2.0 ** 23
TWO_PI = (6.28125, 0.0019340515136718750, 1.2556659146e-06)
CAUSAL_W = 384

C_ID, C_ONES, C_BLK, C_ROT, C_LT, C_TRIL, C_ND, C_CAUSAL, C_SLOT, C_GRP, C_THR, C_FREQ, C_END = (
    0, 128, 256, 384, 512, 640, 768, 1152, 1536, 1568, 1600, 1608, 1609)


def shape_constants():
    c = np.zeros((P, C_END), np.float32)
    row = np.arange(P)
    c[:, C_ID:C_ONES] = np.eye(P)
    c[:, C_ONES:C_BLK] = 1
    c[:, C_BLK:C_ROT] = row[:, None] // 64 == row[None, :] // 64
    for half in (0, 64):
        for d in range(8):
            c[half + d + 8, C_ROT + half + d] = -1
            c[half + d, C_ROT + half + d + 8] = 1
    c[:, C_LT:C_TRIL] = row[:, None] < row[None, :]
    c[:, C_TRIL:C_ND] = row[None, :] <= row[:, None]
    for base, q0, n in ((0, 0, 128), (128, 128, 256)):
        dist = q0 + row[:, None] - np.arange(n)[None, :]
        c[:, C_ND + base:C_ND + base + n] = np.where(dist >= 0, -dist, NEG)
        c[:, C_CAUSAL + base:C_CAUSAL + base + n] = np.where(dist >= 0, 0, NEG)
    c[:, C_SLOT:C_GRP] = np.arange(SLOTS)
    c[:, C_GRP:C_THR] = np.arange(EXPERTS) // (EXPERTS // GROUPS)
    c[:, C_THR:C_THR + 7] = SLOTS * np.arange(1, MAX_ROUNDS)
    c[:, C_THR + 7] = 1e9
    freq = (1.0 / (np.float32(500000.0) ** (np.arange(0, 16, 2, dtype=np.float32) / np.float32(16)))).astype(np.float32)
    for half in (0, 64):
        c[half:half + 16, C_FREQ] = np.tile(freq, 2)
    return c


G_MIX, G_XQ, G_MEM, G_FFN1, G_MIX2, G_MEM2, G_FFN2, G_KV, G_LNG, G_LNB, G_DWB, G_SGUB, G_A = (
    0, 8, 16, 24, 40, 56, 72, 88, 96, 102, 108, 114, 118)
CONV_TAPS, CONV_TILES = 31, 6
TAP_GROUPS = -(-CONV_TAPS // 4)
DW_ROWS = CONV_TAPS * CONV_TILES
G_DW, G_HEAD = 128, 128 + DW_ROWS
G_END = G_HEAD + 6
HG_MQ, HG_MK, HG_K, HG_Q = 0, 2, 4, 5


def weight_plan(w):
    plan = []

    def cols(name, layer, n, start=0):
        a = w[name][layer] if layer is not None else w[name]
        plan.extend((a, start + CW * i, "cols") for i in range(n))

    def ffn(gate, up, down, layer):
        for i in range(PAIRS):
            plan.extend([(w[gate][layer], CW * i, "cols"), (w[up][layer], CW * i, "cols"),
                         (w[down][layer], CW * i, "rows")])

    cols("w_in", 0, 10)
    cols("w_kv_mem", 0, 8)
    cols("w_out", 0, 4)
    cols("w_q_mem", 0, 4)
    cols("w_o_mem", 0, 4)
    starts = {"before_moe": len(plan)}
    cols("w_mem_kv_2", 0, 2)
    cols("w_mem_kv_2", 1, 2)
    starts["ffn0"] = len(plan)
    ffn("ffn1_w_gate_2", "ffn1_w_up_2", "ffn1_w_down_2", 0)
    for i in range(3):
        cols("a_w_in_2", 0, 1, CW * i)
        cols("a_w_in_2", 0, 1, CW * (3 + i))
    cols("a_w_in_2", 0, 1, CW * 6)
    cols("w_o_2", 0, 4)
    starts["ffn1"] = len(plan)
    ffn("ffn2_w_gate_2", "ffn2_w_up_2", "ffn2_w_down_2", 0)
    cols("w_kv_2", None, 6)
    starts["ffn2"] = len(plan)
    ffn("ffn1_w_gate_2", "ffn1_w_up_2", "ffn1_w_down_2", 1)
    cols("b_w_in_2", 0, 4)
    cols("w_o_2", 1, 4)
    starts["ffn3"] = len(plan)
    ffn("ffn2_w_gate_2", "ffn2_w_up_2", "ffn2_w_down_2", 1)
    return plan, starts


def build(nc, ins, consts, out):
    plan, starts = weight_plan(ins)
    n_chunks = len(plan)
    moe_at = starts["before_moe"]
    assert moe_at % RAW == 0
    ffn_starts = [starts[f"ffn{i}"] for i in range(4)]
    in_ffn = {c for s in ffn_starts for c in range(s, s + 3 * PAIRS)}
    with ExitStack() as ctx:
        def sb(name, shape, dt=F32):
            return ctx.enter_context(nc.sbuf_tensor(name, shape, dt))

        def sem(name):
            return ctx.enter_context(nc.semaphore(name))

        ps = [ctx.enter_context(nc.psum_tensor(f"bank{i}", [P, 512], F32)) for i in range(8)]
        S_BANK, TR_BANK, O_BANK = (4, 5), 6, 7

        raw = sb("raw", [P, RAW, CH])
        whi = sb("whi", [P, SPLIT, CH], F32R)
        wlo = sb("wlo", [P, SPLIT, CH], F32R)
        xhi = [sb(f"x{i}hi", [P, KT, TOK], F32R) for i in range(2)]
        xlo = [sb(f"x{i}lo", [P, KT, TOK], F32R) for i in range(2)]
        h = sb("h", [P, TT, D])
        xn = sb("xn", [P, TT, D])
        arena = sb("arena", [P, 9728])
        hh_hi = sb("hh_hi", [P, 2, TOK], F32R)
        hh_lo = sb("hh_lo", [P, 2, TOK], F32R)
        prob = sb("prob", [P, 2, 512])
        prob_t = sb("prob_t", [P, 2, 512])
        cst = sb("cst", [P, C_END])
        cols = sb("cols", [P, G_END])
        small = sb("small", [P, 640])
        wr_hi, wr_lo = [t[:, :, :].rearrange("p a b -> p (a b)")[:, 0:KT * 36].rearrange("p (k n) -> p k n", k=KT)
                        for t in (hh_hi, hh_lo)]
        subln = sb("subln", [P, P])
        zeros = sb("zeros", [P, 512], BF16)
        picks = sb("picks", [P, 2, 2, 8], U32)
        extra_i = sb("extra_i", [P, 1], I32)

        ident = cst[:, C_ID:C_ID + P]
        ones = cst[:, C_ONES:C_ONES + P]
        blk64 = cst[:, C_BLK:C_BLK + P]
        rot = cst[:, C_ROT:C_ROT + P]
        before = cst[:, C_LT:C_LT + P]
        slot_row = cst[:, C_SLOT:C_SLOT + SLOTS]

        def area(at, *shape):
            n = int(np.prod(shape))
            v = arena[:, at:at + n]
            if len(shape) == 1:
                return v
            return v.rearrange("p (a b) -> p a b", a=shape[0])

        u_a, v_a, val_a = area(0, 2, 512), area(1024, 2, 512), area(2048, 2, 512)
        q_t, k_t = area(3072, 4, TOK), area(4096, 4, TOK)
        mem_a = area(5120, 2, D)
        k1_t, v1_a = area(5120, 8, TOK), area(7168, 2, D)
        ln_gb = area(7168, 2, 512)
        sgu_w, sgu_wt = area(8192, 4, P), area(8704, 4, P)
        q1_t = area(0, 8, TOK)
        gain_b = area(2048, 2, D)
        sel, selw = area(4096, TT, EG * SLOTS), area(4352, TT, EG * P)
        xg, spread = area(5376, KT, EG * SLOTS), area(6400, EG, TOK)
        y_sb = area(7424, D)
        e_silu, e_h, e_ht = area(8448, P), area(8576, P), area(8704, P)
        wr_raw = area(8832, KT, 36)
        mem2_a = area(0, 2, D)
        f_silu, f_prod = area(2048, 2, TOK), area(2560, 2, TOK)
        k2_t = [area(4096 + 512 * l, 2, TOK) for l in range(2)]
        v2_a = [area(5120 + 512 * l, 2, CW) for l in range(2)]
        kb_t, vb_a = area(6144, 6, TOK), area(7680, 2, 768)
        cos_t, sin_t = area(9216, TOK), area(9472, TOK)
        PADW = CONV_TAPS - 1 + TOK
        conv_in, conv_out = area(0, 6, PADW), area(1728, 6, TOK)
        sig = area(8192, 2, TOK)
        diag = area(6144, 16, P)
        conv_sq = xn[:, :, :].rearrange("p t d -> p (t d)")[:, 0:CONV_TILES * TOK].rearrange("p (a b) -> p a b", a=CONV_TILES)
        qm_t = area(3328, 2, TOK)
        qb_t = area(0, 6, TOK)
        sq = area(1536, 2, TOK)
        tmp = area(2048, 2, TOK)
        rs = area(2560, 2, TOK)

        at = [0]

        def take(n):
            at[0] += n
            return small[:, at[0] - n:at[0]]

        sumsq, meansq, root, rstd = take(2), take(2), take(2), take(2)
        nmax, psum_e, rsum = take(8), take(8), take(8)
        oss, oms, ort, ors = take(8), take(8), take(8), take(8)
        bn6, bn2 = take(48), take(16)
        lamp, lams, lame, neglam = take(2), take(2), take(2), take(1)
        logit, glog, gmax = take(72), take(16), take(16)
        gneg, gsum, ggate, gidx = take(2), take(2), take(2), take(2)
        emask = take(64)
        emax = take(16)
        ediff, eexp, eden, w1, w2 = take(2), take(2), take(2), take(2), take(2)
        eidx = take(4)
        rb = take(36)
        tmax, thr, extra_f = take(1), take(8), take(1)
        posm, wgt = sb("posm", [P, TT, EXPERTS + EG]), sb("wgt", [P, TT, EXPERTS + EG])
        hot = sb("hot", [P, TT, EXPERTS])
        hot2 = sb("hot2", [P, TT, EXPERTS])
        lamv = prob[:, 0, 0:256].rearrange("p (a b) -> p a b", a=4)
        posi = prob_t[:, 0, 0:TOK].bitcast(I32)
        rows_a = prob[:, 1, 0:P]
        rows_b = prob[:, 1, P:2 * P]
        rows_c = prob[:, 1, 2 * P:3 * P]

        in_x = [sem(f"in_x{tt}") for tt in range(TT)]
        in_c, in_rows, in_bc, in_mem, in_mem2, in_late, in_sgu = [sem(n) for n in (
            "in_consts", "in_rows", "in_broadcast", "in_mem", "in_mem2", "in_late", "in_sgu")]
        raw_in = [sem(f"raw_in{i}") for i in range(RAW)]
        hi_ready, lo_ready = sem("hi_ready"), sem("lo_ready")
        chunk_used = sem("chunk_used")
        evac_a, evac_v = sem("evac_a"), sem("evac_v")
        ss_ready, ms_ready, rt_ready, xn_ready = [sem(n) for n in ("ss_ready", "ms_ready", "rt_ready", "xn_ready")]
        tr_done, xhi_ready, xlo_ready = sem("tr_done"), sem("xhi_ready"), sem("xlo_ready")
        s_full, s_bias, nm_ready, e_ready, p_ready, t_done, pt_ready, o_done, o_hi, o_evac = [sem(n) for n in (
            "s_full", "s_bias", "nm_ready", "e_ready", "p_ready", "t_done", "pt_ready", "o_done", "o_hi", "o_evac")]
        sq_ready, hs_done, hms_ready, hrt_ready, hn_ready, rot_done = [sem(n) for n in (
            "sq_ready", "hs_done", "hms_ready", "hrt_ready", "hn_ready", "rot_done")]
        v_link, a_link = sem("v_link"), sem("a_link")
        cols_t, cols_ready, zero_ready = sem("cols_t"), sem("cols_ready"), sem("zero_ready")
        bn_ready, bn_root, wt_done, wt_ready, vn_ready, sp_done, sgu_done = [sem(n) for n in (
            "bn_ready", "bn_root", "wt_done", "wt_ready", "vn_ready", "sp_done", "sgu_done")]
        lam_ready, lam_exp, o_ss, o_ms, o_rt, mixed_ready = [sem(n) for n in (
            "lam_ready", "lam_exp", "o_ss", "o_ms", "o_rt", "mixed_ready")]
        h_ready = sem("h_ready")
        ffn_half, h_tile = sem("ffn_half"), sem("h_tile")
        gu0_done, silu_ready, prod_ready, hhi_ready, hlo_ready = [sem(n) for n in (
            "gu0_done", "silu_ready", "prod_ready", "hhi_ready", "hlo_ready")]
        sig_ready, conv_ready, csum_done, cmu_ready, cent_ready, csq_ready, cms_ready, crt_ready, cn_ready, \
            csilu_ready, chi_ready, clo_ready = [sem(n) for n in (
                "sig_ready", "conv_ready", "csum_done", "cmu_ready", "cent_ready", "csq_ready", "cms_ready",
                "crt_ready", "cn_ready", "csilu_ready", "chi_ready", "clo_ready")]
        rope_done = sem("rope_done")
        diag_ready, diag_used, tap_done = [sem(n) for n in (
            "diag_ready", "diag_used", "tap_done")]
        wt_copied, o_copied, wr_split, h_added, glu_done = [sem(n) for n in (
            "wt_copied", "o_copied", "wr_split", "h_added", "glu_done")]
        rope_half, rope_sin = sem("rope_half"), sem("rope_sin")
        wr_ready, r_done, r_bias, r_exp, r_pick, r_ediff, r_eexp, hot_ready, pos_done, extra_ready = [sem(n) for n in (
            "wr_ready", "r_done", "r_bias", "r_exp", "r_pick", "r_ediff", "r_eexp", "hot_ready", "pos_done",
            "extra_ready")]
        moe_done, out_done = sem("moe_done"), sem("out_done")

        def expert_sems(tag):
            return {n: sem(f"{tag}_{n}") for n in (
                "sel", "selw", "fill", "evac", "raw_used", "gu", "silu", "hm", "ht_full", "ht", "y_full", "y0", "y1",
                "spread")}

        main, over = expert_sems("moe"), expert_sems("over")
        over_in = sem("over_in")

        linear = [c for c in range(n_chunks) if c not in in_ffn]
        act_evac = set(range(0, 4)) | set(range(22, 26))
        evac_count, seen = {}, {"a": 0, "v": 0}
        for c in linear:
            e = "a" if c in act_evac else "v"
            seen[e] += 1
            evac_count[c] = (e, seen[e])

        def linear_bank(c):
            return ps[linear.index(c) % 4]

        def chunk_source(c):
            a, col, kind = plan[c]
            if kind == "cols":
                return a.rearrange("(k p) n -> p k n", p=P)[:, :, col:col + CW]
            return a.rearrange("(k p) n -> p k n", p=P)[:, col // P:col // P + 2, :]

        def chunk_slot(c, kind):
            return raw[:, c % RAW, :].rearrange("p (k n) -> p k n", k=KT if kind == "cols" else 2)

        def landed(c):
            return 16 * (c // RAW + 1 + (EXPERTS if c >= moe_at else 0))

        def prob_slot(u):
            s = u % 2 if u < 8 else u % 4
            return prob[:, s, :] if s < 2 else xn[:, 0, 512 * (s - 2):512 * (s - 1)]

        def stat_cols(u, tt=None):
            s = 2 * (u % 2 if u < 8 else u % 4)
            return slice(s, s + 2) if tt is None else slice(s + tt, s + tt + 1)

        def slot_free(u):
            return u // 2 if u < 8 else max(4, u - 7)

        SPARE = {}
        for phase, c in ((0, starts["ffn0"] + 3 * PAIRS + 8), (1, starts["ffn2"] + 3 * PAIRS + 5)):
            SPARE[phase] = [linear.index(c + i) % 4 for i in range(2)]

        def turned_bank(head):
            return ps[TR_BANK if head < 8 or head % 2 == 0 else SPARE[int(head >= 12)][0]]

        def out_bank(head):
            return ps[O_BANK if head < 8 or head // 2 % 2 == 0 else SPARE[int(head >= 12)][1]]

        block = ctx.enter_context(nc.Block())

        @block.sync
        def _(sp):
            for tt in range(TT):
                sp.dma_start(h[:, tt, :], ins["x"][0][tt * P:tt * P + P, :]).then_inc(in_x[tt], 16)
            sp.dma_start(cst[:, :], consts).then_inc(in_c, 16)

            def load_chunk(c):
                if c >= RAW and c != moe_at and not moe_at <= c < moe_at + RAW:
                    sp.wait_ge(lo_ready, c - RAW + 1)
                sp.dma_start(chunk_slot(c, plan[c][2]), chunk_source(c)).then_inc(raw_in[c % RAW], 16)

            for c in range(moe_at):
                load_chunk(c)

            def load_expert(x, slot, sem_):
                if slot < 4:
                    a = ins["w_gate" if slot < 2 else "w_up"][0].rearrange("e (k p) n -> p e k n", p=P)
                    src = a[:, bass.ds(x, 1), 4 * (slot % 2):4 * (slot % 2) + 4, :]
                    dst = raw[:, slot, :].rearrange("p (o k n) -> p o k n", o=1, k=4)
                else:
                    a = ins["w_down"][0].rearrange("e (k p) n -> p e k n", p=P)
                    src = a[:, bass.ds(x, 1), 2 * (slot - 4):2 * (slot - 4) + 2, :]
                    dst = raw[:, slot, :].rearrange("p (o k n) -> p o k n", o=1, k=2)
                sp.dma_start(dst, src).then_inc(sem_, 16)

            for slot in range(RAW):
                sp.wait_ge(lo_ready, moe_at - RAW + slot + 1)
                load_expert(0, slot, raw_in[slot])
            with sp.Fori(1, EXPERTS) as x:
                for slot in range(3):
                    sp.wait_ge(main["raw_used"], 3 * x - 2 + slot)
                    load_expert(x, slot, raw_in[slot])
                sp.wait_ge(main["gu"], x)
                load_expert(x, 3, raw_in[3])
                sp.wait_ge(main["y_full"], 2 * x)
                load_expert(x, 4, raw_in[4])
                load_expert(x, 5, raw_in[5])
            sp.wait_ge(main["y_full"], 2 * EXPERTS)
            sp.wait_ge(extra_ready, 1)
            extra = sp.value_load(extra_i[0:1, 0:1], min_val=0, max_val=MAX_ROUNDS - 1)
            with sp.If(extra > 0):
                with sp.Fori(0, extra) as r:
                    with sp.Fori(0, EXPERTS) as x:
                        sp.wait_ge(over["spread"], EXPERTS * r + x + 1)
                        for slot in range(RAW):
                            load_expert(x, slot, over_in)
            sp.wait_ge(moe_done, 1)
            ffn_first = {s: i for i, s in enumerate(ffn_starts)}
            c = moe_at
            while c < n_chunks:
                load_chunk(c)
                c += 1
                if c - RAW in ffn_first:
                    s = c - RAW
                    gate, up, down = (plan[s + j][0] for j in range(3))
                    with sp.Fori(1, PAIRS // 2) as i:
                        for j in range(RAW):
                            sp.wait_ge(lo_ready, s + 6 * i + (j - RAW + 1))
                            half = j // 3
                            if j % 3 < 2:
                                src = (gate, up)[j % 3].rearrange("(k p) n -> p k n", p=P)[:, :, bass.ds(2 * CW * i + CW * half, CW)]
                            else:
                                src = down.rearrange("(k p) n -> p k n", p=P)[:, bass.ds(4 * i + 2 * half, 2), :]
                            sp.dma_start(chunk_slot(s + j, "cols" if j % 3 < 2 else "rows"), src).then_inc(raw_in[(s + j) % RAW], 16)
                    c = s + 6 * (PAIRS // 2)
            sp.wait_ge(h_ready, 9)
            sp.dma_start(out[0].rearrange("(t p) d -> p t d", p=P), h[:, :, :]).then_inc(out_done, 16)
            sp.wait_ge(out_done, 16)

        @block.gpsimd
        def _(pool):
            pool.dma_start(mem_a, ins["mem"][0].rearrange("(t p) d -> p t d", p=P)).then_inc(in_mem, 16)
            pool.dma_start(sgu_w, ins["sgu_w"][0].rearrange("g t s -> t g s")).then_inc(in_sgu, 16)
            pool.dma_start(ln_gb[:, 0, :], ins["sgu_ln_g"][0].rearrange("g c -> (g c)").partition_broadcast(P)).then_inc(in_sgu, 16)
            pool.dma_start(ln_gb[:, 1, :], ins["sgu_ln_b"][0].rearrange("g c -> (g c)").partition_broadcast(P)).then_inc(in_sgu, 16)
            for i, name in enumerate(("lambda_q1", "lambda_k1", "lambda_q2", "lambda_k2")):
                pool.dma_start(lamv[:, i, :], ins[name][0].partition_broadcast(P)).then_inc(in_bc, 16)
            pool.dma_start(subln[:, :], ins["diff_subln"][0].partition_broadcast(P)).then_inc(in_bc, 16)
            pool.dma_start(rb[:, 0:4], ins["b_router_group"][0].partition_broadcast(P)).then_inc(in_bc, 16)
            pool.dma_start(rb[:, 4:36], ins["b_router_expert"][0].partition_broadcast(P)).then_inc(in_bc, 16)
            pool.dma_start(posi, ins["positions_2"][0].partition_broadcast(P)).then_inc(in_bc, 16)
            pool.wait_ge(h_ready, 1)
            pool.dma_start(gain_b[:, 0, :], ins["norm_ffn"][0].partition_broadcast(P)).then_inc(in_late, 16)
            pool.dma_start(gain_b[:, 1, :], ins["norm_final"].partition_broadcast(P)).then_inc(in_late, 16)
            pool.wait_ge(h_ready, 2)
            pool.dma_start(wr_raw[:, :, 0:4], ins["w_router_group"][0].rearrange("(k p) n -> p k n", p=P)).then_inc(in_late, 16)
            pool.dma_start(wr_raw[:, :, 4:36], ins["w_router_expert"][0].rearrange("(k p) n -> p k n", p=P)).then_inc(in_late, 16)
            pool.dma_start(mem2_a, ins["mem_2"][0].rearrange("(t p) d -> p t d", p=P)).then_inc(in_mem2, 16)
            pool.wait_ge(h_ready, 3)
            for g in range(TAP_GROUPS):
                if g >= 2:
                    pool.wait_ge(diag_used, g - 1)
                taps_n = min(4, CONV_TAPS - 4 * g)
                for t in range(2):
                    first = G_DW + 6 * 4 * g + 4 + t
                    dst = diag[:, 8 * (g % 2):8 * (g % 2) + 8, :].rearrange("p (j t) c -> p j t c", t=2)[:, 0:taps_n, t, :]
                    ins_ = pool.tensor_tensor(dst, ident.unsqueeze(1).broadcast_to([P, taps_n, P]),
                                              cols[:, first:first + 6 * (taps_n - 1) + 1:6].unsqueeze(2).broadcast_to([P, taps_n, P]),
                                              ALU.mult)
                ins_.then_inc(diag_ready, 1)

        @block.tensor
        def _(pe):
            n = {"turn": 0, "unit": 0, "head": 0, "out": 0, "hs": 0, "rot": 0}

            def split_product(dst, a_hi, a_lo, b_hi, b_lo, first, last):
                pe.matmul(dst, a_hi, b_hi, start=first, stop=False, skip_group_check=True)
                pe.matmul(dst, a_lo, b_hi, start=False, stop=False, skip_group_check=True)
                return pe.matmul(dst, a_hi, b_lo, start=False, stop=last, skip_group_check=True)

            def turn(src, gained=True):
                sem_, rows_written = gained
                first = n["turn"]

                def tiles(kp, tt):
                    for k in (2 * kp, 2 * kp + 1):
                        at_ = (k % 2) * TOK + tt * P
                        mm = pe.transpose(ps[6 + (first + kp) % 2][:, at_:at_ + P], src[:, tt, k * P:k * P + P], ident)
                    return mm

                if rows_written > 1:
                    pe.wait_ge(sem_, rows_written - 1)
                else:
                    pe.wait_ge(sem_, rows_written)
                for kp in range(2):
                    if first + kp >= 2:
                        pe.wait_ge(xlo_ready, first + kp - 1)
                    tiles(kp, 0)
                pe.wait_ge(sem_, rows_written)
                for kp in range(2):
                    tiles(kp, 1).then_inc(tr_done, 1)
                for kp in range(2, KT // 2):
                    pe.wait_ge(xlo_ready, first + kp - 1)
                    tiles(kp, 0)
                    tiles(kp, 1).then_inc(tr_done, 1)
                n["turn"] += KT // 2

            def x_part(k, fresh):
                if fresh and k % 2 == 0:
                    pe.wait_ge(xlo_ready, n["turn"] - KT // 2 + k // 2 + 1)

            def linear_rows(c, x, fresh=False):
                bank, s = linear_bank(c), c % SPLIT
                start_linear(c)
                hi = whi[:, s, :].rearrange("p (k n) -> p k n", k=KT)
                lo = wlo[:, s, :].rearrange("p (k n) -> p k n", k=KT)
                for tt in range(TT):
                    for k in range(KT):
                        x_part(k, fresh and tt == 0)
                        mm = split_product(bank[:, tt * CW:tt * CW + CW], xhi[x][:, k, tt * P:tt * P + P],
                                           xlo[x][:, k, tt * P:tt * P + P], hi[:, k, :], lo[:, k, :], k == 0, k == KT - 1)
                mm.then_inc(chunk_used, 1)

            def linear_cols(c, x, fresh=False):
                bank, s = linear_bank(c), c % SPLIT
                start_linear(c)
                hi = whi[:, s, :].rearrange("p (k n) -> p k n", k=KT)
                lo = wlo[:, s, :].rearrange("p (k n) -> p k n", k=KT)
                for j in range(2):
                    for k in range(KT):
                        x_part(k, fresh and j == 0)
                        mm = split_product(bank[:, j * TOK:j * TOK + TOK], hi[:, k, j * P:j * P + P],
                                           lo[:, k, j * P:j * P + P], xhi[x][:, k, :], xlo[x][:, k, :], k == 0, k == KT - 1)
                mm.then_inc(chunk_used, 1)

            def start_linear(c):
                pe.wait_ge(lo_ready, c + 1)
                at = linear.index(c)
                if at >= 4:
                    e, count = evac_count[linear[at - 4]]
                    pe.wait_ge(evac_a if e == "a" else evac_v, count)

            def x_ready():
                pe.wait_ge(xlo_ready, n["turn"])

            def scores(parts):
                u = n["unit"]
                if u >= 2:
                    pe.wait_ge(e_ready, u - 1)
                for cols_, pairs in parts:
                    for i, (q, k) in enumerate(pairs):
                        mm = pe.matmul(ps[4 + u % 2][:, cols_], q, k, start=i == 0, stop=i == len(pairs) - 1,
                                       skip_group_check=True)
                mm.then_inc(s_full, 1)
                n["unit"] += 1

            def causal_scores(q, k):
                scores([(slice(0, 128), [(q[:, 0:P], k[:, 0:P])]), (slice(128, 384), [(q[:, P:TOK], k[:, 0:TOK])])])

            def turn_probs(p, blocks):
                hd = n["head"]
                pe.wait_ge(p_ready, hd + 1)
                if hd >= 1:
                    pe.wait_ge(pt_ready, hd if hd <= 8 else hd - 1)
                for i, src in enumerate(blocks):
                    mm = pe.transpose(turned_bank(hd)[:, i * P:i * P + P], p[:, src:src + P], ident)
                mm.then_inc(t_done, 1)
                n["head"] += 1

            def values(parts, hd, first=True):
                pe.wait_ge(pt_ready, hd + 1)
                if first and n["out"] >= 1:
                    pe.wait_ge(o_evac, n["out"] if hd <= 8 else n["out"] - 1)
                for rows_, cols_, pairs, st, sp_ in parts:
                    for i, (a, b) in enumerate(pairs):
                        mm = pe.matmul(out_bank(hd)[rows_, cols_], a, b, start=st and i == 0,
                                       stop=sp_ and i == len(pairs) - 1, skip_group_check=True)
                mm.then_inc(o_done, 1)

            FULL_BLOCKS = (0, 256, 128, 384)
            CAUSAL_BLOCKS = (0, 128, 256)

            pe.wait_ge(in_c, 16)
            pe.wait_ge(in_rows, 16 * 22)
            pe.transpose(ps[5][:, 0:G_A], rows_a[0:G_A, :], ident[0:G_A, 0:G_A])
            pe.transpose(ps[5][:, 128:256], rows_b, ident)
            m = DW_ROWS - P + 6
            pe.transpose(ps[5][:, 256:256 + m], rows_c[0:m, :], ident[0:m, 0:m]).then_inc(cols_t, 1)

            turn(xn, (xn_ready, 2))
            for c in range(4):
                linear_rows(c, 0, c == 0)
            for c in range(4, 8):
                linear_cols(c, 0)
            for c in range(8, 10):
                linear_rows(c, 0)
            pe.wait_ge(wt_done, 1)
            for g in range(4):
                mm = pe.transpose(ps[4][:, g * P:g * P + P], sgu_w[:, g, :], ident)
            mm.then_inc(wt_ready, 1)
            turn(xn, (xn_ready, 4))
            pe.wait_ge(vn_ready, 1)
            pe.wait_ge(wt_copied, 1)
            for tt in range(TT):
                for g in range(4):
                    mm = pe.matmul(ps[4 + tt][:, g * P:g * P + P], sgu_wt[:, g, :], v_a[:, tt, g * P:g * P + P],
                                   start=True, stop=True)
                mm.then_inc(sp_done, 1)
            pe.wait_ge(sgu_done, 1)

            x_ready()
            for hd in range(4):
                for i in range(2):
                    half = slice(64 * i, 64 * i + 64)
                    pe.wait_ge(evac_v, evac_count[7][1])
                    causal_scores(q_t[half, hd, :], k_t[half, hd, :])
                for c in (10 + 2 * hd, 11 + 2 * hd):
                    (linear_cols if c < 14 else linear_rows)(c, 1)
                turn_probs(prob[:, 0, :], CAUSAL_BLOCKS)
                pt = prob_t[:, hd % 2, :]
                v = val_a[:, :, hd * P:hd * P + P]
                values([(slice(0, P), slice(0, P), [(pt[:, 0:P], v[:, 0, :])], True, True),
                        (slice(0, P), slice(P, 2 * P), [(pt[:, P:2 * P], v[:, 0, :]), (pt[:, 2 * P:3 * P], v[:, 1, :])],
                         True, True)], hd)
                n["out"] += 1
            turn(xn, (mixed_ready, 1))
            for c in range(18, 22):
                linear_rows(c, 0, c == 18)

            def full_scores(head):
                parts = [(slice(tt * TOK, tt * TOK + TOK),
                          [(q1_t[:, 2 * head + j, tt * P:tt * P + P], k1_t[:, 2 * head + j, :]) for j in range(2)])
                         for tt in range(TT)]
                pe.wait_ge(evac_a, evac_count[22 + head][1])
                scores(parts)

            def full_out(head):
                turn_probs(prob_slot(8 + head), FULL_BLOCKS)
                pt = prob_t[:, (n["head"] - 1) % 2, :].rearrange("p (m q) -> p m q", m=2)
                values([(slice(0, P), slice(j * TOK, j * TOK + TOK),
                         [(v1_a[:, mt, head * 256 + j * P:head * 256 + j * P + P], pt[:, mt, :]) for mt in range(2)],
                         True, True) for j in range(2)], n["head"] - 1)
                n["out"] += 1

            turn(xn, (xn_ready, 6))
            pe.wait_ge(evac_v, evac_count[17][1])
            linear_cols(22, 1, True)
            linear_cols(23, 1)
            full_scores(0)
            linear_cols(24, 1)
            full_scores(1)
            full_out(0)
            linear_cols(25, 1)
            full_scores(2)
            full_out(1)
            full_scores(3)
            full_out(2)
            full_out(3)
            pe.wait_ge(o_evac, n["out"])
            for c in range(26, 30):
                linear_rows(c, 0)

            turn(xn, (xn_ready, 8))
            x_ready()
            pe.wait_ge(wr_ready, 1)
            for tt in range(TT):
                for k in range(KT):
                    mm = split_product(ps[4][:, tt * 36:tt * 36 + 36], xhi[0][:, k, tt * P:tt * P + P],
                                       xlo[0][:, k, tt * P:tt * P + P], wr_hi[:, k, :], wr_lo[:, k, :], k == 0, k == KT - 1)
            mm.then_inc(r_done, 1)
            pe.wait_ge(hot_ready, 1)
            for at_, pairs in ((0, [(before, 0)]), (32, [(ones, 0), (before, 1)]), (64, [(ones, 0), (ones, 1)])):
                for i, (lhs, tt) in enumerate(pairs):
                    mm = pe.matmul(ps[5][:, at_:at_ + 32], lhs, hot[:, tt, :], start=i == 0, stop=i == len(pairs) - 1,
                                   skip_group_check=True)
            mm.then_inc(pos_done, 1)

            pe.wait_ge(zero_ready, 1)
            for b in range(4):
                pe.matmul(ps[b][:, :], zeros[:, 0:P], zeros[:, :], start=True, stop=False, skip_group_check=True)

            def gather(half, s, width, dst, src):
                for k in range(4 * half, 4 * half + 4):
                    for tt in range(TT):
                        mm = pe.matmul(dst[:, (k % 4) * width:(k % 4) * width + width], xn[:, tt, k * P:k * P + P],
                                       src[:, tt, 0:width], start=tt == 0, stop=tt == TT - 1, skip_group_check=True)
                return mm

            def gate_up(x_of, arrived, s):
                for which in range(2):
                    for k in range(KT):
                        slot = 2 * which + k // 4
                        if k % 4 == 0:
                            arrived(slot)
                        w_k = raw[:, slot, :].rearrange("p (k n) -> p k n", k=4)
                        for j in range(4):
                            mm = pe.matmul(ps[4][32 * j:32 * j + 32, which * P:which * P + P], x_of(k),
                                           w_k[:, k % 4, j * P:j * P + P], start=k == 0, stop=k == KT - 1,
                                           skip_group_check=True)
                        if k == 3 or (k == 7 and which == 0):
                            mm.then_inc(s["raw_used"], 1)
                mm.then_inc(s["gu"], 1)

            def turn_hidden(s, count):
                pe.wait_ge(s["hm"], count)
                pe.transpose(ps[4][:, 256:384], e_h, ident).then_inc(s["ht_full"], 1)

            def down(arrived, s, count):
                pe.wait_ge(s["ht"], count)
                arrived(4)
                arrived(5)
                for half in range(2):
                    for j in range(4):
                        w_j = raw[:, 4 + j // 2, :].rearrange("p (k n) -> p k n", k=2)
                        mm = pe.matmul(ps[6 + half][32 * j:32 * j + 32, :], e_ht[:, 32 * j:32 * j + 32],
                                       w_j[:, j % 2, half * 512:half * 512 + 512], start=True, stop=True,
                                       skip_group_check=True)
                    mm.then_inc(s["y_full"], 1)

            def spread_out(e, s, count):
                pe.wait_ge(s["y0"], count)
                pe.wait_ge(s["y1"], count)
                for tt in range(TT):
                    for half in range(2):
                        mm = pe.matmul(ps[2 * tt + half][:, :], spread[:, e, tt * P:tt * P + P],
                                       y_sb[:, half * 512:half * 512 + 512], start=False, stop=False,
                                       skip_group_check=True)
                mm.then_inc(s["spread"], 1)

            def gather_half(half, count):
                pe.wait_ge(main["evac"], count)
                gather(half, main, EG * SLOTS, ps[5], sel).then_inc(main["fill"], 1)

            def turn_spread(half, count):
                pe.wait_ge(main["evac"], count)
                for i in range(2):
                    for tt in range(TT):
                        mm = pe.transpose(ps[5][:, i * TOK + tt * P:i * TOK + tt * P + P],
                                          selw[:, tt, (2 * half + i) * P:(2 * half + i) * P + P], ident)
                mm.then_inc(main["fill"], 1)

            pe.wait_ge(main["sel"], 1)
            gather(0, main, EG * SLOTS, ps[5], sel).then_inc(main["fill"], 1)
            gather_half(1, 1)
            with pe.Fori(0, EXPERTS // EG) as g:
                for e in range(EG):
                    def arrived(slot):
                        pe.wait_ge(raw_in[slot], 64 * g + 16 * e + landed(slot) + 16 * (moe_at // RAW))

                    if e == 0:
                        pe.wait_ge(main["evac"], 4 * g + 2)
                    gate_up(lambda k: xg[:, k, e * SLOTS:e * SLOTS + SLOTS], arrived, main)
                    if e == 0:
                        pe.wait_ge(main["selw"], g + 1)
                        turn_spread(0, 4 * g + 2)
                    else:
                        spread_out(e - 1, main, 4 * g + e)
                    turn_hidden(main, 4 * g + e + 1)
                    if e == 0:
                        turn_spread(1, 4 * g + 3)
                        pe.wait_ge(main["evac"], 4 * g + 4)
                    down(arrived, main, 4 * g + e + 1)
                pe.wait_ge(main["sel"], g + 2)
                gather_half(0, 4 * g + 4)
                spread_out(EG - 1, main, 4 * g + 4)
                gather_half(1, 4 * g + 5)
            pe.wait_ge(extra_ready, 1)
            extra = pe.value_load(extra_i[0:1, 0:1], min_val=0, max_val=MAX_ROUNDS - 1)
            with pe.If(extra > 0):
                pe.wait_ge(main["evac"], EXPERTS + 2)
                pe.matmul(ps[0][:, :], zeros[:, 0:P], zeros[:, :], start=False, stop=False,
                          skip_group_check=True).then_inc(over["spread"], 1)
                with pe.Fori(0, extra) as r:
                    with pe.Fori(0, EXPERTS) as x:
                        step = EXPERTS * r + x + 1
                        pe.wait_ge(over["selw"], step)
                        for half in range(2):
                            for k in range(4 * half, 4 * half + 4):
                                for tt in range(TT):
                                    pe.matmul(ps[5][:, k * SLOTS:k * SLOTS + SLOTS], xn[:, tt, k * P:k * P + P],
                                              sel[:, tt, 0:SLOTS], start=tt == 0, stop=tt == TT - 1, skip_group_check=True)
                        for tt in range(TT):
                            mm = pe.transpose(ps[5][:, 256 + tt * P:256 + tt * P + P], selw[:, tt, 0:P], ident)
                        mm.then_inc(over["fill"], 1)
                        pe.wait_ge(over["evac"], step)
                        pe.wait_ge(over_in, 16 * RAW * step)
                        gate_up(lambda k: xg[:, k, 0:SLOTS], lambda slot: None, over)
                        turn_hidden(over, step)
                        down(lambda slot: None, over, step)
                        spread_out(0, over, step)
            for b in range(4):
                mm = pe.matmul(ps[b][:, :], zeros[:, 0:P], zeros[:, :], start=False, stop=True, skip_group_check=True)
            mm.then_inc(moe_done, 1)

            def head_sums():
                pe.wait_ge(sq_ready, n["hs"] + 1)
                if n["hs"] >= 1:
                    pe.wait_ge(hms_ready, n["hs"])
                pe.matmul(ps[7][:, :], blk64, prob[:, 0, :], start=True, stop=True).then_inc(hs_done, 1)
                n["hs"] += 1

            def rotate(heads, norms):
                pe.wait_ge(hn_ready, norms)
                if n["rot"] >= 1:
                    pe.wait_ge(rope_done, n["rot"])
                pe.matmul(ps[6][:, :], rot, heads, start=True, stop=True).then_inc(rot_done, 1)
                n["rot"] += 1

            def memory_head(q, layer, head):
                half = slice(64 * (head % 2), 64 * (head % 2) + 64)

                def out(hd, pt):
                    pt = pt.rearrange("p (m q) -> p m q", m=2)
                    values([(half, slice(0, TOK), [(v2_a[layer][:, mt, head * 64:head * 64 + 64], pt[:, mt, :])
                                                   for mt in range(2)], True, True)], hd, head % 2 == 0)
                return (lambda: scores([(slice(tt * TOK, tt * TOK + TOK),
                                         [(q[half, head // 2, tt * P:tt * P + P], k2_t[layer][half, head // 2, :])])
                                        for tt in range(TT)]), FULL_BLOCKS, out)

            def causal_head(head):
                half = slice(64 * (head % 2), 64 * (head % 2) + 64)

                def out(hd, pt):
                    v = vb_a[:, :, head * 64:head * 64 + 64]
                    values([(half, slice(0, TOK), [(v[:, 0, :], pt[:, 0:TOK])], True, False),
                            (half, slice(P, TOK), [(v[:, 1, :], pt[:, TOK:TOK + P])], False, True)], hd, head % 2 == 0)
                return lambda: causal_scores(qb_t[half, head // 2, :], kb_t[half, head // 2, :]), CAUSAL_BLOCKS, out

            def attend(heads, beside=None):
                first, unit = n["head"], n["unit"]
                for s in range(len(heads) + 3):
                    if s < len(heads):
                        heads[s][0]()
                    if beside is not None:
                        beside(s)
                    if 2 <= s < len(heads) + 2:
                        turn_probs(prob_slot(unit + s - 2), heads[s - 2][1])
                    if s >= 3:
                        hd = first + s - 3
                        heads[s - 3][2](hd, prob_t[:, hd % 2, :])
                        n["out"] += hd % 2

            def tap_group(g):
                pe.wait_ge(diag_ready, g + 1)
                for j in range(4 * g, min(4 * g + 4, CONV_TAPS)):
                    for t in range(2):
                        mm = pe.matmul(tap_bank[:, t * TOK:t * TOK + TOK], diag[:, 8 * (g % 2) + 2 * (j % 4) + t, :],
                                       conv_in[:, 4 + t, j:j + TOK], start=False, stop=j == CONV_TAPS - 1,
                                       skip_group_check=True)
                mm.then_inc(diag_used, 1)

            def swiglu(q, x):
                s, b = ffn_starts[q], FT * q
                for bank in range(4):
                    pe.matmul(ps[bank][:, :], zeros[:, 0:P], zeros[:, :], start=True, stop=False, skip_group_check=True)

                def gate_or_up(slot, col, last_first):
                    hi = whi[:, slot, :].rearrange("p (k n) -> p k n", k=KT)
                    lo = wlo[:, slot, :].rearrange("p (k n) -> p k n", k=KT)
                    for j in range(2):
                        for k in range(KT):
                            x_part(k, col == 0 and j == 0)
                            mm = split_product(ps[4 + j][:, col:col + TOK], hi[:, k, j * P:j * P + P],
                                               lo[:, k, j * P:j * P + P], xhi[x][:, k, :], xlo[x][:, k, :],
                                               k == 0, k == KT - 1)
                        if j == 0 and last_first:
                            mm.then_inc(gu0_done, 1)
                    mm.then_inc(chunk_used, 1)

                def pair(i, phase, last):
                    cb = s + 3 * i
                    pe.wait_ge(lo_ready, cb + 1)
                    gate_or_up(phase % SPLIT, 0, False)
                    pe.wait_ge(lo_ready, cb + 2)
                    gate_or_up((phase + 1) % SPLIT, TOK, True)
                    pe.wait_ge(lo_ready, cb + 3)
                    slot = (phase + 2) % SPLIT
                    hi = whi[:, slot, :].rearrange("p (k n) -> p k n", k=2)
                    lo = wlo[:, slot, :].rearrange("p (k n) -> p k n", k=2)
                    for j in range(2):
                        pe.wait_ge(hlo_ready, 2 * i + (b + j + 1))
                        for tt in range(TT):
                            for half in range(2):
                                mm = split_product(ps[2 * tt + half][:, :], hh_hi[:, j, tt * P:tt * P + P],
                                                   hh_lo[:, j, tt * P:tt * P + P], hi[:, j, half * 512:half * 512 + 512],
                                                   lo[:, j, half * 512:half * 512 + 512], False, last and j == 1)
                            if last and j == 1 and tt == 0:
                                mm.then_inc(ffn_half, 1)
                    mm.then_inc(chunk_used, 1)

                with pe.Fori(0, PAIRS - 1) as i:
                    pair(i, s % SPLIT, False)
                pair(PAIRS - 1, s % SPLIT, True)

            turn(xn, (xn_ready, 10))
            turn(xn, (xn_ready, 10))
            x_ready()
            for layer in range(2):
                c = moe_at + 2 * layer
                linear_cols(c, 1 - layer)
                linear_rows(c + 1, 1 - layer)
                head_sums()
            turn(xn, (xn_ready, 12))
            swiglu(0, 1)
            turn(xn, (xn_ready, 14))
            c0 = ffn_starts[0] + 3 * PAIRS
            for c in range(c0, c0 + 7):
                linear_cols(c, 0, c == c0)
            head_sums()
            pe.wait_ge(hn_ready, n["hs"])
            tap_bank = linear_bank(c0 + 7)
            pe.matmul(tap_bank[:, :], zeros[:, 0:P], zeros[:, :], start=True, stop=False, skip_group_check=True)

            def taps_beside(step):
                for g in range(2 * step, min(2 * step + 2, TAP_GROUPS)):
                    tap_group(g)

            attend([memory_head(qm_t, 0, head) for head in range(4)], taps_beside)
            pe.wait_ge(conv_ready, 1)
            for ct in range(CONV_TILES):
                mm = pe.matmul(ps[6][:, 0:TOK], ones, conv_out[:, ct, :], start=ct == 0, stop=ct == CONV_TILES - 1)
            mm.then_inc(csum_done, 1)
            pe.wait_ge(csq_ready, 1)
            for ct in range(CONV_TILES):
                mm = pe.matmul(ps[7][:, 0:TOK], ones, conv_sq[:, ct, :], start=ct == 0, stop=ct == CONV_TILES - 1)
            mm.then_inc(csum_done, 1)
            pe.wait_ge(clo_ready, 1)
            for c in range(c0 + 7, c0 + 11):
                linear_rows(c, 1)
            turn(xn, (xn_ready, 16))
            swiglu(1, 0)
            turn(xn, (xn_ready, 18))
            c0 = ffn_starts[1] + 3 * PAIRS
            linear_cols(c0, 1, True)
            turn(xn, (xn_ready, 18))
            linear_cols(c0 + 1, 1)
            x_ready()
            hs = n["hs"]
            head_sums()
            linear_cols(c0 + 2, 1)
            rotate(kb_t[:, 0:2, :], hs + 1)
            head_sums()
            linear_rows(c0 + 3, 1)
            rotate(kb_t[:, 2:4, :], hs + 2)
            head_sums()
            linear_rows(c0 + 4, 1)
            rotate(kb_t[:, 4:6, :], hs + 3)
            linear_rows(c0 + 5, 1)
            pe.wait_ge(evac_v, evac_count[c0 + 5][1])
            swiglu(2, 0)
            turn(xn, (xn_ready, 20))
            c0 = ffn_starts[2] + 3 * PAIRS
            linear_cols(c0, 1, True)
            linear_cols(c0 + 1, 1)
            hs = n["hs"]
            x_ready()
            head_sums()
            linear_cols(c0 + 2, 1)
            rotate(qb_t[:, 0:2, :], hs + 1)
            head_sums()
            linear_cols(c0 + 3, 1)
            rotate(qb_t[:, 2:4, :], hs + 2)
            head_sums()
            rotate(qb_t[:, 4:6, :], hs + 3)
            head_sums()
            pe.wait_ge(rope_done, 6)
            pe.wait_ge(hn_ready, n["hs"])
            attend([causal_head(head) for head in range(12)] + [memory_head(qm_t, 1, head) for head in range(4)])
            pe.wait_ge(o_evac, n["out"])
            for c in range(c0 + 4, c0 + 8):
                linear_rows(c, 0)
            turn(xn, (xn_ready, 22))
            swiglu(3, 1)

        @block.scalar
        def _(act):
            n = {"chunk": 0, "norm": 0, "turn": 0, "unit": 0, "head": 0, "ohi": 0, "hs": 0}

            def round_chunk(c):
                act.wait_ge(raw_in[c % RAW], landed(c))
                if c >= SPLIT:
                    act.wait_ge(chunk_used, c - SPLIT + 1)
                act.activation(whi[:, c % SPLIT, :], raw[:, c % RAW, :], ACT.Copy).then_inc(hi_ready, 1)

            def round_to(c):
                while n["chunk"] < min(c, n_chunks) and not (n["chunk"] == moe_at and not n.get("moe")):
                    round_chunk(n["chunk"])
                    n["chunk"] += 1

            def row_stats(src, ready=None):
                i = n["norm"]
                if n["turn"]:
                    act.wait_ge(tr_done, n["turn"])
                for tt in range(TT):
                    if ready is not None:
                        act.wait_ge(*ready[tt])
                    act.activation(xn[:, tt, :], src[:, tt, :], ACT.Square,
                                   accum_out=sumsq[:, tt:tt + 1]).then_inc(ss_ready, 1)
                act.wait_ge(ms_ready, i + 1)
                act.activation(root, meansq, ACT.Sqrt).then_inc(rt_ready, 1)
                n["norm"] += 1

            def split_turned(x, gain):
                for kp in range(KT // 2):
                    fill = n["turn"]
                    act.wait_ge(tr_done, fill + 1)
                    for kk in range(2):
                        k = 2 * kp + kk
                        ins_ = act.activation(xhi[x][:, k, :], ps[6 + fill % 2][:, kk * TOK:kk * TOK + TOK], ACT.Copy,
                                              scale=1.0 if gain is None else cols[:, gain + k:gain + k + 1])
                    ins_.then_inc(xhi_ready, 1)
                    n["turn"] += 1

            def exps(width, src, scale, in_bank):
                u = n["unit"]
                act.wait_ge(nm_ready, u + 1)
                if in_bank:
                    act.wait_ge(t_done, slot_free(u))
                if width == CAUSAL_W:
                    parts = (slice(0, P), slice(P, CAUSAL_W))
                else:
                    parts = (slice(0, TOK), slice(TOK, 2 * TOK))
                for tt, cols_ in enumerate(parts):
                    ins_ = act.activation(prob_slot(u)[:, cols_], src[:, cols_], ACT.Exp, scale=scale,
                                          bias=nmax[:, stat_cols(u, tt)], accum_out=psum_e[:, stat_cols(u, tt)])
                ins_.then_inc(e_ready, 1)
                n["unit"] += 1

            def copy_probs(width):
                hd = n["head"]
                act.wait_ge(t_done, hd + 1)
                if hd >= 2:
                    act.wait_ge(o_done, hd - 1)
                act.activation(prob_t[:, hd % 2, 0:width], turned_bank(hd)[:, 0:width], ACT.Copy).then_inc(pt_ready, 1)
                n["head"] += 1

            def out_hi(x, k0, tiles, heads):
                act.wait_ge(o_done, heads)
                act.activation(xhi[x][:, k0:k0 + tiles, :], out_bank(heads - 1)[:, 0:tiles * TOK].rearrange("p (a b) -> p a b", a=tiles),
                               ACT.Copy).then_inc(o_hi, 1)
                n["ohi"] += 1

            def bank_rows(c):
                return linear_bank(c)[:, :].rearrange("p (t n) -> p t n", t=2)

            def used(c):
                act.wait_ge(chunk_used, c + 1)

            at_row = [0]

            def rows(dst, r0, src):
                n = src.shape[0]
                act.dma_start(dst[r0:r0 + n, :], src).then_inc(in_rows, 16)
                at_row[0] += 1

            for r0, name in ((G_MIX, "norm_mix"), (G_XQ, "norm_xq"), (G_MEM, "norm_mem")):
                rows(rows_a, r0, ins[name][0].rearrange("(k p) -> k p", p=P))
            for r0, name in ((G_FFN1, "ffn1_norm_g_2"), (G_MIX2, "mix_norm_g_2"), (G_MEM2, "mem_norm_g_2"),
                             (G_FFN2, "ffn2_norm_g_2")):
                rows(rows_a, r0, ins[name].rearrange("l (k p) -> (l k) p", p=P))
            rows(rows_a, G_KV, ins["kv_norm_g_2"].rearrange("(k p) -> k p", p=P))
            for r0, name in ((G_LNG, "a_ln_g_2"), (G_LNB, "a_ln_b_2"), (G_DWB, "a_dw_bias_2")):
                rows(rows_a, r0, ins[name][0].rearrange("(k p) -> k p", p=P))
            rows(rows_a, G_SGUB, ins["sgu_b"][0])
            taps = ins["a_dw_kernel_2"][0].rearrange("j o (k p) -> (j o k) p", p=P)
            rows(rows_b, 0, taps[0:P])
            rows(rows_c, 0, taps[P:DW_ROWS])
            for half in (0, 64):
                for r, (name, layers) in ((HG_MQ, ("mem_q_norm_g_2", 2)), (HG_MK, ("mem_k_norm_g_2", 2)),
                                     (HG_K, ("k_norm_g_2", 1)), (HG_Q, ("b_q_norm_g_2", 1))):
                    src = ins[name] if name != "k_norm_g_2" else ins[name].rearrange("(o p) -> o p", o=1)
                    r0 = DW_ROWS - P + r
                    act.dma_start(rows_c[r0:r0 + layers, half:half + 64], src).then_inc(in_rows, 16)
                    at_row[0] += 1
            assert at_row[0] == 22
            row_stats(h, ((in_x[0], 16), (in_x[1], 16)))
            round_to(1)
            act.wait_ge(cols_ready, 1)
            split_turned(0, G_MIX)
            round_to(3)
            for c in range(10):
                round_to(c + 3)
                if c < 4:
                    used(c)
                    dst = (u_a if c < 2 else v_a)[:, :, (c % 2) * CW:(c % 2) * CW + CW]
                    act.activation(dst, bank_rows(c), ACT.Gelu).then_inc(evac_a, 1)
                if c == 4:
                    act.wait_ge(in_mem, 16)
                    row_stats(mem_a)
                if c == 6:
                    act.wait_ge(bn_ready, 1)
                    act.activation(ort, oms, ACT.Sqrt).then_inc(bn_root, 1)
                    act.wait_ge(lam_ready, 1)
                    act.activation(lame, lams, ACT.Exp).then_inc(lam_exp, 1)
                    act.wait_ge(rope_half, 1)
                    act.activation(sin_t, f_silu[:, 0, :], ACT.Sin).then_inc(rope_sin, 1)
                    act.activation(cos_t, f_silu[:, 0, :], ACT.Sin, scale=0.5).then_inc(rope_sin, 1)
            act.wait_ge(wt_ready, 1)
            act.activation(sgu_wt.rearrange("p a b -> p (a b)"), ps[4][:, :], ACT.Copy).then_inc(wt_copied, 1)
            split_turned(1, G_MEM)
            for hd in range(4):
                for c in (10 + 2 * hd, 11 + 2 * hd):
                    slope = 2.0 ** (-8.0 * (hd + 1) / 4)
                    exps(CAUSAL_W, prob[:, n["unit"] % 2, :], slope, False)
                    round_to(c + 3)
                copy_probs(CAUSAL_W)
                act.wait_ge(o_copied, hd + 1)
                for tt in range(TT):
                    act.activation(u_a[:, tt, hd * P:hd * P + P], xn[:, tt, 512 + hd * P:512 + hd * P + P],
                                   ACT.Square, accum_out=oss[:, 2 * hd + tt:2 * hd + tt + 1]).then_inc(o_ss, 1)
            act.wait_ge(o_ms, 1)
            act.activation(ort, oms, ACT.Sqrt).then_inc(o_rt, 1)
            split_turned(0, None)
            for c in range(18, 22):
                round_to(c + 3)
            act.wait_ge(h_ready, 1)
            row_stats(h)
            split_turned(1, G_XQ)

            def queries(c):
                round_to(c + 3)
                used(c)
                act.activation(q1_t[:, 2 * (c - 22):2 * (c - 22) + 2, :], bank_rows(c), ACT.Copy).then_inc(evac_a, 1)

            def full_exps(scale):
                u = n["unit"]
                exps(512, ps[4 + u % 2], scale, True)

            queries(22)
            queries(23)
            full_exps(1.0 / 16)
            queries(24)
            full_exps(1.0 / 16)
            copy_probs(512)
            out_hi(0, 0, 2, 5)
            queries(25)
            full_exps(1.0 / 16)
            copy_probs(512)
            out_hi(0, 2, 2, 6)
            full_exps(1.0 / 16)
            copy_probs(512)
            out_hi(0, 4, 2, 7)
            copy_probs(512)
            out_hi(0, 6, 2, 8)
            for c in range(26, 30):
                round_to(c + 3)
            act.wait_ge(h_ready, 2)
            row_stats(h)
            split_turned(0, None)
            act.wait_ge(in_late, 64)
            act.activation(wr_hi, wr_raw, ACT.Copy).then_inc(wr_split, 1)
            act.wait_ge(r_bias, 1)
            for tt in range(TT):
                ins_ = act.activation(prob[:, 0, 4 * tt:4 * tt + 4], glog[:, 8 * tt:8 * tt + 4], ACT.Exp,
                                      bias=gneg[:, tt:tt + 1], accum_out=gsum[:, tt:tt + 1])
            ins_.then_inc(r_exp, 1)
            act.wait_ge(r_ediff, 1)
            act.activation(eexp, ediff, ACT.Exp).then_inc(r_eexp, 1)

            def copy_gathered(half, count):
                act.wait_ge(main["fill"], count)
                act.activation(xg[:, 4 * half:4 * half + 4, :], ps[5][:, :].rearrange("p (k n) -> p k n", k=4),
                               ACT.Copy).then_inc(main["evac"], 1)

            def copy_spread(half, count):
                act.wait_ge(main["fill"], count)
                act.activation(spread[:, 2 * half:2 * half + 2, :], ps[5][:, :].rearrange("p (k n) -> p k n", k=2),
                               ACT.Copy).then_inc(main["evac"], 1)

            def expert_silu(s, count):
                act.wait_ge(s["gu"], count)
                act.activation(e_silu, ps[4][:, 0:P], ACT.Silu).then_inc(s["silu"], 1)

            def expert_out(s, first_half):
                act.wait_ge(s["y_full"], first_half)
                act.activation(y_sb[:, 0:512], ps[6][:, :], ACT.Copy).then_inc(s["y0"], 1)

            copy_gathered(0, 1)
            copy_gathered(1, 2)
            with act.Fori(0, EXPERTS // EG) as g:
                for e in range(EG):
                    expert_silu(main, 4 * g + e + 1)
                    if e == 0:
                        copy_spread(0, 4 * g + 3)
                        copy_spread(1, 4 * g + 4)
                    expert_out(main, 8 * g + 2 * e + 1)
                copy_gathered(0, 4 * g + 5)
                copy_gathered(1, 4 * g + 6)
            act.wait_ge(extra_ready, 1)
            extra = act.value_load(extra_i[0:1, 0:1], min_val=0, max_val=MAX_ROUNDS - 1)
            with act.If(extra > 0):
                with act.Fori(0, extra) as r:
                    with act.Fori(0, EXPERTS) as x:
                        step = EXPERTS * r + x + 1
                        act.wait_ge(over["fill"], step)
                        act.activation(xg[:, :, 0:SLOTS], ps[5][:, 0:256].rearrange("p (k n) -> p k n", k=KT), ACT.Copy)
                        act.activation(spread[:, 0, :], ps[5][:, 256:512], ACT.Copy).then_inc(over["evac"], 1)
                        expert_silu(over, step)
                        expert_out(over, 2 * step - 1)

            act.wait_ge(moe_done, 1)
            n["moe"] = True
            act.wait_ge(in_mem2, 16)
            row_stats(mem2_a)
            split_turned(1, G_MEM2)
            split_turned(0, G_MEM2 + 8)
            act.wait_ge(h_added, 1)
            row_stats(h)

            def head_squares(c):
                used(c)
                if n["hs"] >= 1:
                    act.wait_ge(hs_done, n["hs"])
                act.activation(prob[:, 0, :], linear_bank(c)[:, :], ACT.Square).then_inc(sq_ready, 1)

            def head_root():
                act.wait_ge(hms_ready, n["hs"] + 1)
                act.activation(prob[:, 1, :], prob[:, 1, :], ACT.Sqrt).then_inc(hrt_ready, 1)
                n["hs"] += 1

            def swiglu(q):
                s, b = ffn_starts[q], PAIRS * q
                round_to(s + 3)

                def silus(i, cb):
                    act.wait_ge(gu0_done, i + (b + 1))
                    act.activation(f_silu[:, 0, :], ps[4][:, 0:TOK], ACT.Silu).then_inc(silu_ready, 1)
                    act.wait_ge(chunk_used, cb + 2)
                    act.activation(f_silu[:, 1, :], ps[5][:, 0:TOK], ACT.Silu).then_inc(silu_ready, 1)

                with act.Fori(0, PAIRS // 2) as it:
                    for half in range(2):
                        i, cb = 2 * it + half, 6 * it + (s + 3 * half)
                        for j in range(3):
                            c0_ = s + 3 * half + 3 + j
                            act.wait_ge(raw_in[c0_ % RAW], 16 * it + landed(c0_))
                            act.wait_ge(chunk_used, 6 * it + (c0_ - SPLIT + 1))
                            act.activation(whi[:, c0_ % SPLIT, :], raw[:, c0_ % RAW, :], ACT.Copy).then_inc(hi_ready, 1)
                            if j == 0:
                                silus(i, cb)
                n["chunk"] = s + 3 * PAIRS
                cb = s + 3 * (PAIRS - 1)
                round_to(cb + 4)
                silus(PAIRS - 1, cb)
                round_to(cb + 6)

            for layer in range(2):
                c = moe_at + 2 * layer
                round_to(c + 3)
                head_squares(c)
                round_to(c + 4)
                head_root()
            act.wait_ge(h_ready, 3)
            row_stats(h)
            split_turned(1, G_FFN1)
            swiglu(0)
            row_stats(h, ((h_tile, 1), (h_ready, 4)))
            split_turned(0, G_MIX2)
            c0 = ffn_starts[0] + 3 * PAIRS
            for i in range(3):
                round_to(c0 + 2 * i + 4)
                used(c0 + 2 * i + 1)
                if i >= 1:
                    act.wait_ge(glu_done, i)
                act.activation(sig, bank_rows(c0 + 2 * i + 1), ACT.Sigmoid).then_inc(sig_ready, 1)
            round_to(c0 + 9)
            head_squares(c0 + 6)
            head_root()

            def attend(widths, x, tiles):
                first = n["head"]
                for s in range(len(widths) + 4):
                    if s < len(widths):
                        if widths[s] == CAUSAL_W:
                            exps(CAUSAL_W, prob_slot(n["unit"]), 1.0, False)
                        else:
                            full_exps(0.125)
                    if 2 <= s < len(widths) + 2:
                        copy_probs(widths[s - 2])
                    if s >= 5 and s % 2:
                        out_hi(x, tiles[(s - 5) // 2], 1, first + s - 3)

            attend([512] * 4, 1, (6, 7))
            act.wait_ge(csum_done, 1)
            act.activation(prob[:, 0, 0:TOK], ps[6][:, 0:TOK], ACT.Copy, scale=1.0 / 768).then_inc(cmu_ready, 1)
            act.wait_ge(cent_ready, 1)
            act.activation(conv_sq, conv_out, ACT.Square).then_inc(csq_ready, 1)
            act.wait_ge(cms_ready, 1)
            act.activation(prob[:, 0, 0:TOK], prob[:, 1, 0:TOK], ACT.Sqrt).then_inc(crt_ready, 1)
            act.wait_ge(cn_ready, 1)
            for ct in range(CONV_TILES):
                ins_ = act.activation(conv_sq[:, ct, :], conv_out[:, ct, :], ACT.Silu, scale=cols[:, G_LNG + ct:G_LNG + ct + 1],
                                      bias=cols[:, G_LNB + ct:G_LNB + ct + 1])
            ins_.then_inc(csilu_ready, 1)
            act.wait_ge(csilu_ready, 1)
            act.activation(xhi[1][:, 0:CONV_TILES, :], conv_sq, ACT.Copy).then_inc(chi_ready, 1)
            round_to(c0 + 14)
            act.wait_ge(h_ready, 5)
            row_stats(h)
            split_turned(0, G_FFN2)
            swiglu(1)
            row_stats(h, ((h_tile, 2), (h_ready, 6)))
            split_turned(1, G_KV)
            c0 = ffn_starts[1] + 3 * PAIRS
            split_turned(0, G_FFN1 + 8)
            for i in range(3):
                round_to(c0 + i + 4)
                head_squares(c0 + i)
                head_root()
            round_to(c0 + 9)
            swiglu(2)
            row_stats(h, ((h_tile, 3), (h_ready, 7)))
            split_turned(1, G_MIX2 + 8)
            c0 = ffn_starts[2] + 3 * PAIRS
            for i in range(4):
                round_to(c0 + i + 4)
                head_squares(c0 + i)
                head_root()
            attend([CAUSAL_W] * 12 + [512] * 4, 0, range(8))
            round_to(c0 + 11)
            act.wait_ge(h_ready, 8)
            row_stats(h)
            split_turned(1, G_FFN2 + 8)
            swiglu(3)

        @block.vector
        def _(dve):
            n = {"chunk": 0, "norm": 0, "turn": 0, "unit": 0, "head": 0, "out": 0, "hs": 0, "rot": 0, "link": 0, "h": 0}

            def link(ins_):
                n["link"] += 1
                ins_.then_inc(v_link, 1)
                dve.wait_ge(v_link, n["link"])

            def split_chunk(c):
                dve.wait_ge(hi_ready, c + 1)
                dve.tensor_tensor(wlo[:, c % SPLIT, :], raw[:, c % RAW, :], whi[:, c % SPLIT, :].bitcast(F32),
                                  ALU.subtract).then_inc(lo_ready, 1)

            def split_to(c):
                while n["chunk"] < min(c, n_chunks) and not (n["chunk"] == moe_at and not n.get("moe")):
                    split_chunk(n["chunk"])
                    n["chunk"] += 1

            def row_scale():
                i = n["norm"]
                dve.wait_ge(ss_ready, 2 * i + 2)
                dve.tensor_scalar(meansq, sumsq, 1.0 / D, RMS_EPS, ALU.mult, ALU.add).then_inc(ms_ready, 1)
                dve.wait_ge(rt_ready, i + 1)
                link(dve.reciprocal(rstd, root))
                n["norm"] += 1

            def normed_rows(src):
                row_scale()
                for tt in range(TT):
                    dve.tensor_scalar(xn[:, tt, :], src[:, tt, :], rstd[:, tt:tt + 1], None, ALU.mult).then_inc(xn_ready, 1)

            def split_turned(x, gain):
                for kp in range(KT // 2):
                    fill = n["turn"]
                    dve.wait_ge(xhi_ready, fill + 1)
                    for kk in range(2):
                        k = 2 * kp + kk
                        src = ps[6 + fill % 2][:, kk * TOK:kk * TOK + TOK]
                        if gain is None:
                            ins_ = dve.tensor_tensor(xlo[x][:, k, :], src, xhi[x][:, k, :].bitcast(F32), ALU.subtract)
                        else:
                            ins_ = dve.scalar_tensor_tensor(xlo[x][:, k, :], src, cols[:, gain + k:gain + k + 1],
                                                            xhi[x][:, k, :].bitcast(F32), ALU.mult, ALU.subtract)
                    ins_.then_inc(xlo_ready, 1)
                    n["turn"] += 1

            def bank_rows(c):
                return linear_bank(c)[:, :].rearrange("p (t n) -> p t n", t=2)

            def used(c):
                dve.wait_ge(chunk_used, c + 1)

            def copy_out(c, dst):
                used(c)
                dve.tensor_copy(dst, bank_rows(c)).then_inc(evac_v, 1)

            def add_to_h(c, j):
                used(c)
                dst = h[:, :, j * CW:j * CW + CW]
                dve.tensor_tensor(dst, dst, bank_rows(c), ALU.add).then_inc(evac_v, 1)

            def h_updated():
                dve.wait_ge(evac_v, evac_count[n["last_h"]][1])
                dve.tensor_copy(bn2[:, 0:1], rstd[:, 0:1]).then_inc(h_ready, 1)

            def causal_max(bias, mult, slope):
                u = n["unit"]
                slot, nm = prob_slot(u), nmax[:, stat_cols(u)]
                dve.wait_ge(s_full, u + 1)
                if slot_free(u):
                    dve.wait_ge(t_done, slot_free(u))
                link(dve.scalar_tensor_tensor(slot[:, 0:CAUSAL_W], ps[4 + u % 2][:, 0:CAUSAL_W], mult, bias,
                                              ALU.mult, ALU.add))
                dve.tensor_reduce(nm[:, 0:1], slot[:, 0:P], AX, ALU.max, negate=True)
                ins_ = dve.tensor_reduce(nm[:, 1:2], slot[:, P:CAUSAL_W], AX, ALU.max, negate=True)
                if slope != 1.0:
                    link(ins_)
                    ins_ = dve.tensor_scalar(nm, nm, slope, None, ALU.mult)
                ins_.then_inc(nm_ready, 1)
                n["unit"] += 1

            def full_max(scale):
                u = n["unit"]
                dve.wait_ge(s_full, u + 1)
                nm = nmax[:, stat_cols(u)]
                link(dve.tensor_reduce(nm, ps[4 + u % 2][:, :].rearrange("p (t n) -> p t n", t=2), AX, ALU.max, negate=True))
                dve.tensor_scalar(nm, nm, scale, None, ALU.mult).then_inc(nm_ready, 1)
                n["unit"] += 1

            def probs(u, width):
                dve.wait_ge(e_ready, u + 1)
                r, slot = rsum[:, stat_cols(u)], prob_slot(u)
                link(dve.reciprocal(r, psum_e[:, stat_cols(u)]))
                parts = (slice(0, P), slice(P, CAUSAL_W)) if width == CAUSAL_W else (slice(0, TOK), slice(TOK, 2 * TOK))
                for tt, cols_ in enumerate(parts):
                    ins_ = dve.tensor_scalar(slot[:, cols_], slot[:, cols_], r[:, tt:tt + 1], None, ALU.mult)
                ins_.then_inc(p_ready, 1)
                n["head"] += 1

            def diff_probs(hd):
                dve.wait_ge(e_ready, 2 * hd + 2)
                link(dve.reciprocal(rsum[:, 0:4], psum_e[:, 0:4]))
                link(dve.tensor_scalar(rsum[:, 2:4], rsum[:, 2:4], neglam, None, ALU.mult))
                parts = (slice(0, P), slice(P, CAUSAL_W))
                for tt, cols_ in enumerate(parts):
                    ins_ = dve.tensor_scalar(prob[:, 0, cols_], prob[:, 0, cols_], rsum[:, tt:tt + 1], None, ALU.mult)
                link(ins_)
                for tt, cols_ in enumerate(parts):
                    ins_ = dve.scalar_tensor_tensor(prob[:, 0, cols_], prob[:, 1, cols_], rsum[:, 2 + tt:3 + tt],
                                                    prob[:, 0, cols_], ALU.mult, ALU.add)
                ins_.then_inc(p_ready, 1)
                n["head"] += 1

            def out_lo(x, k0, tiles, head):
                dve.wait_ge(o_hi, n["olo"] + 1)
                dve.tensor_tensor(xlo[x][:, k0:k0 + tiles, :], out_bank(head)[:, 0:tiles * TOK].rearrange("p (a b) -> p a b", a=tiles),
                                  xhi[x][:, k0:k0 + tiles, :].bitcast(F32), ALU.subtract).then_inc(o_evac, 1)
                n["olo"] += 1

            n["olo"] = 0

            dve.memset(zeros[:, :], 0.0).then_inc(zero_ready, 1)
            for tt in range(TT):
                dve.wait_ge(in_x[tt], 16)
            normed_rows(h)
            dve.wait_ge(cols_t, 1)
            m = DW_ROWS - P + 6
            dve.tensor_copy(cols[:, 0:G_A], ps[5][:, 0:G_A])
            dve.tensor_copy(cols[:, 128:256 + m], ps[5][:, 128:256 + m]).then_inc(cols_ready, 1)
            split_to(1)
            split_turned(0, G_MIX)
            split_to(3)
            for c in range(10):
                split_to(c + 3)
                if 4 <= c < 6:
                    copy_out(c, q_t[:, 2 * (c - 4):2 * (c - 4) + 2, :])
                elif 6 <= c < 8:
                    copy_out(c, k_t[:, 2 * (c - 6):2 * (c - 6) + 2, :])
                elif c >= 8:
                    copy_out(c, val_a[:, :, (c - 8) * CW:(c - 8) * CW + CW])
                if c == 4:
                    row_scale()
                    dve.wait_ge(in_mem, 16)
                    for tt in range(TT):
                        dve.tensor_scalar(xn[:, tt, :], mem_a[:, tt, :], rstd[:, tt:tt + 1], None, ALU.mult).then_inc(xn_ready, 1)
                if c == 5:
                    dve.wait_ge(evac_a, 4)
                    for i in range(8):
                        tt, g = i // 4, i % 4
                        ins_ = dve.bn_stats(bn6[:, 6 * i:6 * i + 6], v_a[:, tt, g * P:g * P + P])
                    link(ins_)
                    for i in range(8):
                        ins_ = dve.bn_aggr(bn2[:, 2 * i:2 * i + 2], bn6[:, 6 * i:6 * i + 6])
                    link(ins_)
                    dve.tensor_scalar(oms, bn2[:, 1:16:2], LN_EPS, None, ALU.add).then_inc(bn_ready, 1)
                if c == 6:
                    dve.wait_ge(in_bc, 16 * 8)
                    link(dve.tensor_tensor(lamv[:, 0:4:2, :], lamv[:, 0:4:2, :], lamv[:, 1:4:2, :], ALU.mult))
                    dve.tensor_reduce(lams, lamv[:, 0:4:2, :], AX, ALU.add).then_inc(lam_ready, 1)
                    ang, turns = f_silu[:, 0, :], f_silu[:, 1, :]
                    link(dve.tensor_copy(ang, posi))
                    link(dve.tensor_scalar(ang, ang, cst[:, C_FREQ:C_FREQ + 1], None, ALU.mult))
                    link(dve.tensor_scalar(turns, ang, float(np.float32(1 / (2 * np.pi))), MAGIC, ALU.mult, ALU.add))
                    link(dve.tensor_scalar(turns, turns, MAGIC, None, ALU.subtract))
                    for part in TWO_PI:
                        link(dve.scalar_tensor_tensor(ang, turns, -part, ang, ALU.mult, ALU.add))
                    dve.tensor_scalar(ang, ang, -3.1415925, 3.1415925, ALU.max, ALU.min).then_inc(rope_half, 1)
                if c == 7:
                    dve.wait_ge(lam_exp, 1)
                    dve.scalar_tensor_tensor(neglam, lame[:, 1:2], -LAMBDA_INIT, lame[:, 0:1], ALU.add, ALU.subtract)
                    dve.tensor_scalar(subln[:, :], subln[:, :], 1.0 - LAMBDA_INIT, None, ALU.mult)
                    dve.wait_ge(rope_sin, 2)
                    link(dve.tensor_tensor(cos_t, cos_t, cos_t, ALU.mult))
                    dve.tensor_scalar(cos_t, cos_t, -2.0, 1.0, ALU.mult, ALU.add)
                    dve.wait_ge(in_sgu, 48)
                    for g in range(4):
                        ins_ = dve.tensor_tensor(sgu_w[:, g, :], sgu_w[:, g, :], cst[:, C_TRIL:C_TRIL + P], ALU.mult)
                    ins_.then_inc(wt_done, 1)
                    dve.wait_ge(bn_root, 1)
                    link(dve.reciprocal(ors, ort))
                    for i in range(8):
                        v = v_a[:, i // 4, (i % 4) * P:(i % 4) * P + P]
                        ins_ = dve.tensor_scalar(v, v, bn2[:, 2 * i:2 * i + 1], ors[:, i:i + 1], ALU.subtract, ALU.mult)
                    link(ins_)
                    for j, op in enumerate((ALU.mult, ALU.add)):
                        for tt in range(TT):
                            ins_ = dve.tensor_tensor(v_a[:, tt, :], v_a[:, tt, :], ln_gb[:, j, :], op)
                        if j == 0:
                            link(ins_)
                    ins_.then_inc(vn_ready, 1)
            split_turned(1, G_MEM)
            for tt in range(TT):
                dve.wait_ge(sp_done, tt + 1)
                for g in range(4):
                    ins_ = dve.scalar_tensor_tensor(xn[:, tt, g * P:g * P + P], ps[4 + tt][:, g * P:g * P + P],
                                                    cols[:, G_SGUB + g:G_SGUB + g + 1], u_a[:, tt, g * P:g * P + P],
                                                    ALU.add, ALU.mult)
            ins_.then_inc(sgu_done, 1)
            for hd in range(4):
                slope = 2.0 ** (-8.0 * (hd + 1) / 4)
                for c in (10 + 2 * hd, 11 + 2 * hd):
                    causal_max(cst[:, C_ND:C_ND + CAUSAL_W], 0.125 / slope, slope)
                    split_to(c + 3)
                diff_probs(hd)
                for c in (10 + 2 * hd, 11 + 2 * hd):
                    if c < 14:
                        copy_out(c, k1_t[:, 2 * (c - 10):2 * (c - 10) + 2, :])
                    else:
                        copy_out(c, v1_a[:, :, (c - 14) * CW:(c - 14) * CW + CW])
                dve.wait_ge(o_done, hd + 1)
                dve.tensor_copy(xn[:, :, 512 + hd * P:512 + hd * P + P],
                                ps[O_BANK][:, 0:2 * P].rearrange("p (t n) -> p t n", t=2)).then_inc(o_evac, 1)
                dve.wait_ge(o_evac, hd + 1)
                dve.tensor_copy(bn2[:, 0:1], rstd[:, 0:1]).then_inc(o_copied, 1)
            dve.wait_ge(o_ss, 8)
            dve.tensor_scalar(oms, oss, 1.0 / P, RMS_EPS, ALU.mult, ALU.add).then_inc(o_ms, 1)
            dve.wait_ge(o_rt, 1)
            link(dve.reciprocal(ors, ort))
            for hd in range(4):
                for tt in range(TT):
                    o = xn[:, tt, 512 + hd * P:512 + hd * P + P]
                    ins_ = dve.scalar_tensor_tensor(o, o, ors[:, 2 * hd + tt:2 * hd + tt + 1], subln[:, :], ALU.mult, ALU.mult)
            ins_.then_inc(mixed_ready, 1)
            split_turned(0, None)
            for c in range(18, 22):
                split_to(c + 3)
                add_to_h(c, c - 18)
            n["last_h"] = 21
            h_updated()
            normed_rows(h)
            split_turned(1, G_XQ)
            split_to(26)
            full_max(1.0 / 16)
            split_to(27)
            full_max(1.0 / 16)
            probs(8, 512)
            split_to(28)
            full_max(1.0 / 16)
            out_lo(0, 0, 2, 4)
            probs(9, 512)
            out_lo(0, 2, 2, 5)
            full_max(1.0 / 16)
            probs(10, 512)
            out_lo(0, 4, 2, 6)
            probs(11, 512)
            out_lo(0, 6, 2, 7)
            for c in range(26, 30):
                split_to(c + 3)
                add_to_h(c, c - 26)
            n["last_h"] = 29
            h_updated()
            row_scale()
            dve.wait_ge(in_late, 64)
            for tt in range(TT):
                ins_ = dve.tensor_scalar(xn[:, tt, :], h[:, tt, :], rstd[:, tt:tt + 1], None, ALU.mult)
            link(ins_)
            for tt in range(TT):
                dve.tensor_tensor(xn[:, tt, :], xn[:, tt, :], gain_b[:, 0, :], ALU.mult).then_inc(xn_ready, 1)
            dve.memset(glog, -3e38)
            dve.memset(posm[:, :, EXPERTS:], -1.0)
            dve.memset(wgt[:, :, EXPERTS:], 0.0)
            split_turned(0, None)
            dve.wait_ge(wr_split, 1)
            dve.tensor_tensor(wr_lo, wr_raw, wr_hi.bitcast(F32), ALU.subtract).then_inc(wr_ready, 1)
            dve.wait_ge(r_done, 1)
            for tt in range(TT):
                ins_ = dve.tensor_tensor(logit[:, 36 * tt:36 * tt + 36], ps[4][:, 36 * tt:36 * tt + 36], rb, ALU.add)
            link(ins_)
            for tt in range(TT):
                ins_ = dve.tensor_copy(glog[:, 8 * tt:8 * tt + 4], logit[:, 36 * tt:36 * tt + 4])
            link(ins_)
            for tt in range(TT):
                ins_ = dve.max(gmax[:, 8 * tt:8 * tt + 8], glog[:, 8 * tt:8 * tt + 8])
            link(ins_)
            for tt in range(TT):
                ins_ = dve.max_index(picks[:, 0, tt, :], gmax[:, 8 * tt:8 * tt + 8], glog[:, 8 * tt:8 * tt + 8])
            link(ins_)
            dve.tensor_copy(gidx, picks[:, 0, :, 0])
            dve.tensor_scalar(gneg, gmax[:, 0:16:8], -1.0, None, ALU.mult).then_inc(r_bias, 1)
            dve.wait_ge(r_bias, 1)
            for tt in range(TT):
                ins_ = dve.tensor_scalar(emask[:, 32 * tt:32 * tt + 32], cst[:, C_GRP:C_GRP + 32], gidx[:, tt:tt + 1], None,
                                         ALU.is_equal)
            link(ins_)
            for tt in range(TT):
                lg = logit[:, 36 * tt + 4:36 * tt + 36]
                ins_ = dve.tensor_tensor(lg, lg, emask[:, 32 * tt:32 * tt + 32], ALU.mult)
            link(ins_)
            link(dve.tensor_scalar(emask, emask, -NEG, NEG, ALU.mult, ALU.add))
            for tt in range(TT):
                lg = logit[:, 36 * tt + 4:36 * tt + 36]
                ins_ = dve.tensor_tensor(lg, lg, emask[:, 32 * tt:32 * tt + 32], ALU.add)
            link(ins_)
            for tt in range(TT):
                ins_ = dve.max(emax[:, 8 * tt:8 * tt + 8], logit[:, 36 * tt + 4:36 * tt + 36])
            link(ins_)
            for tt in range(TT):
                ins_ = dve.max_index(picks[:, 1, tt, :], emax[:, 8 * tt:8 * tt + 8], logit[:, 36 * tt + 4:36 * tt + 36])
            link(ins_)
            dve.tensor_copy(eidx[:, 0:4].rearrange("p (t i) -> p t i", t=2), picks[:, 1, :, 0:2])
            dve.tensor_tensor(ediff, emax[:, 1:16:8], emax[:, 0:16:8], ALU.subtract).then_inc(r_ediff, 1)
            dve.wait_ge(r_exp, 1)
            link(dve.reciprocal(ggate, gsum))
            dve.wait_ge(r_eexp, 1)
            link(dve.tensor_scalar(eden, eexp, 1.0, None, ALU.add))
            link(dve.reciprocal(eden, eden))
            link(dve.tensor_tensor(w1, ggate, eden, ALU.mult))
            link(dve.tensor_tensor(w2, w1, eexp, ALU.mult))
            for tt in range(TT):
                dve.tensor_scalar(hot[:, tt, :], slot_row, eidx[:, 2 * tt:2 * tt + 1], None, ALU.is_equal)
                ins_ = dve.tensor_scalar(hot2[:, tt, :], slot_row, eidx[:, 2 * tt + 1:2 * tt + 2], None, ALU.is_equal)
            link(ins_)
            for tt in range(TT):
                ins_ = dve.tensor_scalar(wgt[:, tt, 0:EXPERTS], hot[:, tt, :], w1[:, tt:tt + 1], None, ALU.mult)
            link(ins_)
            for tt in range(TT):
                ins_ = dve.scalar_tensor_tensor(wgt[:, tt, 0:EXPERTS], hot2[:, tt, :], w2[:, tt:tt + 1],
                                                wgt[:, tt, 0:EXPERTS], ALU.mult, ALU.add)
            dve.tensor_tensor(hot[:, :, :], hot[:, :, :], hot2[:, :, :], ALU.add).then_inc(hot_ready, 1)
            dve.wait_ge(hot_ready, 1)
            dve.wait_ge(pos_done, 1)
            for tt in range(TT):
                ins_ = dve.scalar_tensor_tensor(posm[:, tt, 0:EXPERTS], ps[5][:, 32 * tt:32 * tt + 32], 1.0, hot[:, tt, :],
                                                ALU.add, ALU.mult)
            link(ins_)
            link(dve.tensor_scalar(posm[:, :, 0:EXPERTS], posm[:, :, 0:EXPERTS], -1.0, None, ALU.add))
            link(dve.tensor_reduce(tmax, ps[5][:, 64:96], AX, ALU.max))
            link(dve.tensor_scalar(thr, cst[:, C_THR:C_THR + 8], tmax, None, ALU.is_lt))
            link(dve.tensor_reduce(extra_f, thr, AX, ALU.add))
            dve.tensor_copy(extra_i[:, :], extra_f).then_inc(extra_ready, 1)

            def select(g, s):
                for tt in range(TT):
                    at_ = posm[:, tt, bass.ds(g * EG, EG)]
                    ins_ = dve.tensor_tensor(sel[:, tt, :].rearrange("p (e s) -> p e s", e=EG),
                                             at_.unsqueeze(2).broadcast_to([P, EG, SLOTS]),
                                             slot_row.unsqueeze(1).broadcast_to([P, EG, SLOTS]), ALU.is_equal)
                ins_.then_inc(s, 1)

            def hidden(s, count):
                dve.wait_ge(s["silu"], count)
                dve.tensor_tensor(e_h, e_silu, ps[4][:, P:2 * P], ALU.mult).then_inc(s["hm"], 1)
                dve.wait_ge(s["ht_full"], count)
                dve.tensor_copy(e_ht, ps[4][:, 256:384]).then_inc(s["ht"], 1)

            def expert_out(s, halves):
                dve.wait_ge(s["y_full"], halves)
                dve.tensor_copy(y_sb[:, 512:1024], ps[7][:, :]).then_inc(s["y1"], 1)

            select(0, main["sel"])
            with dve.Fori(0, EXPERTS // EG) as g:
                dve.wait_ge(main["sel"], g + 1)
                for tt in range(TT):
                    one = sel[:, tt, :].rearrange("p (e s) -> p e s", e=EG)
                    share = wgt[:, tt, bass.ds(g * EG, EG)].unsqueeze(2).broadcast_to([P, EG, SLOTS])
                    for rep in range(4):
                        dst = selw[:, tt, :].rearrange("p (e r s) -> p e r s", e=EG, r=4)[:, :, rep, :]
                        ins_ = dve.tensor_tensor(dst, one, share, ALU.mult)
                ins_.then_inc(main["selw"], 1)
                dve.wait_ge(main["selw"], g + 1)
                dve.wait_ge(main["fill"], 4 * g + 2)
                select(g + 1, main["sel"])
                for e in range(EG):
                    hidden(main, 4 * g + e + 1)
                    expert_out(main, 8 * g + 2 * e + 2)
            extra = dve.value_load(extra_i[0:1, 0:1], min_val=0, max_val=MAX_ROUNDS - 1)
            with dve.If(extra > 0):
                with dve.Fori(0, extra) as r:
                    dve.wait_ge(over["spread"], EXPERTS * r + 1)
                    dve.tensor_scalar(posm[:, :, 0:EXPERTS], posm[:, :, 0:EXPERTS], -float(SLOTS), None,
                                      ALU.add).then_inc(over["sel"], 1)
                    dve.wait_ge(over["sel"], EXPERTS * r + r + 1)
                    dve.tensor_copy(bn2[:, 0:1], posm[:, 0, 0:1])
                    with dve.Fori(0, EXPERTS) as x:
                        step = EXPERTS * r + x + 1
                        dve.wait_ge(over["spread"], step)
                        for tt in range(TT):
                            ins_ = dve.tensor_scalar(sel[:, tt, 0:SLOTS], slot_row, posm[:, tt, bass.ds(x, 1)], None,
                                                     ALU.is_equal)
                        ins_.then_inc(over["sel"], 1)
                        dve.wait_ge(over["sel"], EXPERTS * r + r + x + 2)
                        for tt in range(TT):
                            for rep in range(4):
                                ins_ = dve.tensor_scalar(selw[:, tt, rep * SLOTS:rep * SLOTS + SLOTS], sel[:, tt, 0:SLOTS],
                                                         wgt[:, tt, bass.ds(x, 1)], None, ALU.mult)
                        ins_.then_inc(over["selw"], 1)
                        hidden(over, step)
                        expert_out(over, 2 * step)

            dve.wait_ge(moe_done, 1)
            n["moe"] = True
            row_scale()
            dve.wait_ge(in_mem2, 16)
            for tt in range(TT):
                dve.tensor_scalar(xn[:, tt, :], mem2_a[:, tt, :], rstd[:, tt:tt + 1], None, ALU.mult).then_inc(xn_ready, 1)
            for tt in range(TT):
                for half in range(2):
                    dst = h[:, tt, half * 512:half * 512 + 512]
                    ins_ = dve.tensor_tensor(dst, dst, ps[2 * tt + half][:, :], ALU.add)
            ins_.then_inc(h_added, 1)
            dve.wait_ge(h_added, 1)
            split_turned(1, G_MEM2)
            split_turned(0, G_MEM2 + 8)
            row_scale()
            for tt in range(TT):
                ins_ = dve.scalar_tensor_tensor(h[:, tt, :], h[:, tt, :], rstd[:, tt:tt + 1], gain_b[:, 1, :], ALU.mult, ALU.mult)
            ins_.then_inc(h_ready, 1)
            dve.wait_ge(h_ready, 3)

            def head_norm(c, dst, gain):
                dve.wait_ge(hs_done, n["hs"] + 1)
                dve.tensor_scalar(prob[:, 1, :], ps[7][:, :], 1.0 / 64, RMS_EPS, ALU.mult, ALU.add).then_inc(hms_ready, 1)
                dve.wait_ge(hrt_ready, n["hs"] + 1)
                link(dve.reciprocal(prob[:, 1, :], prob[:, 1, :]))
                link(dve.scalar_tensor_tensor(dst, bank_rows(c), cols[:, G_HEAD + gain:G_HEAD + gain + 1],
                                              prob[:, 1, :].rearrange("p (a b) -> p a b", a=2), ALU.mult, ALU.mult))
                n["hs"] += 1
                dve.tensor_copy(bn2[:, 0:1], rstd[:, 0:1]).then_inc(hn_ready, 1)
                dve.tensor_copy(bn2[:, 2:3], rstd[:, 0:1]).then_inc(evac_v, 1)

            def rope(qk):
                dve.wait_ge(rot_done, n["rot"] + 1)
                half_turned = prob_t[:, 0, :].rearrange("p (a b) -> p a b", a=2)
                for j in range(2):
                    dve.tensor_tensor(half_turned[:, j, :], ps[6][:, j * TOK:j * TOK + TOK], sin_t, ALU.mult)
                    ins_ = dve.tensor_tensor(qk[:, j, :], qk[:, j, :], cos_t, ALU.mult)
                link(ins_)
                dve.tensor_tensor(qk, qk, half_turned, ALU.add).then_inc(rope_done, 1)
                n["rot"] += 1

            def swiglu(q):
                s, b = ffn_starts[q], FT * q
                split_to(s + 3)

                def hidden_tile(i, j):
                    dve.wait_ge(silu_ready, 2 * i + (b + j + 1))
                    dve.tensor_tensor(f_prod[:, j, :], f_silu[:, j, :], ps[4 + j][:, TOK:2 * TOK], ALU.mult).then_inc(prod_ready, 1)
                    dve.wait_ge(prod_ready, 2 * i + (b + j + 1))
                    dve.tensor_copy(hh_hi[:, j, :], f_prod[:, j, :]).then_inc(hhi_ready, 1)
                    dve.wait_ge(hhi_ready, 2 * i + (b + j + 1))
                    dve.tensor_tensor(hh_lo[:, j, :], f_prod[:, j, :], hh_hi[:, j, :].bitcast(F32),
                                      ALU.subtract).then_inc(hlo_ready, 1)

                with dve.Fori(0, PAIRS // 2) as it:
                    for half in range(2):
                        for j in range(3):
                            c0_ = s + 3 * half + 3 + j
                            dve.wait_ge(hi_ready, 6 * it + (c0_ + 1))
                            dve.tensor_tensor(wlo[:, c0_ % SPLIT, :], raw[:, c0_ % RAW, :],
                                              whi[:, c0_ % SPLIT, :].bitcast(F32), ALU.subtract).then_inc(lo_ready, 1)
                            if j == 0:
                                hidden_tile(2 * it + half, 0)
                                hidden_tile(2 * it + half, 1)
                n["chunk"] = s + 3 * PAIRS
                cb = s + 3 * (PAIRS - 1)
                split_to(cb + 4)
                hidden_tile(PAIRS - 1, 0)
                hidden_tile(PAIRS - 1, 1)
                split_to(cb + 6)
                for tt in range(TT):
                    if tt == 0:
                        dve.wait_ge(ffn_half, q + 1)
                    else:
                        dve.wait_ge(chunk_used, s + 3 * PAIRS)
                    for half in range(2):
                        dst = h[:, tt, half * 512:half * 512 + 512]
                        ins_ = dve.scalar_tensor_tensor(dst, ps[2 * tt + half][:, :], 0.5, dst, ALU.mult, ALU.add)
                    ins_.then_inc(h_tile if tt == 0 else h_ready, 1)
                dve.wait_ge(h_ready, (4, 6, 7, 9)[q])

            for layer in range(2):
                c = moe_at + 2 * layer
                split_to(c + 4)
                head_norm(c, k2_t[layer], HG_MK + layer)
                copy_out(c + 1, v2_a[layer])
            normed_rows(h)
            split_turned(1, G_FFN1)
            swiglu(0)
            normed_rows(h)
            split_turned(0, G_MIX2)
            c0 = ffn_starts[0] + 3 * PAIRS
            dve.memset(conv_in[:, :, 0:CONV_TAPS - 1], 0.0)
            taps_left = [(2 * pair_ + t, j) for pair_ in range(2) for j in range(CONV_TAPS) for t in range(2)]

            def tap(times):
                for _ in range(min(times, len(taps_left))):
                    done = 4 * CONV_TAPS - len(taps_left)
                    ct, j = taps_left.pop(0)
                    w_j = cols[:, G_DW + 6 * j + ct:G_DW + 6 * j + ct + 1]
                    if j == 0:
                        ins_ = dve.tensor_scalar(conv_out[:, ct, :], conv_in[:, ct, 0:TOK], w_j,
                                                 cols[:, G_DWB + ct:G_DWB + ct + 1], ALU.mult, ALU.add)
                    else:
                        dve.wait_ge(tap_done, done - 1)
                        ins_ = dve.scalar_tensor_tensor(conv_out[:, ct, :], conv_in[:, ct, j:j + TOK], w_j,
                                                        conv_out[:, ct, :], ALU.mult, ALU.add)
                    ins_.then_inc(tap_done, 1)

            for i in range(3):
                for c in range(c0 + 2 * i + 2, c0 + 2 * i + 4):
                    split_to(c)
                    if i >= 1:
                        tap(8)
                split_to(c0 + 2 * i + 4)
                dve.wait_ge(sig_ready, i + 1)
                dve.tensor_tensor(conv_in[:, 2 * i:2 * i + 2, CONV_TAPS - 1:], sig, bank_rows(c0 + 2 * i), ALU.mult).then_inc(glu_done, 1)
                dve.wait_ge(glu_done, i + 1)
                dve.tensor_copy(bn2[:, 0:1], rstd[:, 0:1]).then_inc(evac_v, 1)
                dve.tensor_copy(bn2[:, 2:3], rstd[:, 0:1]).then_inc(evac_v, 1)
            split_to(c0 + 9)
            tap(8)
            head_norm(c0 + 6, qm_t, HG_MQ)

            def attend(widths, x, tiles, beside=None):
                unit, head = n["unit"], n["unit"] - 4
                for s in range(len(widths) + 4):
                    if s < len(widths):
                        if widths[s] == CAUSAL_W:
                            causal_max(cst[:, C_CAUSAL:C_CAUSAL + CAUSAL_W], 0.125, 1.0)
                        else:
                            full_max(0.125)
                    if 1 <= s < len(widths) + 1:
                        probs(unit + s - 1, widths[s - 1])
                    if s >= 5 and s % 2:
                        out_lo(x, tiles[(s - 5) // 2], 1, head + s - 4)
                    if beside is not None:
                        beside()

            attend([512] * 4, 1, (6, 7), lambda: tap(10))
            tap(len(taps_left))
            dve.wait_ge(diag_used, TAP_GROUPS)
            for t in range(2):
                ins_ = dve.tensor_scalar(conv_out[:, 4 + t, :], linear_bank(c0 + 7)[:, t * TOK:t * TOK + TOK],
                                         cols[:, G_DWB + 4 + t:G_DWB + 5 + t], None, ALU.add)
            ins_.then_inc(conv_ready, 1)
            dve.wait_ge(conv_ready, 1)
            dve.wait_ge(cmu_ready, 1)
            for ct in range(CONV_TILES):
                ins_ = dve.tensor_tensor(conv_out[:, ct, :], conv_out[:, ct, :], prob[:, 0, 0:TOK], ALU.subtract)
            ins_.then_inc(cent_ready, 1)
            dve.wait_ge(csum_done, 2)
            dve.tensor_scalar(prob[:, 1, 0:TOK], ps[7][:, 0:TOK], 1.0 / 768, RMS_EPS, ALU.mult, ALU.add).then_inc(cms_ready, 1)
            dve.wait_ge(crt_ready, 1)
            link(dve.reciprocal(prob[:, 1, 0:TOK], prob[:, 0, 0:TOK]))
            for ct in range(CONV_TILES):
                ins_ = dve.tensor_tensor(conv_out[:, ct, :], conv_out[:, ct, :], prob[:, 1, 0:TOK], ALU.mult)
            ins_.then_inc(cn_ready, 1)
            dve.wait_ge(chi_ready, 1)
            dve.tensor_tensor(xlo[1][:, 0:CONV_TILES, :], conv_sq, xhi[1][:, 0:CONV_TILES, :].bitcast(F32),
                              ALU.subtract).then_inc(clo_ready, 1)
            for j in range(4):
                split_to(c0 + 10 + j + 1)
                add_to_h(c0 + 7 + j, j)
            n["last_h"] = c0 + 10
            h_updated()
            normed_rows(h)
            split_turned(0, G_FFN2)
            swiglu(1)
            normed_rows(h)
            split_turned(1, G_KV)
            c0 = ffn_starts[1] + 3 * PAIRS
            split_turned(0, G_FFN1 + 8)
            for i in range(3):
                split_to(c0 + i + 4)
                head_norm(c0 + i, kb_t[:, 2 * i:2 * i + 2, :], HG_K)
                if i >= 1:
                    rope(kb_t[:, 2 * i - 2:2 * i, :])
            for i in range(3):
                split_to(c0 + i + 7)
                if i == 1:
                    rope(kb_t[:, 4:6, :])
                copy_out(c0 + 3 + i, vb_a[:, :, i * CW:i * CW + CW])
            swiglu(2)
            normed_rows(h)
            split_turned(1, G_MIX2 + 8)
            c0 = ffn_starts[2] + 3 * PAIRS
            for i in range(3):
                split_to(c0 + i + 4)
                head_norm(c0 + i, qb_t[:, 2 * i:2 * i + 2, :], HG_Q)
                if i >= 1:
                    rope(qb_t[:, 2 * i - 2:2 * i, :])
            split_to(c0 + 7)
            rope(qb_t[:, 4:6, :])
            head_norm(c0 + 3, qm_t, HG_MQ + 1)
            attend([CAUSAL_W] * 12 + [512] * 4, 0, range(8))
            for j in range(4):
                split_to(c0 + 7 + j + 1)
                add_to_h(c0 + 4 + j, j)
            n["last_h"] = c0 + 7
            h_updated()
            normed_rows(h)
            split_turned(1, G_FFN2 + 8)
            swiglu(3)


_INS = ['x', 'mem', 'norm_mix', 'w_in', 'sgu_ln_g', 'sgu_ln_b', 'sgu_w', 'sgu_b', 'lambda_q1', 'lambda_k1', 'lambda_q2',
        'lambda_k2', 'diff_subln', 'w_out', 'norm_xq', 'norm_mem', 'w_q_mem', 'w_kv_mem', 'w_o_mem', 'norm_ffn',
        'w_router_group', 'b_router_group', 'w_router_expert', 'b_router_expert', 'w_gate', 'w_up', 'w_down',
        'norm_final', 'mem_2', 'positions_2', 'ffn1_norm_g_2', 'ffn1_w_gate_2', 'ffn1_w_up_2', 'ffn1_w_down_2',
        'mix_norm_g_2', 'mem_norm_g_2', 'w_mem_kv_2', 'mem_q_norm_g_2', 'mem_k_norm_g_2', 'w_o_2', 'ffn2_norm_g_2',
        'ffn2_w_gate_2', 'ffn2_w_up_2', 'ffn2_w_down_2', 'a_w_in_2', 'a_dw_kernel_2', 'a_dw_bias_2', 'a_ln_g_2',
        'a_ln_b_2', 'kv_norm_g_2', 'w_kv_2', 'k_norm_g_2', 'b_w_in_2', 'b_q_norm_g_2']
_OUT = ((1, TOK, D), 'float32')


def kernel(**inputs):
    import concourse.bacc as _bacc
    from concourse.bass_utils import run_bass_kernel_spmd as _run

    nc = _bacc.Bacc("TRN2", target_bir_lowering=False, num_devices=1)
    arrays, ins = {}, {}
    for name in _INS:
        a = np.ascontiguousarray(inputs[name])
        arrays[f"in_{name}_dram"] = a
        ins[name] = nc.dram_tensor(f"in_{name}_dram", a.shape, mybir.dt.from_np(a.dtype), kind="ExternalInput").ap()
    arrays["shape_constants"] = shape_constants()
    consts = nc.dram_tensor("shape_constants", (P, C_END), F32, kind="ExternalInput").ap()
    out = nc.dram_tensor("out_0_dram", _OUT[0], F32, kind="ExternalOutput").ap()
    build(nc, ins, consts, out)
    r = _run(nc, [arrays], core_ids=[0])
    return r.results[0]["out_0_dram"]
```

```python
from contextlib import ExitStack

import concourse.bass as bass
import numpy as np
from concourse import mybir

P = 128
F32 = mybir.dt.float32
F32R = mybir.dt.float32r
BF16 = mybir.dt.bfloat16
I32 = mybir.dt.int32
U32 = mybir.dt.uint32
ALU = mybir.AluOpType
ACT = mybir.ActivationFunctionType
AX = mybir.AxisListType.X

TOK = 256
TT = TOK // P
D = 1024
KT = D // P
CW = 256
RAW = 6
SPLIT = 3
CH = KT * CW
D_FF = 2816
PAIRS = D_FF // CW
FT = D_FF // P
EXPERTS, GROUPS, D_EXPERT = 32, 4, 512
SLOTS = 32
EG = 4
MAX_ROUNDS = TOK // SLOTS
RMS_EPS, LN_EPS = 1e-6, 1e-5
LAMBDA_INIT = 0.8 - 0.6
NEG = -1e30
MAGIC = 1.5 * 2.0 ** 23
TWO_PI = (6.28125, 0.0019340515136718750, 1.2556659146e-06)
CAUSAL_W = 384

C_ID, C_ONES, C_BLK, C_ROT, C_LT, C_TRIL, C_ND, C_CAUSAL, C_SLOT, C_GRP, C_THR, C_FREQ, C_END = (
    0, 128, 256, 384, 512, 640, 768, 1152, 1536, 1568, 1600, 1608, 1609)


def shape_constants():
    c = np.zeros((P, C_END), np.float32)
    row = np.arange(P)
    c[:, C_ID:C_ONES] = np.eye(P)
    c[:, C_ONES:C_BLK] = 1
    c[:, C_BLK:C_ROT] = row[:, None] // 64 == row[None, :] // 64
    for half in (0, 64):
        for d in range(8):
            c[half + d + 8, C_ROT + half + d] = -1
            c[half + d, C_ROT + half + d + 8] = 1
    c[:, C_LT:C_TRIL] = row[:, None] < row[None, :]
    c[:, C_TRIL:C_ND] = row[None, :] <= row[:, None]
    for base, q0, n in ((0, 0, 128), (128, 128, 256)):
        dist = q0 + row[:, None] - np.arange(n)[None, :]
        c[:, C_ND + base:C_ND + base + n] = np.where(dist >= 0, -dist, NEG)
        c[:, C_CAUSAL + base:C_CAUSAL + base + n] = np.where(dist >= 0, 0, NEG)
    c[:, C_SLOT:C_GRP] = np.arange(SLOTS)
    c[:, C_GRP:C_THR] = np.arange(EXPERTS) // (EXPERTS // GROUPS)
    c[:, C_THR:C_THR + 7] = SLOTS * np.arange(1, MAX_ROUNDS)
    c[:, C_THR + 7] = 1e9
    freq = (1.0 / (np.float32(500000.0) ** (np.arange(0, 16, 2, dtype=np.float32) / np.float32(16)))).astype(np.float32)
    for half in (0, 64):
        c[half:half + 16, C_FREQ] = np.tile(freq, 2)
    return c


G_MIX, G_XQ, G_MEM, G_FFN1, G_MIX2, G_MEM2, G_FFN2, G_KV, G_LNG, G_LNB, G_DWB, G_SGUB, G_A = (
    0, 8, 16, 24, 40, 56, 72, 88, 96, 102, 108, 114, 118)
CONV_TAPS, CONV_TILES = 31, 6
TAP_GROUPS = [(j, 4) for j in range(0, CONV_TAPS, 4)]
PE_TAPS = 12
TAP_GROUPS += [(j, 2) for j in range(0, PE_TAPS, 4)]
DW_ROWS = CONV_TAPS * CONV_TILES
G_DW, G_HEAD = 128, 128 + DW_ROWS
G_END = G_HEAD + 6
HG_MQ, HG_MK, HG_K, HG_Q = 0, 2, 4, 5


def weight_plan(w):
    plan = []

    def cols(name, layer, n, start=0):
        a = w[name][layer] if layer is not None else w[name]
        plan.extend((a, start + CW * i, "cols") for i in range(n))

    def ffn(gate, up, down, layer):
        for i in range(PAIRS):
            plan.extend([(w[gate][layer], CW * i, "cols"), (w[up][layer], CW * i, "cols"),
                         (w[down][layer], CW * i, "rows")])

    cols("w_in", 0, 10)
    cols("w_kv_mem", 0, 8)
    cols("w_out", 0, 4)
    cols("w_q_mem", 0, 4)
    cols("w_o_mem", 0, 4)
    cols("w_mem_kv_2", 0, 2)
    cols("w_mem_kv_2", 1, 2)
    starts = {"before_moe": len(plan)}
    starts["ffn0"] = len(plan)
    ffn("ffn1_w_gate_2", "ffn1_w_up_2", "ffn1_w_down_2", 0)
    for i in range(3):
        cols("a_w_in_2", 0, 1, CW * i)
        cols("a_w_in_2", 0, 1, CW * (3 + i))
    cols("a_w_in_2", 0, 1, CW * 6)
    cols("w_o_2", 0, 4)
    starts["ffn1"] = len(plan)
    ffn("ffn2_w_gate_2", "ffn2_w_up_2", "ffn2_w_down_2", 0)
    cols("w_kv_2", None, 6)
    starts["ffn2"] = len(plan)
    ffn("ffn1_w_gate_2", "ffn1_w_up_2", "ffn1_w_down_2", 1)
    cols("b_w_in_2", 0, 1, CW * 3)
    cols("b_w_in_2", 0, 3)
    cols("w_o_2", 1, 4)
    starts["ffn3"] = len(plan)
    ffn("ffn2_w_gate_2", "ffn2_w_up_2", "ffn2_w_down_2", 1)
    return plan, starts


def build(nc, ins, consts, out):
    plan, starts = weight_plan(ins)
    n_chunks = len(plan)
    moe_at = starts["before_moe"]
    mem2_at = moe_at - 4
    assert starts["ffn0"] == moe_at
    ffn_starts = [starts[f"ffn{i}"] for i in range(4)]
    in_ffn = {c for s in ffn_starts for c in range(s, s + 3 * PAIRS)}
    with ExitStack() as ctx:
        def sb(name, shape, dt=F32):
            return ctx.enter_context(nc.sbuf_tensor(name, shape, dt))

        def sem(name):
            return ctx.enter_context(nc.semaphore(name))

        ps = [ctx.enter_context(nc.psum_tensor(f"bank{i}", [P, 512], F32)) for i in range(8)]
        S_BANK, TR_BANK, O_BANK = (4, 5), 6, 7

        raw = sb("raw", [P, RAW, CH])
        with ExitStack() as parts:
            whi = parts.enter_context(nc.sbuf_tensor("whi", [P, SPLIT, CH], F32R))
            wlo = parts.enter_context(nc.sbuf_tensor("wlo", [P, SPLIT, CH], F32R))
        odd_expert = sb("odd_expert", [P, RAW, CH])
        xhi = [sb(f"x{i}hi", [P, KT, TOK], F32R) for i in range(2)]
        xlo = [sb(f"x{i}lo", [P, KT, TOK], F32R) for i in range(2)]
        h = sb("h", [P, TT, D])
        xn = sb("xn", [P, TT, D])
        arena = sb("arena", [P, 9728])
        hh_hi = sb("hh_hi", [P, 2, TOK], F32R)
        hh_lo = sb("hh_lo", [P, 2, TOK], F32R)
        prob = sb("prob", [P, 2, 512])
        prob_t = sb("prob_t", [P, 2, 512])
        cst = sb("cst", [P, C_END])
        cols = sb("cols", [P, G_END])
        small = sb("small", [P, 640])
        wr_hi, wr_lo = [t[:, :, :].rearrange("p a b -> p (a b)")[:, 0:KT * 36].rearrange("p (k n) -> p k n", k=KT)
                        for t in (hh_hi, hh_lo)]
        subln = sb("subln", [P, P])
        zeros = sb("zeros", [P, 512], BF16)
        picks = sb("picks", [P, 2, 2, 8], U32)
        extra_i = sb("extra_i", [P, 1], I32)

        ident = cst[:, C_ID:C_ID + P]
        ones = cst[:, C_ONES:C_ONES + P]
        blk64 = cst[:, C_BLK:C_BLK + P]
        rot = cst[:, C_ROT:C_ROT + P]
        before = cst[:, C_LT:C_LT + P]
        slot_row = cst[:, C_SLOT:C_SLOT + SLOTS]

        def area(at, *shape):
            n = int(np.prod(shape))
            v = arena[:, at:at + n]
            if len(shape) == 1:
                return v
            return v.rearrange("p (a b) -> p a b", a=shape[0])

        u_a, v_a, val_a = area(0, 2, 512), area(1024, 2, 512), area(2048, 2, 512)
        q_t, k_t = area(3072, 4, TOK), area(4096, 4, TOK)
        mem_a = area(5120, 2, D)
        k1_t, v1_a = area(5120, 8, TOK), area(7168, 2, D)
        ln_gb = area(7168, 2, 512)
        sgu_w, sgu_wt = area(8192, 4, P), area(8704, 4, P)
        q1_t = area(0, 8, TOK)
        gain_b = area(2048, D)
        sel, selw = area(4096, TT, EG * SLOTS), area(4352, TT, EG * P)
        xg, spread = area(5376, KT, EG * SLOTS), area(6400, EG, TOK)
        y_sb = area(7424, D)
        e_silu, e_h, e_ht = area(8448, P), area(8576, P), area(8704, P)
        wr_raw = area(8832, KT, 36)
        mem2_a = area(0, 2, D)
        f_silu, f_prod = area(2048, 2, TOK), area(2560, 2, TOK)
        k2_t = [area(at_, 2, TOK) for at_ in (3072, 0)]
        v2_a = [area(at_, 2, CW) for at_ in (3584, 512)]
        kb_t, vb_a = area(6144, 6, TOK), area(7680, 2, 768)
        cos_t, sin_t = area(9216, TOK), area(9472, TOK)
        PADW = CONV_TAPS - 1 + TOK
        conv_in, conv_out = area(4096, 6, PADW), area(1024, 6, TOK)
        sig = area(2560, 2, TOK)
        diag = area(6144, 16, P)
        conv_sq = xn[:, :, :].rearrange("p t d -> p (t d)")[:, 0:CONV_TILES * TOK].rearrange("p (a b) -> p a b", a=CONV_TILES)
        qm_t = [area(8192, 2, TOK), area(5632, 2, TOK)]
        qb_t = area(4096, 6, TOK)

        at = [0]

        def take(n):
            at[0] += n
            return small[:, at[0] - n:at[0]]

        sumsq, meansq, root, rstd = take(2), take(2), take(2), take(2)
        nmax, psum_e, rsum = take(8), take(8), take(8)
        oss, oms, ort, ors = take(8), take(8), take(8), take(8)
        bn6, bn2 = take(48), take(16)
        lams, lame, neglam = take(2), take(2), take(1)
        logit, glog, gmax = take(72), take(16), take(16)
        gneg, gsum, ggate, gidx = take(2), take(2), take(2), take(2)
        emask = take(64)
        emax = take(16)
        ediff, eexp, eden, w1, w2 = take(2), take(2), take(2), take(2), take(2)
        eidx = take(4)
        rb = take(36)
        warmth = take(32)
        tmax, thr, extra_f = take(1), take(8), take(1)
        posm, wgt = sb("posm", [P, TT, EXPERTS + EG]), sb("wgt", [P, TT, EXPERTS + EG])
        hot = sb("hot", [P, TT, EXPERTS])
        hot2 = sb("hot2", [P, TT, EXPERTS])
        lamv = prob[:, 0, 0:256].rearrange("p (a b) -> p a b", a=4)
        posi = prob_t[:, 0, 0:TOK].bitcast(I32)
        rows_a = prob[:, 1, 0:P]
        rows_b = prob[:, 1, P:2 * P]
        rows_c = prob[:, 1, 2 * P:3 * P]

        in_x = [sem(f"in_x{tt}") for tt in range(TT)]
        in_c, in_rows, in_bc, in_mem, in_mem2, in_late, in_sgu = [sem(n) for n in (
            "in_consts", "in_rows", "in_broadcast", "in_mem", "in_mem2", "in_late", "in_sgu")]
        raw_in = [sem(f"raw_in{i}") for i in range(RAW)]
        hi_ready, lo_ready = sem("hi_ready"), sem("lo_ready")
        chunk_used = sem("chunk_used")
        evac_a, evac_v = sem("evac_a"), sem("evac_v")
        ss_ready, ms_ready, rt_ready, xn_ready = [sem(n) for n in ("ss_ready", "ms_ready", "rt_ready", "xn_ready")]
        tr_done, xhi_ready, xlo_ready = sem("tr_done"), sem("xhi_ready"), sem("xlo_ready")
        s_full, nm_ready, e_ready, p_ready, t_done, pt_ready, o_done, o_hi, o_evac = [sem(n) for n in (
            "s_full", "nm_ready", "e_ready", "p_ready", "t_done", "pt_ready", "o_done", "o_hi", "o_evac")]
        sq_ready, hs_done, hms_ready, hrt_ready, hn_ready, rot_done = [sem(n) for n in (
            "sq_ready", "hs_done", "hms_ready", "hrt_ready", "hn_ready", "rot_done")]
        v_link = sem("v_link")
        cols_t, cols_ready, zero_ready = sem("cols_t"), sem("cols_ready"), sem("zero_ready")
        bn_ready, bn_root, wt_done, wt_ready, vn_ready, sp_done, sgu_done = [sem(n) for n in (
            "bn_ready", "bn_root", "wt_done", "wt_ready", "vn_ready", "sp_done", "sgu_done")]
        lam_ready, lam_exp, o_ss, o_ms, o_rt, mixed_ready = [sem(n) for n in (
            "lam_ready", "lam_exp", "o_ss", "o_ms", "o_rt", "mixed_ready")]
        h_ready = sem("h_ready")
        ffn_half, h_tile = sem("ffn_half"), sem("h_tile")
        gu0_done, silu_ready, prod_ready, hhi_ready, hlo_ready = [sem(n) for n in (
            "gu0_done", "silu_ready", "prod_ready", "hhi_ready", "hlo_ready")]
        sig_ready, conv_ready, csum_done, cmu_ready, cent_ready, csq_ready, cms_ready, crt_ready, cn_ready, \
            csilu_ready, chi_ready, clo_ready = [sem(n) for n in (
                "sig_ready", "conv_ready", "csum_done", "cmu_ready", "cent_ready", "csq_ready", "cms_ready",
                "crt_ready", "cn_ready", "csilu_ready", "chi_ready", "clo_ready")]
        rope_done = sem("rope_done")
        diag_ready, diag_used, tap_done = [sem(n) for n in (
            "diag_ready", "diag_used", "tap_done")]
        wt_copied, o_copied, wr_split, h_added, glu_done = [sem(n) for n in (
            "wt_copied", "o_copied", "wr_split", "h_added", "glu_done")]
        rope_half, rope_sin = sem("rope_half"), sem("rope_sin")
        wr_ready, r_done, r_bias, r_exp, r_ediff, r_eexp, hot_ready, pos_done, extra_ready = [sem(n) for n in (
            "wr_ready", "r_done", "r_bias", "r_exp", "r_ediff", "r_eexp", "hot_ready", "pos_done",
            "extra_ready")]
        moe_done, out_done = sem("moe_done"), sem("out_done")

        def expert_sems(tag):
            return {n: sem(f"{tag}_{n}") for n in (
                "sel", "selw", "fill", "evac", "raw_used", "gu", "silu", "hm", "ht_full", "ht", "y_full", "y0", "y1",
                "spread")}

        main, over = expert_sems("moe"), expert_sems("over")
        in_taps = sem("in_taps")
        over_in, in_final = sem("over_in"), sem("in_final")
        alt_in = [sem(f"alt_in{i}") for i in range(RAW)]

        linear = [c for c in range(n_chunks) if c not in in_ffn]
        kv_at = starts["ffn1"] + 3 * PAIRS
        act_evac = set(range(0, 4)) | set(range(22, 26)) | set(range(kv_at + 3, kv_at + 6))
        evac_count, seen = {}, {"a": 0, "v": 0}
        for c in linear:
            e = "a" if c in act_evac else "v"
            seen[e] += 1
            evac_count[c] = (e, seen[e])

        def linear_bank(c):
            return ps[linear.index(c) % 4]

        def chunk_source(c):
            a, col, kind = plan[c]
            if kind == "cols":
                return a.rearrange("(k p) n -> p k n", p=P)[:, :, col:col + CW]
            return a.rearrange("(k p) n -> p k n", p=P)[:, col // P:col // P + 2, :]

        def chunk_slot(c, kind):
            return raw[:, c % RAW, :].rearrange("p (k n) -> p k n", k=KT if kind == "cols" else 2)

        def expert_slot(parity, slot):
            if parity == 0:
                return raw[:, slot, :]
            return odd_expert[:, slot, :]

        def expert_landed(slot):
            return 16 * (len(range(slot, moe_at, RAW)) + 1)

        def landed(c):
            return 16 * (c // RAW + 1 + (EXPERTS // 2 if c >= moe_at else 0))

        def prob_slot(u):
            if u >= 8 and u % 4 < 2:
                return xn[:, 0, 512 * (u % 4):512 * (u % 4) + 512]
            return prob[:, u % 2, :]

        def stat_cols(u, tt=None):
            s = 2 * (u % 2 if u < 8 else u % 4)
            return slice(s, s + 2) if tt is None else slice(s + tt, s + tt + 1)

        def slot_free(u):
            return u // 2 if u < 8 else max(4, u - 7)

        SPARE = {}
        for phase, c in ((0, starts["ffn0"] + 3 * PAIRS + 8), (1, starts["ffn2"] + 3 * PAIRS + 5)):
            SPARE[phase] = [linear.index(c + i) % 4 for i in range(2)]

        WIDE_TURNS = (2, 3, 7, 8, 9, 10, 12, 13)

        def fill_bank(fill):
            return ps[4 + fill % 4 if fill // 4 in WIDE_TURNS else 6 + fill % 2]

        def turned_bank(head):
            return ps[TR_BANK if head < 8 or head % 2 == 0 else SPARE[int(head >= 12)][0]]

        def out_bank(head):
            return ps[O_BANK if head < 8 or head // 2 % 2 == 0 else SPARE[int(head >= 12)][1]]

        block = ctx.enter_context(nc.Block())

        @block.sync
        def _(sp):
            for tt in range(TT):
                sp.dma_start(h[:, tt, :], ins["x"][0][tt * P:tt * P + P, :]).then_inc(in_x[tt], 16)
            sp.dma_start(cst[:, :], consts).then_inc(in_c, 16)

            def load_chunk(c):
                if c >= RAW and not moe_at <= c < moe_at + RAW:
                    sp.wait_ge(lo_ready, c - RAW + 1)
                sp.dma_start(chunk_slot(c, plan[c][2]), chunk_source(c)).then_inc(raw_in[c % RAW], 16)

            load_chunk(0)
            sp.wait_ge(in_rows, 16 * 12)
            sp.wait_ge(in_taps, 16 * 10)
            for c in range(1, moe_at):
                load_chunk(c)

            def load_expert(x, parity, slot, sem_):
                if slot < 4:
                    a = ins["w_gate" if slot < 2 else "w_up"][0].rearrange("e (k p) n -> p e k n", p=P)
                    src = a[:, bass.ds(x, 1), 4 * (slot % 2):4 * (slot % 2) + 4, :]
                    dst = expert_slot(parity, slot).rearrange("p (o k n) -> p o k n", o=1, k=4)
                else:
                    a = ins["w_down"][0].rearrange("e (k p) n -> p e k n", p=P)
                    src = a[:, bass.ds(x, 1), 2 * (slot - 4):2 * (slot - 4) + 2, :]
                    dst = expert_slot(parity, slot).rearrange("p (o k n) -> p o k n", o=1, k=2)
                sp.dma_start(dst, src).then_inc(sem_, 16)

            def load_experts(y, parity):
                for slot in range(3):
                    sp.wait_ge(main["raw_used"], 6 * y + (3 * parity - 5 + slot))
                    load_expert(2 * y + parity, parity, slot, (raw_in, alt_in)[parity][slot])
                sp.wait_ge(main["gu"], 2 * y + (parity - 1))
                load_expert(2 * y + parity, parity, 3, (raw_in, alt_in)[parity][3])
                sp.wait_ge(main["y_full"], 4 * y + (2 * parity - 2))
                for slot in (4, 5):
                    load_expert(2 * y + parity, parity, slot, (raw_in, alt_in)[parity][slot])

            for slot in range(RAW):
                sp.wait_ge(lo_ready, max(range(slot, moe_at, RAW)) + 1)
                load_expert(0, 0, slot, raw_in[slot])
            for slot in range(2 * SPLIT):
                sp.wait_ge(chunk_used, max(range(slot % SPLIT, moe_at, SPLIT)) + 1)
                load_expert(1, 1, slot, alt_in[slot])
            with sp.Fori(1, EXPERTS // 2) as y:
                load_experts(y, 0)
                load_experts(y, 1)
            sp.wait_ge(main["y_full"], 2 * EXPERTS - 2)
            for c in range(moe_at, moe_at + RAW):
                load_chunk(c)
            sp.wait_ge(main["y_full"], 2 * EXPERTS)
            sp.wait_ge(extra_ready, 1)
            extra = sp.value_load(extra_i[0:1, 0:1], min_val=0, max_val=MAX_ROUNDS - 1)
            with sp.If(extra > 0):
                with sp.Fori(0, extra) as r:
                    with sp.Fori(0, EXPERTS) as x:
                        sp.wait_ge(over["spread"], EXPERTS * r + x + 1)
                        for slot in range(RAW):
                            load_expert(x, 1, slot, over_in)
            c = moe_at + RAW
            while c < n_chunks:
                if c - RAW in ffn_starts:
                    s = c - RAW
                    gate, up, down = (plan[s + j][0] for j in range(3))
                    with sp.Fori(1, PAIRS // 2) as i:
                        for j in range(RAW):
                            sp.wait_ge(lo_ready, s + 6 * i + (j - RAW + 1))
                            half = j // 3
                            if j % 3 < 2:
                                src = (gate, up)[j % 3].rearrange("(k p) n -> p k n", p=P)[:, :, bass.ds(2 * CW * i + CW * half, CW)]
                            else:
                                src = down.rearrange("(k p) n -> p k n", p=P)[:, bass.ds(4 * i + 2 * half, 2), :]
                            sp.dma_start(chunk_slot(s + j, "cols" if j % 3 < 2 else "rows"), src).then_inc(raw_in[(s + j) % RAW], 16)
                    c = s + 6 * (PAIRS // 2)
                load_chunk(c)
                c += 1
            sp.wait_ge(h_ready, 9)
            sp.dma_start(out[0].rearrange("(t p) d -> p t d", p=P), h[:, :, :]).then_inc(out_done, 16)
            sp.wait_ge(out_done, 16)

        @block.gpsimd
        def _(pool):
            taps = ins["a_dw_kernel_2"][0].rearrange("j o (k p) -> (j o k) p", p=P)
            pool.dma_start(rows_b, taps[0:P]).then_inc(in_taps, 16)
            pool.dma_start(rows_c[0:DW_ROWS - P, :], taps[P:DW_ROWS]).then_inc(in_taps, 16)
            for half in (0, 64):
                for r, (name, layers) in ((HG_MQ, ("mem_q_norm_g_2", 2)), (HG_MK, ("mem_k_norm_g_2", 2)),
                                          (HG_K, ("k_norm_g_2", 1)), (HG_Q, ("b_q_norm_g_2", 1))):
                    src = ins[name] if name != "k_norm_g_2" else ins[name].rearrange("(o p) -> o p", o=1)
                    r0 = DW_ROWS - P + r
                    pool.dma_start(rows_c[r0:r0 + layers, half:half + 64], src).then_inc(in_taps, 16)
            pool.wait_ge(in_taps, 16 * 10)
            pool.wait_ge(in_rows, 16 * 12)
            pool.dma_start(mem_a, ins["mem"][0].rearrange("(t p) d -> p t d", p=P)).then_inc(in_mem, 16)
            pool.dma_start(sgu_w, ins["sgu_w"][0].rearrange("g t s -> t g s")).then_inc(in_sgu, 16)
            pool.dma_start(ln_gb[:, 0, :], ins["sgu_ln_g"][0].rearrange("g c -> (g c)").partition_broadcast(P)).then_inc(in_sgu, 16)
            pool.dma_start(ln_gb[:, 1, :], ins["sgu_ln_b"][0].rearrange("g c -> (g c)").partition_broadcast(P)).then_inc(in_sgu, 16)
            for i, name in enumerate(("lambda_q1", "lambda_k1", "lambda_q2", "lambda_k2")):
                pool.dma_start(lamv[:, i, :], ins[name][0].partition_broadcast(P)).then_inc(in_bc, 16)
            pool.dma_start(subln[:, :], ins["diff_subln"][0].partition_broadcast(P)).then_inc(in_bc, 16)
            pool.dma_start(rb[:, 0:4], ins["b_router_group"][0].partition_broadcast(P)).then_inc(in_bc, 16)
            pool.dma_start(rb[:, 4:36], ins["b_router_expert"][0].partition_broadcast(P)).then_inc(in_bc, 16)
            pool.dma_start(posi, ins["positions_2"][0].partition_broadcast(P)).then_inc(in_bc, 16)
            pool.wait_ge(h_ready, 1)
            pool.dma_start(gain_b, ins["norm_ffn"][0].partition_broadcast(P)).then_inc(in_late, 16)
            pool.wait_ge(s_full, 12)
            pool.dma_start(mem2_a, ins["mem_2"][0].rearrange("(t p) d -> p t d", p=P)).then_inc(in_mem2, 16)
            pool.wait_ge(o_done, 8)
            pool.dma_start(wr_raw[:, :, 0:4], ins["w_router_group"][0].rearrange("(k p) n -> p k n", p=P)).then_inc(in_late, 16)
            pool.dma_start(wr_raw[:, :, 4:36], ins["w_router_expert"][0].rearrange("(k p) n -> p k n", p=P)).then_inc(in_late, 16)
            pool.wait_ge(xn_ready, 10)
            pool.dma_start(gain_b, ins["norm_final"].partition_broadcast(P)).then_inc(in_final, 16)
            pool.wait_ge(h_ready, 3)
            for g, (j0, tile) in enumerate(TAP_GROUPS):
                if g >= 2:
                    pool.wait_ge(diag_used, g - 1)
                taps_n = min(4, CONV_TAPS - j0)
                for t in range(2):
                    first = G_DW + 6 * j0 + tile + t
                    dst = diag[:, 8 * (g % 2):8 * (g % 2) + 8, :].rearrange("p (j t) c -> p j t c", t=2)[:, 0:taps_n, t, :]
                    ins_ = pool.tensor_tensor(dst, ident.unsqueeze(1).broadcast_to([P, taps_n, P]),
                                              cols[:, first:first + 6 * (taps_n - 1) + 1:6].unsqueeze(2).broadcast_to([P, taps_n, P]),
                                              ALU.mult)
                ins_.then_inc(diag_ready, 1)

        @block.tensor
        def _(pe):
            n = {"turn": 0, "unit": 0, "head": 0, "out": 0, "hs": 0, "rot": 0}

            def split_product(dst, a_hi, a_lo, b_hi, b_lo, first, last):
                pe.matmul(dst, a_hi, b_hi, start=first, stop=False, skip_group_check=True)
                pe.matmul(dst, a_lo, b_hi, start=False, stop=False, skip_group_check=True)
                return pe.matmul(dst, a_hi, b_lo, start=False, stop=last, skip_group_check=True)

            def turn(src, gained=True):
                sem_, rows_written = gained
                first = n["turn"]

                def tiles(kp, tt):
                    for k in (2 * kp, 2 * kp + 1):
                        at_ = (k % 2) * TOK + tt * P
                        mm = pe.transpose(fill_bank(first + kp)[:, at_:at_ + P], src[:, tt, k * P:k * P + P], ident)
                    return mm

                if rows_written > 1:
                    pe.wait_ge(sem_, rows_written - 1)
                else:
                    pe.wait_ge(sem_, rows_written)
                ahead = 4 if first // 4 in WIDE_TURNS else 2
                if first:
                    pe.wait_ge(xlo_ready, first)
                for kp in range(ahead):
                    tiles(kp, 0)
                pe.wait_ge(sem_, rows_written)
                for kp in range(ahead):
                    tiles(kp, 1).then_inc(tr_done, 1)
                for kp in range(ahead, KT // 2):
                    pe.wait_ge(xlo_ready, first + kp - 1)
                    tiles(kp, 0)
                    tiles(kp, 1).then_inc(tr_done, 1)
                n["turn"] += KT // 2

            def x_part(k, fresh):
                if fresh and k % 2 == 0:
                    pe.wait_ge(xlo_ready, n["turn"] - KT // 2 + k // 2 + 1)

            def linear_rows(c, x, fresh=False, tiles_ready=None):
                bank, s = linear_bank(c), c % SPLIT
                start_linear(c)
                hi = whi[:, s, :].rearrange("p (k n) -> p k n", k=KT)
                lo = wlo[:, s, :].rearrange("p (k n) -> p k n", k=KT)
                for tt in range(TT):
                    for k in range(KT):
                        x_part(k, fresh and tt == 0)
                        if tiles_ready is not None and tt == 0 and k < CONV_TILES:
                            pe.wait_ge(tiles_ready, k + 1)
                        mm = split_product(bank[:, tt * CW:tt * CW + CW], xhi[x][:, k, tt * P:tt * P + P],
                                           xlo[x][:, k, tt * P:tt * P + P], hi[:, k, :], lo[:, k, :], k == 0, k == KT - 1)
                mm.then_inc(chunk_used, 1)

            def linear_cols(c, x, fresh=False):
                bank, s = linear_bank(c), c % SPLIT
                start_linear(c)
                hi = whi[:, s, :].rearrange("p (k n) -> p k n", k=KT)
                lo = wlo[:, s, :].rearrange("p (k n) -> p k n", k=KT)
                for j in range(2):
                    for k in range(KT):
                        x_part(k, fresh and j == 0)
                        mm = split_product(bank[:, j * TOK:j * TOK + TOK], hi[:, k, j * P:j * P + P],
                                           lo[:, k, j * P:j * P + P], xhi[x][:, k, :], xlo[x][:, k, :], k == 0, k == KT - 1)
                mm.then_inc(chunk_used, 1)

            def start_linear(c):
                pe.wait_ge(lo_ready, c + 1)
                at = linear.index(c)
                if at >= 4:
                    e, count = evac_count[linear[at - 4]]
                    pe.wait_ge(evac_a if e == "a" else evac_v, count)

            def x_ready():
                pe.wait_ge(xlo_ready, n["turn"])

            def scores(parts):
                u = n["unit"]
                if u >= 2:
                    pe.wait_ge(e_ready, u - 1)
                for cols_, pairs in parts:
                    for i, (q, k) in enumerate(pairs):
                        mm = pe.matmul(ps[4 + u % 2][:, cols_], q, k, start=i == 0, stop=i == len(pairs) - 1,
                                       skip_group_check=True)
                mm.then_inc(s_full, 1)
                n["unit"] += 1

            def causal_scores(q, k):
                scores([(slice(0, 128), [(q[:, 0:P], k[:, 0:P])]), (slice(128, 384), [(q[:, P:TOK], k[:, 0:TOK])])])

            def turn_probs(p, blocks):
                hd = n["head"]
                pe.wait_ge(p_ready, hd + 1)
                if hd >= 1:
                    pe.wait_ge(pt_ready, hd if hd <= 8 else hd - 1)
                for i, src in enumerate(blocks):
                    mm = pe.transpose(turned_bank(hd)[:, i * P:i * P + P], p[:, src:src + P], ident)
                mm.then_inc(t_done, 1)
                n["head"] += 1

            def values(parts, hd, first=True):
                pe.wait_ge(pt_ready, hd + 1)
                if first and n["out"] >= 1:
                    pe.wait_ge(o_evac, n["out"] if hd <= 8 else n["out"] - 1)
                for rows_, cols_, pairs, st, sp_ in parts:
                    for i, (a, b) in enumerate(pairs):
                        mm = pe.matmul(out_bank(hd)[rows_, cols_], a, b, start=st and i == 0,
                                       stop=sp_ and i == len(pairs) - 1, skip_group_check=True)
                mm.then_inc(o_done, 1)

            def head_sums():
                pe.wait_ge(sq_ready, n["hs"] + 1)
                if n["hs"] >= 1:
                    pe.wait_ge(hms_ready, n["hs"])
                pe.matmul(ps[7][:, :], blk64, prob[:, 0, :], start=True, stop=True).then_inc(hs_done, 1)
                n["hs"] += 1

            FULL_BLOCKS = (0, 256, 128, 384)
            CAUSAL_BLOCKS = (0, 128, 256)

            pe.wait_ge(in_c, 16)
            pe.wait_ge(in_rows, 16 * 12)
            pe.wait_ge(in_taps, 16 * 10)
            pe.transpose(ps[5][:, 0:G_A], rows_a[0:G_A, :], ident[0:G_A, 0:G_A])
            pe.transpose(ps[5][:, 128:256], rows_b, ident)
            m = DW_ROWS - P + 6
            pe.transpose(ps[5][:, 256:256 + m], rows_c[0:m, :], ident[0:m, 0:m]).then_inc(cols_t, 1)

            turn(xn, (xn_ready, 2))
            for c in range(4):
                linear_rows(c, 0, c == 0)
            for c in range(4, 8):
                linear_cols(c, 0)
            turn(xn, (xn_ready, 4))
            for c in range(8, 10):
                linear_rows(c, 0)
            pe.wait_ge(wt_done, 1)
            for g in range(4):
                mm = pe.transpose(ps[4][:, g * P:g * P + P], sgu_w[:, g, :], ident)
            mm.then_inc(wt_ready, 1)
            x_ready()
            linear_cols(10, 1)
            pe.wait_ge(vn_ready, 1)
            pe.wait_ge(wt_copied, 1)
            for tt in range(TT):
                for g in range(4):
                    mm = pe.matmul(ps[4 + tt][:, g * P:g * P + P], sgu_wt[:, g, :], v_a[:, tt, g * P:g * P + P],
                                   start=True, stop=True)
                mm.then_inc(sp_done, 1)
            pe.wait_ge(sgu_done, 1)

            for hd in range(4):
                for i in range(2):
                    half = slice(64 * i, 64 * i + 64)
                    pe.wait_ge(evac_v, evac_count[7][1])
                    causal_scores(q_t[half, hd, :], k_t[half, hd, :])
                for c in range(11 + 2 * hd, min(13 + 2 * hd, 18)):
                    (linear_cols if c < 14 else linear_rows)(c, 1)
                turn_probs(prob[:, 0, :], CAUSAL_BLOCKS)
                pt = prob_t[:, hd % 2, :]
                v = val_a[:, :, hd * P:hd * P + P]
                values([(slice(0, P), slice(0, P), [(pt[:, 0:P], v[:, 0, :])], True, True),
                        (slice(0, P), slice(P, 2 * P), [(pt[:, P:2 * P], v[:, 0, :]), (pt[:, 2 * P:3 * P], v[:, 1, :])],
                         True, True)], hd)
                n["out"] += 1
            turn(xn, (mixed_ready, 1))
            for c in range(18, 22):
                linear_rows(c, 0, c == 18)

            def full_scores(head):
                parts = [(slice(tt * TOK, tt * TOK + TOK),
                          [(q1_t[:, 2 * head + j, tt * P:tt * P + P], k1_t[:, 2 * head + j, :]) for j in range(2)])
                         for tt in range(TT)]
                pe.wait_ge(evac_a, evac_count[22 + head][1])
                scores(parts)

            def full_out(head):
                turn_probs(prob_slot(8 + head), FULL_BLOCKS)
                pt = prob_t[:, (n["head"] - 1) % 2, :].rearrange("p (m q) -> p m q", m=2)
                values([(slice(0, P), slice(j * TOK, j * TOK + TOK),
                         [(v1_a[:, mt, head * 256 + j * P:head * 256 + j * P + P], pt[:, mt, :]) for mt in range(2)],
                         True, True) for j in range(2)], n["head"] - 1)
                n["out"] += 1

            turn(xn, (xn_ready, 6))
            pe.wait_ge(evac_v, evac_count[17][1])
            linear_cols(22, 1, True)
            linear_cols(23, 1)
            full_scores(0)
            linear_cols(24, 1)
            full_scores(1)
            linear_cols(25, 1)
            full_scores(2)
            full_out(0)
            full_scores(3)
            full_out(1)
            full_out(2)
            full_out(3)
            pe.wait_ge(o_evac, n["out"])
            linear_rows(26, 0)
            linear_rows(27, 0)
            turn(mem2_a, (xn_ready, 8))
            linear_rows(28, 0)
            linear_rows(29, 0)
            x_ready()
            linear_cols(mem2_at, 1)
            turn(xn, (xn_ready, 10))
            x_ready()
            pe.wait_ge(wr_ready, 1)
            for tt in range(TT):
                for k in range(KT):
                    mm = split_product(ps[4][:, tt * 36:tt * 36 + 36], xhi[0][:, k, tt * P:tt * P + P],
                                       xlo[0][:, k, tt * P:tt * P + P], wr_hi[:, k, :], wr_lo[:, k, :], k == 0, k == KT - 1)
            mm.then_inc(r_done, 1)
            linear_rows(mem2_at + 1, 1)
            turn(mem2_a, (xn_ready, 8))
            linear_cols(mem2_at + 2, 1, True)
            pe.wait_ge(hot_ready, 1)
            for at_, pairs in ((0, [(before, 0)]), (32, [(ones, 0), (before, 1)]), (64, [(ones, 0), (ones, 1)])):
                for i, (lhs, tt) in enumerate(pairs):
                    mm = pe.matmul(ps[5][:, at_:at_ + 32], lhs, hot[:, tt, :], start=i == 0, stop=i == len(pairs) - 1,
                                   skip_group_check=True)
            mm.then_inc(pos_done, 1)
            x_ready()
            head_sums()
            linear_rows(mem2_at + 3, 1)
            head_sums()

            def gather(half, s, width, dst, src):
                for k in range(4 * half, 4 * half + 4):
                    for tt in range(TT):
                        mm = pe.matmul(dst[:, (k % 4) * width:(k % 4) * width + width], xn[:, tt, k * P:k * P + P],
                                       src[:, tt, 0:width], start=tt == 0, stop=tt == TT - 1, skip_group_check=True)
                return mm

            def gate_up(x_of, parity, arrived, s):
                for which in range(2):
                    for k in range(KT):
                        slot = 2 * which + k // 4
                        if k % 4 == 0:
                            arrived(slot)
                        w_k = expert_slot(parity, slot).rearrange("p (k n) -> p k n", k=4)
                        for j in range(4):
                            mm = pe.matmul(ps[4][32 * j:32 * j + 32, which * P:which * P + P], x_of(k),
                                           w_k[:, k % 4, j * P:j * P + P], start=k == 0, stop=k == KT - 1,
                                           skip_group_check=True)
                        if k == 3 or (k == 7 and which == 0):
                            mm.then_inc(s["raw_used"], 1)
                mm.then_inc(s["gu"], 1)

            def turn_hidden(s, count):
                pe.wait_ge(s["hm"], count)
                pe.transpose(ps[4][:, 256:384], e_h, ident).then_inc(s["ht_full"], 1)

            def down(parity, arrived, s, count):
                pe.wait_ge(s["ht"], count)
                arrived(4)
                arrived(5)
                for half in range(2):
                    for j in range(4):
                        w_j = expert_slot(parity, 4 + j // 2).rearrange("p (k n) -> p k n", k=2)
                        mm = pe.matmul(ps[6 + half][32 * j:32 * j + 32, :], e_ht[:, 32 * j:32 * j + 32],
                                       w_j[:, j % 2, half * 512:half * 512 + 512], start=True, stop=True,
                                       skip_group_check=True)
                    mm.then_inc(s["y_full"], 1)

            def spread_out(e, s, count):
                pe.wait_ge(s["y0"], count)
                pe.wait_ge(s["y1"], count)
                for tt in range(TT):
                    for half in range(2):
                        mm = pe.matmul(ps[2 * tt + half][:, :], spread[:, e, tt * P:tt * P + P],
                                       y_sb[:, half * 512:half * 512 + 512], start=False, stop=False,
                                       skip_group_check=True)
                mm.then_inc(s["spread"], 1)

            def gather_half(half, count):
                pe.wait_ge(main["evac"], count)
                gather(half, main, EG * SLOTS, ps[5], sel).then_inc(main["fill"], 1)

            def turn_spread(half, count):
                pe.wait_ge(main["evac"], count)
                for i in range(2):
                    for tt in range(TT):
                        mm = pe.transpose(ps[5][:, i * TOK + tt * P:i * TOK + tt * P + P],
                                          selw[:, tt, (2 * half + i) * P:(2 * half + i) * P + P], ident)
                mm.then_inc(main["fill"], 1)

            pe.wait_ge(main["sel"], 1)
            gather(0, main, EG * SLOTS, ps[5], sel).then_inc(main["fill"], 1)
            gather_half(1, 1)
            pe.wait_ge(zero_ready, 1)
            pe.wait_ge(evac_v, evac_count[moe_at - 1][1])
            for b in range(4):
                pe.matmul(ps[b][:, :], zeros[:, 0:P], zeros[:, :], start=True, stop=False, skip_group_check=True)
            with pe.Fori(0, EXPERTS // EG) as g:
                for e in range(EG):
                    def arrived(slot):
                        if e % 2 == 0:
                            pe.wait_ge(raw_in[slot], 32 * g + (expert_landed(slot) + 8 * e))
                        else:
                            pe.wait_ge(alt_in[slot], 32 * g + (16 + 8 * (e - 1)))

                    if e == 0:
                        pe.wait_ge(main["evac"], 4 * g + 2)
                    gate_up(lambda k: xg[:, k, e * SLOTS:e * SLOTS + SLOTS], e % 2, arrived, main)
                    if e == 0:
                        pe.wait_ge(main["selw"], g + 1)
                        turn_spread(0, 4 * g + 2)
                    else:
                        spread_out(e - 1, main, 4 * g + e)
                    turn_hidden(main, 4 * g + e + 1)
                    if e == 0:
                        turn_spread(1, 4 * g + 3)
                        pe.wait_ge(main["evac"], 4 * g + 4)
                    down(e % 2, arrived, main, 4 * g + e + 1)
                pe.wait_ge(main["sel"], g + 2)
                gather_half(0, 4 * g + 4)
                spread_out(EG - 1, main, 4 * g + 4)
                gather_half(1, 4 * g + 5)
            pe.wait_ge(extra_ready, 1)
            extra = pe.value_load(extra_i[0:1, 0:1], min_val=0, max_val=MAX_ROUNDS - 1)
            with pe.If(extra > 0):
                pe.wait_ge(main["evac"], EXPERTS + 2)
                pe.matmul(ps[0][:, :], zeros[:, 0:P], zeros[:, :], start=False, stop=False,
                          skip_group_check=True).then_inc(over["spread"], 1)
                with pe.Fori(0, extra) as r:
                    with pe.Fori(0, EXPERTS) as x:
                        step = EXPERTS * r + x + 1
                        pe.wait_ge(over["selw"], step)
                        for half in range(2):
                            for k in range(4 * half, 4 * half + 4):
                                for tt in range(TT):
                                    pe.matmul(ps[5][:, k * SLOTS:k * SLOTS + SLOTS], xn[:, tt, k * P:k * P + P],
                                              sel[:, tt, 0:SLOTS], start=tt == 0, stop=tt == TT - 1, skip_group_check=True)
                        for tt in range(TT):
                            mm = pe.transpose(ps[5][:, 256 + tt * P:256 + tt * P + P], selw[:, tt, 0:P], ident)
                        mm.then_inc(over["fill"], 1)
                        pe.wait_ge(over["evac"], step)
                        pe.wait_ge(over_in, 16 * RAW * step)
                        gate_up(lambda k: xg[:, k, 0:SLOTS], 1, lambda slot: None, over)
                        turn_hidden(over, step)
                        down(1, lambda slot: None, over, step)
                        spread_out(0, over, step)
            for b in range(4):
                mm = pe.matmul(ps[b][:, :], zeros[:, 0:P], zeros[:, :], start=False, stop=True, skip_group_check=True)
            mm.then_inc(moe_done, 1)

            def rotate(heads, norms):
                pe.wait_ge(hn_ready, norms)
                if n["rot"] >= 1:
                    pe.wait_ge(rope_done, n["rot"])
                pe.matmul(ps[6][:, :], rot, heads, start=True, stop=True).then_inc(rot_done, 1)
                n["rot"] += 1

            def memory_head(layer, head):
                half = slice(64 * (head % 2), 64 * (head % 2) + 64)

                def out(hd, pt):
                    pt = pt.rearrange("p (m q) -> p m q", m=2)
                    values([(half, slice(0, TOK), [(v2_a[layer][:, mt, head * 64:head * 64 + 64], pt[:, mt, :])
                                                   for mt in range(2)], True, True)], hd, head % 2 == 0)
                return (lambda: scores([(slice(tt * TOK, tt * TOK + TOK),
                                         [(qm_t[layer][half, head // 2, tt * P:tt * P + P], k2_t[layer][half, head // 2, :])])
                                        for tt in range(TT)]), FULL_BLOCKS, out)

            def causal_head(head):
                half = slice(64 * (head % 2), 64 * (head % 2) + 64)

                def out(hd, pt):
                    v = vb_a[:, :, head * 64:head * 64 + 64]
                    values([(half, slice(0, TOK), [(v[:, 0, :], pt[:, 0:TOK])], True, False),
                            (half, slice(P, TOK), [(v[:, 1, :], pt[:, TOK:TOK + P])], False, True)], hd, head % 2 == 0)
                return lambda: causal_scores(qb_t[half, head // 2, :], kb_t[half, head // 2, :]), CAUSAL_BLOCKS, out

            def attend(heads, beside=None):
                first, unit = n["head"], n["unit"]
                for s in range(len(heads) + 3):
                    if s < len(heads):
                        heads[s][0]()
                    if beside is not None:
                        beside(s)
                    if 2 <= s < len(heads) + 2:
                        turn_probs(prob_slot(unit + s - 2), heads[s - 2][1])
                    if s >= 3:
                        hd = first + s - 3
                        heads[s - 3][2](hd, prob_t[:, hd % 2, :])
                        n["out"] += hd % 2

            def tap_group(g):
                j0, tile = TAP_GROUPS[g]
                last = min(CONV_TAPS if tile == 4 else PE_TAPS, CONV_TAPS) - 1
                pe.wait_ge(diag_ready, g + 1)
                for j in range(j0, min(j0 + 4, CONV_TAPS)):
                    for t in range(2):
                        mm = pe.matmul(tap_bank[tile][:, t * TOK:t * TOK + TOK], diag[:, 8 * (g % 2) + 2 * (j % 4) + t, :],
                                       conv_in[:, tile + t, j:j + TOK], start=False, stop=j == last, skip_group_check=True)
                mm.then_inc(diag_used, 1)

            def swiglu(q, x):
                s, b = ffn_starts[q], FT * q
                for bank in range(4):
                    pe.matmul(ps[bank][:, :], zeros[:, 0:P], zeros[:, :], start=True, stop=False, skip_group_check=True)

                def gate_or_up(slot, col, last_first):
                    hi = whi[:, slot, :].rearrange("p (k n) -> p k n", k=KT)
                    lo = wlo[:, slot, :].rearrange("p (k n) -> p k n", k=KT)
                    for j in range(2):
                        for k in range(KT):
                            x_part(k, col == 0 and j == 0)
                            mm = split_product(ps[4 + j][:, col:col + TOK], hi[:, k, j * P:j * P + P],
                                               lo[:, k, j * P:j * P + P], xhi[x][:, k, :], xlo[x][:, k, :],
                                               k == 0, k == KT - 1)
                        if j == 0 and last_first:
                            mm.then_inc(gu0_done, 1)
                    mm.then_inc(chunk_used, 1)

                def pair(i, phase, last):
                    cb = s + 3 * i
                    pe.wait_ge(lo_ready, cb + 1)
                    gate_or_up(phase % SPLIT, 0, False)
                    pe.wait_ge(lo_ready, cb + 2)
                    gate_or_up((phase + 1) % SPLIT, TOK, True)
                    pe.wait_ge(lo_ready, cb + 3)
                    slot = (phase + 2) % SPLIT
                    hi = whi[:, slot, :].rearrange("p (k n) -> p k n", k=2)
                    lo = wlo[:, slot, :].rearrange("p (k n) -> p k n", k=2)
                    for j in range(2):
                        pe.wait_ge(hlo_ready, 2 * i + (b + j + 1))
                        for tt in range(TT):
                            for half in range(2):
                                mm = split_product(ps[2 * tt + half][:, :], hh_hi[:, j, tt * P:tt * P + P],
                                                   hh_lo[:, j, tt * P:tt * P + P], hi[:, j, half * 512:half * 512 + 512],
                                                   lo[:, j, half * 512:half * 512 + 512], False, last and j == 1)
                            if last and j == 1 and tt == 0:
                                mm.then_inc(ffn_half, 1)
                    mm.then_inc(chunk_used, 1)

                with pe.Fori(0, PAIRS - 1) as i:
                    pair(i, s % SPLIT, False)
                pair(PAIRS - 1, s % SPLIT, True)

            turn(xn, (xn_ready, 12))
            swiglu(0, 1)
            turn(xn, (xn_ready, 14))
            c0 = ffn_starts[0] + 3 * PAIRS
            for c in range(c0, c0 + 7):
                linear_cols(c, 0, c == c0)
            head_sums()
            tap_bank = {4: linear_bank(c0 + 7), 2: linear_bank(c0 + 6)}
            pe.wait_ge(evac_v, evac_count[c0 + 5][1])
            pe.matmul(tap_bank[4][:, :], zeros[:, 0:P], zeros[:, :], start=True, stop=False, skip_group_check=True)

            def taps_beside(step):
                for g in range(2 * step + 2, min(2 * step + 4, len(TAP_GROUPS))):
                    tap_group(g)

            tap_group(0)
            tap_group(1)
            pe.wait_ge(hn_ready, n["hs"])
            pe.wait_ge(evac_v, evac_count[c0 + 6][1])
            pe.matmul(tap_bank[2][:, :], zeros[:, 0:P], zeros[:, :], start=True, stop=False, skip_group_check=True)
            attend([memory_head(0, head) for head in range(4)], taps_beside)
            for i, (sem_, count) in enumerate(((tap_done, 2 * CONV_TAPS), (conv_ready, 1), (conv_ready, 2))):
                pe.wait_ge(sem_, count)
                for ct in ((0, 1), (4, 5), (2, 3))[i]:
                    mm = pe.matmul(ps[6][:, 0:TOK], ones, conv_out[:, ct, :], start=ct == 0, stop=ct == 3)
            mm.then_inc(csum_done, 1)
            for ct in range(CONV_TILES):
                pe.wait_ge(csq_ready, ct + 1)
                mm = pe.matmul(ps[7][:, 0:TOK], ones, conv_sq[:, ct, :], start=ct == 0, stop=ct == CONV_TILES - 1)
            mm.then_inc(csum_done, 1)
            for c in range(c0 + 7, c0 + 11):
                linear_rows(c, 1, tiles_ready=clo_ready if c == c0 + 7 else None)
            turn(xn, (xn_ready, 16))
            swiglu(1, 0)
            turn(xn, (xn_ready, 18))
            c0 = ffn_starts[1] + 3 * PAIRS
            linear_cols(c0, 1, True)
            turn(xn, (xn_ready, 18))
            linear_cols(c0 + 1, 1)
            x_ready()
            hs = n["hs"]
            head_sums()
            linear_cols(c0 + 2, 1)
            rotate(kb_t[:, 0:2, :], hs + 1)
            head_sums()
            linear_rows(c0 + 3, 1)
            rotate(kb_t[:, 2:4, :], hs + 2)
            head_sums()
            linear_rows(c0 + 4, 1)
            rotate(kb_t[:, 4:6, :], hs + 3)
            linear_rows(c0 + 5, 1)
            pe.wait_ge(evac_a, evac_count[c0 + 5][1])
            swiglu(2, 0)
            turn(xn, (xn_ready, 20))
            c0 = ffn_starts[2] + 3 * PAIRS
            linear_cols(c0, 1, True)
            linear_cols(c0 + 1, 1)
            hs = n["hs"]
            x_ready()
            head_sums()
            linear_cols(c0 + 2, 1)
            head_sums()
            linear_cols(c0 + 3, 1)
            rotate(qb_t[:, 0:2, :], hs + 2)
            head_sums()

            def beside_heads(step):
                if step == 0:
                    rotate(qb_t[:, 2:4, :], hs + 3)
                    head_sums()
                if step == 1:
                    rotate(qb_t[:, 4:6, :], hs + 4)
                if step == 2:
                    pe.wait_ge(rope_done, 6)

            pe.wait_ge(rope_done, 4)
            attend([causal_head(head) for head in range(12)] + [memory_head(1, head) for head in range(4)], beside_heads)
            pe.wait_ge(o_evac, n["out"])
            for c in range(c0 + 4, c0 + 8):
                linear_rows(c, 0)
            turn(xn, (xn_ready, 22))
            swiglu(3, 1)

        @block.scalar
        def _(act):
            n = {"warm": 0, "chunk": 0, "norm": 0, "turn": 0, "unit": 0, "head": 0, "ohi": 0, "hs": 0}

            def round_chunk(c):
                act.wait_ge(raw_in[c % RAW], landed(c))
                if c >= SPLIT:
                    act.wait_ge(chunk_used, c - SPLIT + 1)
                act.activation(whi[:, c % SPLIT, :], raw[:, c % RAW, :], ACT.Copy).then_inc(hi_ready, 1)

            def round_to(c):
                while n["chunk"] < min(c, n_chunks) and not (n["chunk"] == moe_at and not n.get("moe")):
                    round_chunk(n["chunk"])
                    n["chunk"] += 1

            def warm(func):
                act.activation(warmth[:, n["warm"]:n["warm"] + 1], ones[:, 0:1], func)
                n["warm"] += 1

            def row_stats(src, ready=None):
                i = n["norm"]
                warm(ACT.Sqrt)
                if n["turn"]:
                    act.wait_ge(tr_done, n["turn"])
                for tt in range(TT):
                    if ready is not None:
                        act.wait_ge(*ready[tt])
                    act.activation(xn[:, tt, :], src[:, tt, :], ACT.Square,
                                   accum_out=sumsq[:, tt:tt + 1]).then_inc(ss_ready, 1)
                act.wait_ge(ms_ready, i + 1)
                act.activation(root, meansq, ACT.Sqrt).then_inc(rt_ready, 1)
                n["norm"] += 1

            def split_turned(x, gain):
                for kp in range(KT // 2):
                    fill = n["turn"]
                    act.wait_ge(tr_done, fill + 1)
                    for kk in range(2):
                        k = 2 * kp + kk
                        ins_ = act.activation(xhi[x][:, k, :], fill_bank(fill)[:, kk * TOK:kk * TOK + TOK], ACT.Copy,
                                              scale=1.0 if gain is None else cols[:, gain + k:gain + k + 1])
                    ins_.then_inc(xhi_ready, 1)
                    n["turn"] += 1

            def exps(width, src, scale, in_bank):
                u = n["unit"]
                act.wait_ge(nm_ready, u + 1)
                if in_bank:
                    act.wait_ge(t_done, slot_free(u))
                if width == CAUSAL_W:
                    parts = (slice(0, P), slice(P, CAUSAL_W))
                else:
                    parts = (slice(0, TOK), slice(TOK, 2 * TOK))
                for tt, cols_ in enumerate(parts):
                    ins_ = act.activation(prob_slot(u)[:, cols_], src[:, cols_], ACT.Exp, scale=scale,
                                          bias=nmax[:, stat_cols(u, tt)], accum_out=psum_e[:, stat_cols(u, tt)])
                ins_.then_inc(e_ready, 1)
                n["unit"] += 1

            def copy_probs(width):
                hd = n["head"]
                act.wait_ge(t_done, hd + 1)
                if hd >= 2:
                    act.wait_ge(o_done, hd - 1)
                act.activation(prob_t[:, hd % 2, 0:width], turned_bank(hd)[:, 0:width], ACT.Copy).then_inc(pt_ready, 1)
                n["head"] += 1

            def out_hi(x, k0, tiles, heads):
                act.wait_ge(o_done, heads)
                act.activation(xhi[x][:, k0:k0 + tiles, :], out_bank(heads - 1)[:, 0:tiles * TOK].rearrange("p (a b) -> p a b", a=tiles),
                               ACT.Copy).then_inc(o_hi, 1)
                n["ohi"] += 1

            def bank_rows(c):
                return linear_bank(c)[:, :].rearrange("p (t n) -> p t n", t=2)

            def used(c):
                act.wait_ge(chunk_used, c + 1)

            at_row = [0]

            def rows(dst, r0, src):
                n = src.shape[0]
                act.dma_start(dst[r0:r0 + n, :], src).then_inc(in_rows, 16)
                at_row[0] += 1

            for r0, name in ((G_MIX, "norm_mix"), (G_XQ, "norm_xq"), (G_MEM, "norm_mem")):
                rows(rows_a, r0, ins[name][0].rearrange("(k p) -> k p", p=P))
            for r0, name in ((G_FFN1, "ffn1_norm_g_2"), (G_MIX2, "mix_norm_g_2"), (G_MEM2, "mem_norm_g_2"),
                             (G_FFN2, "ffn2_norm_g_2")):
                rows(rows_a, r0, ins[name].rearrange("l (k p) -> (l k) p", p=P))
            rows(rows_a, G_KV, ins["kv_norm_g_2"].rearrange("(k p) -> k p", p=P))
            for r0, name in ((G_LNG, "a_ln_g_2"), (G_LNB, "a_ln_b_2"), (G_DWB, "a_dw_bias_2")):
                rows(rows_a, r0, ins[name][0].rearrange("(k p) -> k p", p=P))
            rows(rows_a, G_SGUB, ins["sgu_b"][0])
            assert at_row[0] == 12
            act.wait_ge(in_c, 16)
            row_stats(h, ((in_x[0], 16), (in_x[1], 16)))
            round_to(1)
            act.wait_ge(cols_ready, 1)
            split_turned(0, G_MIX)
            round_to(3)
            for c in range(10):
                round_to(c + 3)
                if c < 4:
                    used(c)
                    dst = (u_a if c < 2 else v_a)[:, :, (c % 2) * CW:(c % 2) * CW + CW]
                    act.activation(dst, bank_rows(c), ACT.Gelu).then_inc(evac_a, 1)
                if c == 4:
                    act.wait_ge(in_mem, 16)
                    row_stats(mem_a)
                if c == 7:
                    split_turned(1, G_MEM)
                if c == 6:
                    act.wait_ge(bn_ready, 1)
                    act.activation(ort, oms, ACT.Sqrt).then_inc(bn_root, 1)
                    act.wait_ge(lam_ready, 1)
                    act.activation(lame, lams, ACT.Exp).then_inc(lam_exp, 1)
                    act.wait_ge(rope_half, 1)
                    act.activation(sin_t, f_silu[:, 0, :], ACT.Sin).then_inc(rope_sin, 1)
                    act.activation(cos_t, f_silu[:, 0, :], ACT.Sin, scale=0.5).then_inc(rope_sin, 1)
            act.wait_ge(wt_ready, 1)
            act.activation(sgu_wt.rearrange("p a b -> p (a b)"), ps[4][:, :], ACT.Copy).then_inc(wt_copied, 1)
            round_to(13)
            for hd in range(4):
                for _ in range(2):
                    exps(CAUSAL_W, prob[:, n["unit"] % 2, :], 2.0 ** (-8.0 * (hd + 1) / 4), False)
                round_to(14 + 2 * hd)
                round_to(15 + 2 * hd)
                copy_probs(CAUSAL_W)
                act.wait_ge(o_copied, hd + 1)
                if hd == 3:
                    warm(ACT.Sqrt)
                for tt in range(TT):
                    act.activation(u_a[:, tt, hd * P:hd * P + P], xn[:, tt, 512 + hd * P:512 + hd * P + P],
                                   ACT.Square, accum_out=oss[:, 2 * hd + tt:2 * hd + tt + 1]).then_inc(o_ss, 1)
            act.wait_ge(o_ms, 1)
            act.activation(ort, oms, ACT.Sqrt).then_inc(o_rt, 1)
            split_turned(0, None)
            for c in range(18, 22):
                round_to(c + 3)
            act.wait_ge(h_ready, 1)
            row_stats(h)
            split_turned(1, G_XQ)

            def queries(c):
                round_to(c + 3)
                used(c)
                act.activation(q1_t[:, 2 * (c - 22):2 * (c - 22) + 2, :], bank_rows(c), ACT.Copy).then_inc(evac_a, 1)

            def full_exps(scale):
                u = n["unit"]
                exps(512, ps[4 + u % 2], scale, True)

            queries(22)
            queries(23)
            full_exps(1.0 / 16)
            queries(24)
            full_exps(1.0 / 16)
            queries(25)
            for head in range(4):
                copy_probs(512)
                if head < 2:
                    full_exps(1.0 / 16)
                out_hi(0, 2 * head, 2, 5 + head)
            def head_squares(c):
                used(c)
                if n["hs"] >= 1:
                    act.wait_ge(hs_done, n["hs"])
                act.activation(prob[:, 0, :], linear_bank(c)[:, :], ACT.Square).then_inc(sq_ready, 1)

            def head_root():
                act.wait_ge(hms_ready, n["hs"] + 1)
                act.activation(prob[:, 1, :], prob[:, 1, :], ACT.Sqrt).then_inc(hrt_ready, 1)
                n["hs"] += 1

            round_to(29)
            act.wait_ge(in_mem2, 16)
            row_stats(mem2_a)
            round_to(30)
            split_turned(1, G_MEM2)
            round_to(32)
            act.wait_ge(h_ready, 2)
            row_stats(h)
            split_turned(0, None)
            act.wait_ge(in_late, 48)
            act.activation(wr_hi, wr_raw, ACT.Copy).then_inc(wr_split, 1)
            head_squares(mem2_at)
            round_to(mem2_at + 4)
            act.wait_ge(r_bias, 1)
            for tt in range(TT):
                ins_ = act.activation(prob_t[:, 0, 4 * tt:4 * tt + 4], glog[:, 8 * tt:8 * tt + 4], ACT.Exp,
                                      bias=gneg[:, tt:tt + 1], accum_out=gsum[:, tt:tt + 1])
            ins_.then_inc(r_exp, 1)
            act.wait_ge(r_ediff, 1)
            act.activation(eexp, ediff, ACT.Exp).then_inc(r_eexp, 1)
            split_turned(1, G_MEM2 + 8)
            head_root()
            head_squares(mem2_at + 2)
            head_root()

            def copy_gathered(half, count):
                act.wait_ge(main["fill"], count)
                act.activation(xg[:, 4 * half:4 * half + 4, :], ps[5][:, :].rearrange("p (k n) -> p k n", k=4),
                               ACT.Copy).then_inc(main["evac"], 1)

            def copy_spread(half, count):
                act.wait_ge(main["fill"], count)
                act.activation(spread[:, 2 * half:2 * half + 2, :], ps[5][:, :].rearrange("p (k n) -> p k n", k=2),
                               ACT.Copy).then_inc(main["evac"], 1)

            def expert_silu(s, count):
                act.wait_ge(s["gu"], count)
                act.activation(e_silu, ps[4][:, 0:P], ACT.Silu).then_inc(s["silu"], 1)

            def expert_out(s, first_half):
                act.wait_ge(s["y_full"], first_half)
                act.activation(y_sb[:, 0:512], ps[6][:, :], ACT.Copy).then_inc(s["y0"], 1)

            copy_gathered(0, 1)
            copy_gathered(1, 2)
            with act.Fori(0, EXPERTS // EG) as g:
                for e in range(EG):
                    expert_silu(main, 4 * g + e + 1)
                    if e == 0:
                        copy_spread(0, 4 * g + 3)
                        copy_spread(1, 4 * g + 4)
                    expert_out(main, 8 * g + 2 * e + 1)
                copy_gathered(0, 4 * g + 5)
                copy_gathered(1, 4 * g + 6)
            act.wait_ge(extra_ready, 1)
            extra = act.value_load(extra_i[0:1, 0:1], min_val=0, max_val=MAX_ROUNDS - 1)
            with act.If(extra > 0):
                with act.Fori(0, extra) as r:
                    with act.Fori(0, EXPERTS) as x:
                        step = EXPERTS * r + x + 1
                        act.wait_ge(over["fill"], step)
                        act.activation(xg[:, :, 0:SLOTS], ps[5][:, 0:256].rearrange("p (k n) -> p k n", k=KT), ACT.Copy)
                        act.activation(spread[:, 0, :], ps[5][:, 256:512], ACT.Copy).then_inc(over["evac"], 1)
                        expert_silu(over, step)
                        expert_out(over, 2 * step - 1)

            act.wait_ge(moe_done, 1)
            n["moe"] = True
            round_to(moe_at + 1)
            row_stats(h, ((h_added, 1), (h_added, 2)))
            round_to(moe_at + 2)

            def swiglu(q):
                s, b = ffn_starts[q], PAIRS * q
                warm(ACT.Silu)
                round_to(s + 3)

                def silus(i, cb):
                    act.wait_ge(gu0_done, i + (b + 1))
                    act.activation(f_silu[:, 0, :], ps[4][:, 0:TOK], ACT.Silu).then_inc(silu_ready, 1)
                    act.wait_ge(chunk_used, cb + 2)
                    act.activation(f_silu[:, 1, :], ps[5][:, 0:TOK], ACT.Silu).then_inc(silu_ready, 1)

                with act.Fori(0, PAIRS // 2) as it:
                    for half in range(2):
                        i, cb = 2 * it + half, 6 * it + (s + 3 * half)
                        for j in range(3):
                            c0_ = s + 3 * half + 3 + j
                            act.wait_ge(raw_in[c0_ % RAW], 16 * it + landed(c0_))
                            act.wait_ge(chunk_used, 6 * it + (c0_ - SPLIT + 1))
                            act.activation(whi[:, c0_ % SPLIT, :], raw[:, c0_ % RAW, :], ACT.Copy).then_inc(hi_ready, 1)
                            if j == 0:
                                silus(i, cb)
                n["chunk"] = s + 3 * PAIRS
                cb = s + 3 * (PAIRS - 1)
                round_to(cb + 4)
                silus(PAIRS - 1, cb)
                round_to(cb + 5)

            row_stats(h, ((h_tile, 1), (h_ready, 3)))
            split_turned(1, G_FFN1)
            swiglu(0)
            row_stats(h, ((h_tile, 2), (h_ready, 4)))
            split_turned(0, G_MIX2)
            c0 = ffn_starts[0] + 3 * PAIRS
            for i in range(3):
                round_to(c0 + 2 * i + 4)
                used(c0 + 2 * i + 1)
                if i >= 1:
                    act.wait_ge(glu_done, i)
                act.activation(sig, bank_rows(c0 + 2 * i + 1), ACT.Sigmoid).then_inc(sig_ready, 1)
            round_to(c0 + 9)
            head_squares(c0 + 6)
            head_root()

            def attend(widths, x, tiles, beside=None):
                first = n["head"]
                warm(ACT.Exp)
                for s in range(len(widths) + 4):
                    if s < len(widths):
                        if widths[s] == CAUSAL_W:
                            exps(CAUSAL_W, prob_slot(n["unit"]), 1.0, False)
                        else:
                            full_exps(0.125)
                    if beside is not None:
                        beside(s)
                    if 2 <= s < len(widths) + 2:
                        copy_probs(widths[s - 2])
                    if s >= 5 and s % 2:
                        out_hi(x, tiles[(s - 5) // 2], 1, first + s - 3)

            attend([512] * 4, 1, (6, 7))
            warm(ACT.Sqrt)
            act.wait_ge(csum_done, 1)
            act.activation(prob[:, 0, 0:TOK], ps[6][:, 0:TOK], ACT.Copy, scale=1.0 / 768).then_inc(cmu_ready, 1)
            for ct in range(CONV_TILES):
                act.wait_ge(cent_ready, ct + 1)
                act.activation(conv_sq[:, ct, :], conv_out[:, ct, :], ACT.Square).then_inc(csq_ready, 1)
            act.wait_ge(cms_ready, 1)
            act.activation(prob[:, 0, 0:TOK], prob[:, 1, 0:TOK], ACT.Sqrt).then_inc(crt_ready, 1)
            warm(ACT.Silu)
            for ct in range(CONV_TILES + 1):
                if ct < CONV_TILES:
                    act.wait_ge(cn_ready, ct + 1)
                    act.activation(conv_sq[:, ct, :], conv_out[:, ct, :], ACT.Silu, scale=cols[:, G_LNG + ct:G_LNG + ct + 1],
                                   bias=cols[:, G_LNB + ct:G_LNB + ct + 1]).then_inc(csilu_ready, 1)
                if ct >= 1:
                    act.wait_ge(csilu_ready, ct)
                    act.activation(xhi[1][:, ct - 1, :], conv_sq[:, ct - 1, :], ACT.Copy).then_inc(chi_ready, 1)
            round_to(c0 + 13)
            act.wait_ge(h_ready, 5)
            row_stats(h)
            split_turned(0, G_FFN2)
            swiglu(1)
            row_stats(h, ((h_tile, 3), (h_ready, 6)))
            split_turned(1, G_KV)
            c0 = ffn_starts[1] + 3 * PAIRS
            split_turned(0, G_FFN1 + 8)
            for i in range(3):
                round_to(c0 + i + 4)
                head_squares(c0 + i)
                head_root()
            for i in range(3):
                round_to(c0 + i + 6)
                used(c0 + 3 + i)
                act.activation(vb_a[:, :, i * CW:i * CW + CW], bank_rows(c0 + 3 + i), ACT.Copy).then_inc(evac_a, 1)
            round_to(c0 + 9)
            swiglu(2)
            row_stats(h, ((h_tile, 4), (h_ready, 7)))
            split_turned(1, G_MIX2 + 8)
            c0 = ffn_starts[2] + 3 * PAIRS
            for i in range(3):
                round_to(c0 + i + 4)
                head_squares(c0 + i)
                head_root()
            round_to(c0 + 7)

            def beside_heads(step):
                if step == 0:
                    head_squares(c0 + 3)
                    head_root()

            attend([CAUSAL_W] * 12 + [512] * 4, 0, range(8), beside_heads)
            round_to(c0 + 10)
            act.wait_ge(h_ready, 8)
            row_stats(h)
            split_turned(1, G_FFN2 + 8)
            swiglu(3)

        @block.vector
        def _(dve):
            n = {"chunk": 0, "norm": 0, "turn": 0, "unit": 0, "head": 0, "out": 0, "hs": 0, "rot": 0, "link": 0, "h": 0}

            def link(ins_):
                n["link"] += 1
                ins_.then_inc(v_link, 1)
                dve.wait_ge(v_link, n["link"])

            def split_chunk(c):
                dve.wait_ge(hi_ready, c + 1)
                dve.tensor_tensor(wlo[:, c % SPLIT, :], raw[:, c % RAW, :], whi[:, c % SPLIT, :].bitcast(F32),
                                  ALU.subtract).then_inc(lo_ready, 1)

            def split_to(c):
                while n["chunk"] < min(c, n_chunks) and not (n["chunk"] == moe_at and not n.get("moe")):
                    split_chunk(n["chunk"])
                    n["chunk"] += 1

            def row_scale():
                i = n["norm"]
                dve.wait_ge(ss_ready, 2 * i + 2)
                dve.tensor_scalar(meansq, sumsq, 1.0 / D, RMS_EPS, ALU.mult, ALU.add).then_inc(ms_ready, 1)
                dve.wait_ge(rt_ready, i + 1)
                link(dve.reciprocal(rstd, root))
                n["norm"] += 1

            def normed_rows(src):
                row_scale()
                for tt in range(TT):
                    dve.tensor_scalar(xn[:, tt, :], src[:, tt, :], rstd[:, tt:tt + 1], None, ALU.mult).then_inc(xn_ready, 1)

            def split_turned(x, gain):
                for kp in range(KT // 2):
                    fill = n["turn"]
                    dve.wait_ge(xhi_ready, fill + 1)
                    for kk in range(2):
                        k = 2 * kp + kk
                        src = fill_bank(fill)[:, kk * TOK:kk * TOK + TOK]
                        if gain is None:
                            ins_ = dve.tensor_tensor(xlo[x][:, k, :], src, xhi[x][:, k, :].bitcast(F32), ALU.subtract)
                        else:
                            ins_ = dve.scalar_tensor_tensor(xlo[x][:, k, :], src, cols[:, gain + k:gain + k + 1],
                                                            xhi[x][:, k, :].bitcast(F32), ALU.mult, ALU.subtract)
                    ins_.then_inc(xlo_ready, 1)
                    n["turn"] += 1

            def bank_rows(c):
                return linear_bank(c)[:, :].rearrange("p (t n) -> p t n", t=2)

            def used(c):
                dve.wait_ge(chunk_used, c + 1)

            def copy_out(c, dst):
                used(c)
                dve.tensor_copy(dst, bank_rows(c)).then_inc(evac_v, 1)

            def add_to_h(c, j):
                used(c)
                dst = h[:, :, j * CW:j * CW + CW]
                dve.tensor_tensor(dst, dst, bank_rows(c), ALU.add).then_inc(evac_v, 1)

            def h_updated():
                dve.wait_ge(evac_v, evac_count[n["last_h"]][1])
                dve.tensor_copy(bn2[:, 0:1], rstd[:, 0:1]).then_inc(h_ready, 1)

            def causal_max(bias, mult, slope):
                u = n["unit"]
                slot, nm = prob_slot(u), nmax[:, stat_cols(u)]
                dve.wait_ge(s_full, u + 1)
                if slot_free(u):
                    dve.wait_ge(t_done, slot_free(u))
                link(dve.scalar_tensor_tensor(slot[:, 0:CAUSAL_W], ps[4 + u % 2][:, 0:CAUSAL_W], mult, bias,
                                              ALU.mult, ALU.add))
                dve.tensor_reduce(nm[:, 0:1], slot[:, 0:P], AX, ALU.max, negate=True)
                ins_ = dve.tensor_reduce(nm[:, 1:2], slot[:, P:CAUSAL_W], AX, ALU.max, negate=True)
                if slope != 1.0:
                    link(ins_)
                    ins_ = dve.tensor_scalar(nm, nm, slope, None, ALU.mult)
                ins_.then_inc(nm_ready, 1)
                n["unit"] += 1

            def full_max(scale):
                u = n["unit"]
                dve.wait_ge(s_full, u + 1)
                nm = nmax[:, stat_cols(u)]
                link(dve.tensor_reduce(nm, ps[4 + u % 2][:, :].rearrange("p (t n) -> p t n", t=2), AX, ALU.max, negate=True))
                dve.tensor_scalar(nm, nm, scale, None, ALU.mult).then_inc(nm_ready, 1)
                n["unit"] += 1

            def probs(u, width):
                dve.wait_ge(e_ready, u + 1)
                r, slot = rsum[:, stat_cols(u)], prob_slot(u)
                link(dve.reciprocal(r, psum_e[:, stat_cols(u)]))
                parts = (slice(0, P), slice(P, CAUSAL_W)) if width == CAUSAL_W else (slice(0, TOK), slice(TOK, 2 * TOK))
                for tt, cols_ in enumerate(parts):
                    ins_ = dve.tensor_scalar(slot[:, cols_], slot[:, cols_], r[:, tt:tt + 1], None, ALU.mult)
                ins_.then_inc(p_ready, 1)
                n["head"] += 1

            def diff_probs(hd):
                dve.wait_ge(e_ready, 2 * hd + 2)
                link(dve.reciprocal(rsum[:, 0:4], psum_e[:, 0:4]))
                link(dve.tensor_scalar(rsum[:, 2:4], rsum[:, 2:4], neglam, None, ALU.mult))
                parts = (slice(0, P), slice(P, CAUSAL_W))
                for tt, cols_ in enumerate(parts):
                    ins_ = dve.tensor_scalar(prob[:, 0, cols_], prob[:, 0, cols_], rsum[:, tt:tt + 1], None, ALU.mult)
                link(ins_)
                for tt, cols_ in enumerate(parts):
                    ins_ = dve.scalar_tensor_tensor(prob[:, 0, cols_], prob[:, 1, cols_], rsum[:, 2 + tt:3 + tt],
                                                    prob[:, 0, cols_], ALU.mult, ALU.add)
                ins_.then_inc(p_ready, 1)
                n["head"] += 1

            def out_lo(x, k0, tiles, head):
                dve.wait_ge(o_hi, n["olo"] + 1)
                dve.tensor_tensor(xlo[x][:, k0:k0 + tiles, :], out_bank(head)[:, 0:tiles * TOK].rearrange("p (a b) -> p a b", a=tiles),
                                  xhi[x][:, k0:k0 + tiles, :].bitcast(F32), ALU.subtract).then_inc(o_evac, 1)
                n["olo"] += 1

            n["olo"] = 0

            dve.memset(zeros[:, :], 0.0).then_inc(zero_ready, 1)
            for tt in range(TT):
                dve.wait_ge(in_x[tt], 16)
            normed_rows(h)
            dve.wait_ge(cols_t, 1)
            m = DW_ROWS - P + 6
            dve.tensor_copy(cols[:, 0:G_A], ps[5][:, 0:G_A])
            dve.tensor_copy(cols[:, 128:256 + m], ps[5][:, 128:256 + m]).then_inc(cols_ready, 1)
            split_to(1)
            split_turned(0, G_MIX)
            split_to(3)
            for c in range(10):
                split_to(c + 3)
                if 4 <= c < 6:
                    copy_out(c, q_t[:, 2 * (c - 4):2 * (c - 4) + 2, :])
                elif 6 <= c < 8:
                    copy_out(c, k_t[:, 2 * (c - 6):2 * (c - 6) + 2, :])
                elif c >= 8:
                    copy_out(c, val_a[:, :, (c - 8) * CW:(c - 8) * CW + CW])
                if c == 7:
                    split_turned(1, G_MEM)
                if c == 4:
                    row_scale()
                    dve.wait_ge(in_mem, 16)
                    for tt in range(TT):
                        dve.tensor_scalar(xn[:, tt, :], mem_a[:, tt, :], rstd[:, tt:tt + 1], None, ALU.mult).then_inc(xn_ready, 1)
                if c == 5:
                    dve.wait_ge(evac_a, 4)
                    for i in range(8):
                        tt, g = i // 4, i % 4
                        ins_ = dve.bn_stats(bn6[:, 6 * i:6 * i + 6], v_a[:, tt, g * P:g * P + P])
                    link(ins_)
                    for i in range(8):
                        ins_ = dve.bn_aggr(bn2[:, 2 * i:2 * i + 2], bn6[:, 6 * i:6 * i + 6])
                    link(ins_)
                    dve.tensor_scalar(oms, bn2[:, 1:16:2], LN_EPS, None, ALU.add).then_inc(bn_ready, 1)
                if c == 6:
                    dve.wait_ge(in_bc, 16 * 8)
                    link(dve.tensor_tensor(lamv[:, 0:4:2, :], lamv[:, 0:4:2, :], lamv[:, 1:4:2, :], ALU.mult))
                    dve.tensor_reduce(lams, lamv[:, 0:4:2, :], AX, ALU.add).then_inc(lam_ready, 1)
                    ang, turns = f_silu[:, 0, :], f_silu[:, 1, :]
                    link(dve.tensor_copy(ang, posi))
                    link(dve.tensor_scalar(ang, ang, cst[:, C_FREQ:C_FREQ + 1], None, ALU.mult))
                    link(dve.tensor_scalar(turns, ang, float(np.float32(1 / (2 * np.pi))), MAGIC, ALU.mult, ALU.add))
                    link(dve.tensor_scalar(turns, turns, MAGIC, None, ALU.subtract))
                    for part in TWO_PI:
                        link(dve.scalar_tensor_tensor(ang, turns, -part, ang, ALU.mult, ALU.add))
                    dve.tensor_scalar(ang, ang, -3.1415925, 3.1415925, ALU.max, ALU.min).then_inc(rope_half, 1)
                if c == 7:
                    dve.wait_ge(lam_exp, 1)
                    dve.scalar_tensor_tensor(neglam, lame[:, 1:2], -LAMBDA_INIT, lame[:, 0:1], ALU.add, ALU.subtract)
                    dve.tensor_scalar(subln[:, :], subln[:, :], 1.0 - LAMBDA_INIT, None, ALU.mult)
                    dve.wait_ge(rope_sin, 2)
                    link(dve.tensor_tensor(cos_t, cos_t, cos_t, ALU.mult))
                    dve.tensor_scalar(cos_t, cos_t, -2.0, 1.0, ALU.mult, ALU.add)
                    dve.wait_ge(in_sgu, 48)
                    for g in range(4):
                        ins_ = dve.tensor_tensor(sgu_w[:, g, :], sgu_w[:, g, :], cst[:, C_TRIL:C_TRIL + P], ALU.mult)
                    ins_.then_inc(wt_done, 1)
                    dve.wait_ge(bn_root, 1)
                    link(dve.reciprocal(ors, ort))
                    for i in range(8):
                        v = v_a[:, i // 4, (i % 4) * P:(i % 4) * P + P]
                        ins_ = dve.tensor_scalar(v, v, bn2[:, 2 * i:2 * i + 1], ors[:, i:i + 1], ALU.subtract, ALU.mult)
                    link(ins_)
                    for j, op in enumerate((ALU.mult, ALU.add)):
                        for tt in range(TT):
                            ins_ = dve.tensor_tensor(v_a[:, tt, :], v_a[:, tt, :], ln_gb[:, j, :], op)
                        if j == 0:
                            link(ins_)
                    ins_.then_inc(vn_ready, 1)
            for tt in range(TT):
                dve.wait_ge(sp_done, tt + 1)
                for g in range(4):
                    ins_ = dve.scalar_tensor_tensor(xn[:, tt, g * P:g * P + P], ps[4 + tt][:, g * P:g * P + P],
                                                    cols[:, G_SGUB + g:G_SGUB + g + 1], u_a[:, tt, g * P:g * P + P],
                                                    ALU.add, ALU.mult)
            ins_.then_inc(sgu_done, 1)
            split_to(13)
            for hd in range(4):
                slope = 2.0 ** (-8.0 * (hd + 1) / 4)
                for _ in range(2):
                    causal_max(cst[:, C_ND:C_ND + CAUSAL_W], 0.125 / slope, slope)
                diff_probs(hd)
                split_to(14 + 2 * hd)
                split_to(15 + 2 * hd)
                for c in (10 + 2 * hd, 11 + 2 * hd):
                    if c < 14:
                        copy_out(c, k1_t[:, 2 * (c - 10):2 * (c - 10) + 2, :])
                    else:
                        copy_out(c, v1_a[:, :, (c - 14) * CW:(c - 14) * CW + CW])
                dve.wait_ge(o_done, hd + 1)
                dve.tensor_copy(xn[:, :, 512 + hd * P:512 + hd * P + P],
                                ps[O_BANK][:, 0:2 * P].rearrange("p (t n) -> p t n", t=2)).then_inc(o_evac, 1)
                dve.wait_ge(o_evac, hd + 1)
                dve.tensor_copy(bn2[:, 0:1], rstd[:, 0:1]).then_inc(o_copied, 1)
            dve.wait_ge(o_ss, 8)
            dve.tensor_scalar(oms, oss, 1.0 / P, RMS_EPS, ALU.mult, ALU.add).then_inc(o_ms, 1)
            dve.wait_ge(o_rt, 1)
            link(dve.reciprocal(ors, ort))
            for hd in range(4):
                for tt in range(TT):
                    o = xn[:, tt, 512 + hd * P:512 + hd * P + P]
                    ins_ = dve.scalar_tensor_tensor(o, o, ors[:, 2 * hd + tt:2 * hd + tt + 1], subln[:, :], ALU.mult, ALU.mult)
            ins_.then_inc(mixed_ready, 1)
            split_turned(0, None)
            for c in range(18, 22):
                split_to(c + 3)
                add_to_h(c, c - 18)
            n["last_h"] = 21
            h_updated()
            normed_rows(h)
            split_turned(1, G_XQ)
            split_to(26)
            full_max(1.0 / 16)
            split_to(27)
            full_max(1.0 / 16)
            probs(8, 512)
            full_max(1.0 / 16)
            split_to(28)
            probs(9, 512)
            out_lo(0, 0, 2, 4)
            full_max(1.0 / 16)
            probs(10, 512)
            out_lo(0, 2, 2, 5)
            probs(11, 512)
            out_lo(0, 4, 2, 6)
            out_lo(0, 6, 2, 7)
            def head_norm(c, dst, gain):
                dve.wait_ge(hs_done, n["hs"] + 1)
                dve.tensor_scalar(prob[:, 1, :], ps[7][:, :], 1.0 / 64, RMS_EPS, ALU.mult, ALU.add).then_inc(hms_ready, 1)
                dve.wait_ge(hrt_ready, n["hs"] + 1)
                link(dve.reciprocal(prob[:, 1, :], prob[:, 1, :]))
                link(dve.scalar_tensor_tensor(dst, bank_rows(c), cols[:, G_HEAD + gain:G_HEAD + gain + 1],
                                              prob[:, 1, :].rearrange("p (a b) -> p a b", a=2), ALU.mult, ALU.mult))
                n["hs"] += 1
                dve.tensor_copy(bn2[:, 0:1], rstd[:, 0:1]).then_inc(hn_ready, 1)
                dve.tensor_copy(bn2[:, 2:3], rstd[:, 0:1]).then_inc(evac_v, 1)

            for c in range(26, 30):
                if c == 28:
                    split_turned(1, G_MEM2)
                if c == 27:
                    row_scale()
                    dve.wait_ge(in_mem2, 16)
                    for tt in range(TT):
                        dve.tensor_scalar(mem2_a[:, tt, :], mem2_a[:, tt, :], rstd[:, tt:tt + 1], None,
                                          ALU.mult).then_inc(xn_ready, 1)
                split_to(min(c + 3, 32))
                add_to_h(c, c - 26)
            n["last_h"] = 29
            h_updated()
            row_scale()
            dve.wait_ge(in_late, 48)
            for tt in range(TT):
                ins_ = dve.tensor_scalar(xn[:, tt, :], h[:, tt, :], rstd[:, tt:tt + 1], None, ALU.mult)
            link(ins_)
            for tt in range(TT):
                dve.tensor_tensor(xn[:, tt, :], xn[:, tt, :], gain_b, ALU.mult).then_inc(xn_ready, 1)
            dve.memset(glog, -3e38)
            dve.memset(posm[:, :, EXPERTS:], -1.0)
            dve.memset(wgt[:, :, EXPERTS:], 0.0)
            split_turned(0, None)
            dve.wait_ge(wr_split, 1)
            dve.tensor_tensor(wr_lo, wr_raw, wr_hi.bitcast(F32), ALU.subtract).then_inc(wr_ready, 1)
            split_to(mem2_at + 4)
            dve.wait_ge(r_done, 1)
            for tt in range(TT):
                ins_ = dve.tensor_tensor(logit[:, 36 * tt:36 * tt + 36], ps[4][:, 36 * tt:36 * tt + 36], rb, ALU.add)
            link(ins_)
            for tt in range(TT):
                ins_ = dve.tensor_copy(glog[:, 8 * tt:8 * tt + 4], logit[:, 36 * tt:36 * tt + 4])
            link(ins_)
            for tt in range(TT):
                ins_ = dve.max(gmax[:, 8 * tt:8 * tt + 8], glog[:, 8 * tt:8 * tt + 8])
            link(ins_)
            for tt in range(TT):
                ins_ = dve.max_index(picks[:, 0, tt, :], gmax[:, 8 * tt:8 * tt + 8], glog[:, 8 * tt:8 * tt + 8])
            link(ins_)
            dve.tensor_copy(gidx, picks[:, 0, :, 0])
            dve.tensor_scalar(gneg, gmax[:, 0:16:8], -1.0, None, ALU.mult).then_inc(r_bias, 1)
            dve.wait_ge(r_bias, 1)
            for tt in range(TT):
                ins_ = dve.tensor_scalar(emask[:, 32 * tt:32 * tt + 32], cst[:, C_GRP:C_GRP + 32], gidx[:, tt:tt + 1], None,
                                         ALU.is_equal)
            link(ins_)
            for tt in range(TT):
                lg = logit[:, 36 * tt + 4:36 * tt + 36]
                ins_ = dve.tensor_tensor(lg, lg, emask[:, 32 * tt:32 * tt + 32], ALU.mult)
            link(ins_)
            link(dve.tensor_scalar(emask, emask, -NEG, NEG, ALU.mult, ALU.add))
            for tt in range(TT):
                lg = logit[:, 36 * tt + 4:36 * tt + 36]
                ins_ = dve.tensor_tensor(lg, lg, emask[:, 32 * tt:32 * tt + 32], ALU.add)
            link(ins_)
            for tt in range(TT):
                ins_ = dve.max(emax[:, 8 * tt:8 * tt + 8], logit[:, 36 * tt + 4:36 * tt + 36])
            link(ins_)
            for tt in range(TT):
                ins_ = dve.max_index(picks[:, 1, tt, :], emax[:, 8 * tt:8 * tt + 8], logit[:, 36 * tt + 4:36 * tt + 36])
            link(ins_)
            dve.tensor_copy(eidx[:, 0:4].rearrange("p (t i) -> p t i", t=2), picks[:, 1, :, 0:2])
            dve.tensor_tensor(ediff, emax[:, 1:16:8], emax[:, 0:16:8], ALU.subtract).then_inc(r_ediff, 1)
            dve.wait_ge(r_exp, 1)
            link(dve.reciprocal(ggate, gsum))
            dve.wait_ge(r_eexp, 1)
            link(dve.tensor_scalar(eden, eexp, 1.0, None, ALU.add))
            link(dve.reciprocal(eden, eden))
            link(dve.tensor_tensor(w1, ggate, eden, ALU.mult))
            link(dve.tensor_tensor(w2, w1, eexp, ALU.mult))
            for tt in range(TT):
                dve.tensor_scalar(hot[:, tt, :], slot_row, eidx[:, 2 * tt:2 * tt + 1], None, ALU.is_equal)
                ins_ = dve.tensor_scalar(hot2[:, tt, :], slot_row, eidx[:, 2 * tt + 1:2 * tt + 2], None, ALU.is_equal)
            link(ins_)
            for tt in range(TT):
                ins_ = dve.tensor_scalar(wgt[:, tt, 0:EXPERTS], hot[:, tt, :], w1[:, tt:tt + 1], None, ALU.mult)
            link(ins_)
            for tt in range(TT):
                ins_ = dve.scalar_tensor_tensor(wgt[:, tt, 0:EXPERTS], hot2[:, tt, :], w2[:, tt:tt + 1],
                                                wgt[:, tt, 0:EXPERTS], ALU.mult, ALU.add)
            dve.tensor_tensor(hot[:, :, :], hot[:, :, :], hot2[:, :, :], ALU.add).then_inc(hot_ready, 1)
            dve.wait_ge(hot_ready, 1)
            split_turned(1, G_MEM2 + 8)
            dve.wait_ge(pos_done, 1)
            for tt in range(TT):
                ins_ = dve.scalar_tensor_tensor(posm[:, tt, 0:EXPERTS], ps[5][:, 32 * tt:32 * tt + 32], 1.0, hot[:, tt, :],
                                                ALU.add, ALU.mult)
            link(ins_)
            link(dve.tensor_scalar(posm[:, :, 0:EXPERTS], posm[:, :, 0:EXPERTS], -1.0, None, ALU.add))
            link(dve.tensor_reduce(tmax, ps[5][:, 64:96], AX, ALU.max))
            link(dve.tensor_scalar(thr, cst[:, C_THR:C_THR + 8], tmax, None, ALU.is_lt))
            link(dve.tensor_reduce(extra_f, thr, AX, ALU.add))
            dve.tensor_copy(extra_i[:, :], extra_f).then_inc(extra_ready, 1)

            def select(g, s):
                for tt in range(TT):
                    at_ = posm[:, tt, bass.ds(g * EG, EG)]
                    ins_ = dve.tensor_tensor(sel[:, tt, :].rearrange("p (e s) -> p e s", e=EG),
                                             at_.unsqueeze(2).broadcast_to([P, EG, SLOTS]),
                                             slot_row.unsqueeze(1).broadcast_to([P, EG, SLOTS]), ALU.is_equal)
                ins_.then_inc(s, 1)

            def hidden(s, count):
                dve.wait_ge(s["silu"], count)
                dve.tensor_tensor(e_h, e_silu, ps[4][:, P:2 * P], ALU.mult).then_inc(s["hm"], 1)
                dve.wait_ge(s["ht_full"], count)
                dve.tensor_copy(e_ht, ps[4][:, 256:384]).then_inc(s["ht"], 1)

            def expert_out(s, halves):
                dve.wait_ge(s["y_full"], halves)
                dve.tensor_copy(y_sb[:, 512:1024], ps[7][:, :]).then_inc(s["y1"], 1)

            select(0, main["sel"])
            for layer in range(2):
                c = mem2_at + 2 * layer
                head_norm(c, k2_t[layer], HG_MK + layer)
                copy_out(c + 1, v2_a[layer])
            with dve.Fori(0, EXPERTS // EG) as g:
                dve.wait_ge(main["sel"], g + 1)
                for tt in range(TT):
                    one = sel[:, tt, :].rearrange("p (e s) -> p e s", e=EG)
                    share = wgt[:, tt, bass.ds(g * EG, EG)].unsqueeze(2).broadcast_to([P, EG, SLOTS])
                    for rep in range(4):
                        dst = selw[:, tt, :].rearrange("p (e r s) -> p e r s", e=EG, r=4)[:, :, rep, :]
                        ins_ = dve.tensor_tensor(dst, one, share, ALU.mult)
                ins_.then_inc(main["selw"], 1)
                dve.wait_ge(main["selw"], g + 1)
                dve.wait_ge(main["fill"], 4 * g + 2)
                select(g + 1, main["sel"])
                for e in range(EG):
                    hidden(main, 4 * g + e + 1)
                    expert_out(main, 8 * g + 2 * e + 2)
            extra = dve.value_load(extra_i[0:1, 0:1], min_val=0, max_val=MAX_ROUNDS - 1)
            with dve.If(extra > 0):
                with dve.Fori(0, extra) as r:
                    dve.wait_ge(over["spread"], EXPERTS * r + 1)
                    dve.tensor_scalar(posm[:, :, 0:EXPERTS], posm[:, :, 0:EXPERTS], -float(SLOTS), None,
                                      ALU.add).then_inc(over["sel"], 1)
                    dve.wait_ge(over["sel"], EXPERTS * r + r + 1)
                    dve.tensor_copy(bn2[:, 0:1], posm[:, 0, 0:1])
                    with dve.Fori(0, EXPERTS) as x:
                        step = EXPERTS * r + x + 1
                        dve.wait_ge(over["spread"], step)
                        for tt in range(TT):
                            ins_ = dve.tensor_scalar(sel[:, tt, 0:SLOTS], slot_row, posm[:, tt, bass.ds(x, 1)], None,
                                                     ALU.is_equal)
                        ins_.then_inc(over["sel"], 1)
                        dve.wait_ge(over["sel"], EXPERTS * r + r + x + 2)
                        for tt in range(TT):
                            for rep in range(4):
                                ins_ = dve.tensor_scalar(selw[:, tt, rep * SLOTS:rep * SLOTS + SLOTS], sel[:, tt, 0:SLOTS],
                                                         wgt[:, tt, bass.ds(x, 1)], None, ALU.mult)
                        ins_.then_inc(over["selw"], 1)
                        hidden(over, step)
                        expert_out(over, 2 * step)

            dve.wait_ge(moe_done, 1)
            n["moe"] = True
            for tt in range(TT):
                for half in range(2):
                    dst = h[:, tt, half * 512:half * 512 + 512]
                    ins_ = dve.tensor_tensor(dst, dst, ps[2 * tt + half][:, :], ALU.add)
                ins_.then_inc(h_added, 1)
            split_to(moe_at + 1)
            dve.wait_ge(h_added, 2)
            row_scale()
            dve.wait_ge(in_final, 16)
            for tt in range(TT):
                ins_ = dve.scalar_tensor_tensor(h[:, tt, :], h[:, tt, :], rstd[:, tt:tt + 1], gain_b, ALU.mult, ALU.mult)
                ins_.then_inc(h_tile if tt == 0 else h_ready, 1)
            dve.wait_ge(h_ready, 3)

            def rope(qk):
                dve.wait_ge(rot_done, n["rot"] + 1)
                half_turned = prob_t[:, 0, :].rearrange("p (a b) -> p a b", a=2)
                for j in range(2):
                    dve.tensor_tensor(half_turned[:, j, :], ps[6][:, j * TOK:j * TOK + TOK], sin_t, ALU.mult)
                    ins_ = dve.tensor_tensor(qk[:, j, :], qk[:, j, :], cos_t, ALU.mult)
                link(ins_)
                dve.tensor_tensor(qk, qk, half_turned, ALU.add).then_inc(rope_done, 1)
                n["rot"] += 1

            def swiglu(q):
                s, b = ffn_starts[q], FT * q
                split_to(s + 3)

                def hidden_tile(i, j):
                    dve.wait_ge(silu_ready, 2 * i + (b + j + 1))
                    dve.tensor_tensor(f_prod[:, j, :], f_silu[:, j, :], ps[4 + j][:, TOK:2 * TOK], ALU.mult).then_inc(prod_ready, 1)
                    dve.wait_ge(prod_ready, 2 * i + (b + j + 1))
                    dve.tensor_copy(hh_hi[:, j, :], f_prod[:, j, :]).then_inc(hhi_ready, 1)
                    dve.wait_ge(hhi_ready, 2 * i + (b + j + 1))
                    dve.tensor_tensor(hh_lo[:, j, :], f_prod[:, j, :], hh_hi[:, j, :].bitcast(F32),
                                      ALU.subtract).then_inc(hlo_ready, 1)

                with dve.Fori(0, PAIRS // 2) as it:
                    for half in range(2):
                        for j in range(3):
                            c0_ = s + 3 * half + 3 + j
                            dve.wait_ge(hi_ready, 6 * it + (c0_ + 1))
                            dve.tensor_tensor(wlo[:, c0_ % SPLIT, :], raw[:, c0_ % RAW, :],
                                              whi[:, c0_ % SPLIT, :].bitcast(F32), ALU.subtract).then_inc(lo_ready, 1)
                            if j == 0:
                                hidden_tile(2 * it + half, 0)
                                hidden_tile(2 * it + half, 1)
                n["chunk"] = s + 3 * PAIRS
                cb = s + 3 * (PAIRS - 1)
                split_to(cb + 4)
                hidden_tile(PAIRS - 1, 0)
                hidden_tile(PAIRS - 1, 1)
                split_to(cb + 5)
                for tt in range(TT):
                    if tt == 0:
                        dve.wait_ge(ffn_half, q + 1)
                    else:
                        dve.wait_ge(chunk_used, s + 3 * PAIRS)
                    for half in range(2):
                        dst = h[:, tt, half * 512:half * 512 + 512]
                        ins_ = dve.scalar_tensor_tensor(dst, ps[2 * tt + half][:, :], 0.5, dst, ALU.mult, ALU.add)
                    ins_.then_inc(h_tile if tt == 0 else h_ready, 1)
                dve.wait_ge(h_ready, (4, 6, 7, 9)[q])

            normed_rows(h)
            split_turned(1, G_FFN1)
            swiglu(0)
            normed_rows(h)
            split_turned(0, G_MIX2)
            c0 = ffn_starts[0] + 3 * PAIRS
            dve.memset(conv_in[:, :, 0:CONV_TAPS - 1], 0.0)
            taps_left = [(first + t, j) for first, j0 in ((0, 0), (2, PE_TAPS)) for j in range(j0, CONV_TAPS) for t in range(2)]
            n_taps = len(taps_left)

            def tap(times):
                for _ in range(min(times, len(taps_left))):
                    done = n_taps - len(taps_left)
                    ct, j = taps_left.pop(0)
                    w_j = cols[:, G_DW + 6 * j + ct:G_DW + 6 * j + ct + 1]
                    if j == (0, PE_TAPS)[ct // 2]:
                        ins_ = dve.tensor_scalar(conv_out[:, ct, :], conv_in[:, ct, j:j + TOK], w_j,
                                                 cols[:, G_DWB + ct:G_DWB + ct + 1], ALU.mult, ALU.add)
                    else:
                        dve.wait_ge(tap_done, done - 1)
                        ins_ = dve.scalar_tensor_tensor(conv_out[:, ct, :], conv_in[:, ct, j:j + TOK], w_j,
                                                        conv_out[:, ct, :], ALU.mult, ALU.add)
                    ins_.then_inc(tap_done, 1)

            for i in range(3):
                for c in range(c0 + 2 * i + 2, c0 + 2 * i + 4):
                    split_to(c)
                    if i >= 1:
                        tap(8)
                split_to(c0 + 2 * i + 4)
                dve.wait_ge(sig_ready, i + 1)
                dve.tensor_tensor(conv_in[:, 2 * i:2 * i + 2, CONV_TAPS - 1:], sig, bank_rows(c0 + 2 * i), ALU.mult).then_inc(glu_done, 1)
                dve.wait_ge(glu_done, i + 1)
                dve.tensor_copy(bn2[:, 0:1], rstd[:, 0:1]).then_inc(evac_v, 1)
                dve.tensor_copy(bn2[:, 2:3], rstd[:, 0:1]).then_inc(evac_v, 1)
            split_to(c0 + 9)
            tap(8)
            head_norm(c0 + 6, qm_t[0], HG_MQ)

            def attend(widths, x, tiles, beside=None):
                unit, head = n["unit"], n["unit"] - 4
                for s in range(len(widths) + 4):
                    if s < len(widths):
                        if widths[s] == CAUSAL_W:
                            causal_max(cst[:, C_CAUSAL:C_CAUSAL + CAUSAL_W], 0.125, 1.0)
                        else:
                            full_max(0.125)
                    if 1 <= s < len(widths) + 1:
                        probs(unit + s - 1, widths[s - 1])
                    if s >= 5 and s % 2:
                        out_lo(x, tiles[(s - 5) // 2], 1, head + s - 4)
                    if beside is not None:
                        beside(s)

            attend([512] * 4, 1, (6, 7), lambda step: tap(10))
            dve.wait_ge(diag_used, len([1 for _, tile in TAP_GROUPS if tile == 4]))
            for t in range(2):
                ins_ = dve.tensor_scalar(conv_out[:, 4 + t, :], linear_bank(c0 + 7)[:, t * TOK:t * TOK + TOK],
                                         cols[:, G_DWB + 4 + t:G_DWB + 5 + t], None, ALU.add)
            ins_.then_inc(conv_ready, 1)
            tap(len(taps_left))
            dve.wait_ge(diag_used, len(TAP_GROUPS))
            dve.wait_ge(tap_done, n_taps)
            dve.tensor_tensor(conv_out[:, 2:4, :], conv_out[:, 2:4, :],
                              linear_bank(c0 + 6)[:, :].rearrange("p (t n) -> p t n", t=2), ALU.add).then_inc(conv_ready, 1)
            dve.wait_ge(conv_ready, 2)
            dve.wait_ge(cmu_ready, 1)
            for ct in range(CONV_TILES):
                dve.tensor_tensor(conv_out[:, ct, :], conv_out[:, ct, :], prob[:, 0, 0:TOK], ALU.subtract).then_inc(cent_ready, 1)
            dve.wait_ge(csum_done, 2)
            dve.tensor_scalar(prob[:, 1, 0:TOK], ps[7][:, 0:TOK], 1.0 / 768, RMS_EPS, ALU.mult, ALU.add).then_inc(cms_ready, 1)
            dve.wait_ge(crt_ready, 1)
            link(dve.reciprocal(prob[:, 1, 0:TOK], prob[:, 0, 0:TOK]))
            for ct in range(CONV_TILES):
                dve.tensor_tensor(conv_out[:, ct, :], conv_out[:, ct, :], prob[:, 1, 0:TOK], ALU.mult).then_inc(cn_ready, 1)
            for ct in range(CONV_TILES):
                dve.wait_ge(chi_ready, ct + 1)
                dve.tensor_tensor(xlo[1][:, ct, :], conv_sq[:, ct, :], xhi[1][:, ct, :].bitcast(F32),
                                  ALU.subtract).then_inc(clo_ready, 1)
            for j in range(4):
                add_to_h(c0 + 7 + j, j)
                split_to(min(c0 + 10 + j + 1, c0 + 13))
            n["last_h"] = c0 + 10
            h_updated()
            normed_rows(h)
            split_turned(0, G_FFN2)
            swiglu(1)
            normed_rows(h)
            split_turned(1, G_KV)
            c0 = ffn_starts[1] + 3 * PAIRS
            split_turned(0, G_FFN1 + 8)
            for i in range(3):
                split_to(c0 + i + 4)
                head_norm(c0 + i, kb_t[:, 2 * i:2 * i + 2, :], HG_K)
                if i >= 1:
                    rope(kb_t[:, 2 * i - 2:2 * i, :])
            for i in range(3):
                split_to(c0 + i + 7)
                if i == 1:
                    rope(kb_t[:, 4:6, :])
            swiglu(2)
            normed_rows(h)
            split_turned(1, G_MIX2 + 8)
            c0 = ffn_starts[2] + 3 * PAIRS
            split_to(c0 + 4)
            head_norm(c0, qm_t[1], HG_MQ + 1)
            split_to(c0 + 5)
            head_norm(c0 + 1, qb_t[:, 0:2, :], HG_Q)
            split_to(c0 + 6)
            rope(qb_t[:, 0:2, :])
            head_norm(c0 + 2, qb_t[:, 2:4, :], HG_Q)

            def beside_heads(step):
                if step == 0:
                    rope(qb_t[:, 2:4, :])
                    head_norm(c0 + 3, qb_t[:, 4:6, :], HG_Q)
                    split_to(c0 + 7)
                if step == 1:
                    rope(qb_t[:, 4:6, :])

            attend([CAUSAL_W] * 12 + [512] * 4, 0, range(8), beside_heads)
            for j in range(4):
                add_to_h(c0 + 4 + j, j)
                split_to(min(c0 + 7 + j + 1, c0 + 10))
            n["last_h"] = c0 + 7
            h_updated()
            normed_rows(h)
            split_turned(1, G_FFN2 + 8)
            swiglu(3)


_INS = ['x', 'mem', 'norm_mix', 'w_in', 'sgu_ln_g', 'sgu_ln_b', 'sgu_w', 'sgu_b', 'lambda_q1', 'lambda_k1', 'lambda_q2',
        'lambda_k2', 'diff_subln', 'w_out', 'norm_xq', 'norm_mem', 'w_q_mem', 'w_kv_mem', 'w_o_mem', 'norm_ffn',
        'w_router_group', 'b_router_group', 'w_router_expert', 'b_router_expert', 'w_gate', 'w_up', 'w_down',
        'norm_final', 'mem_2', 'positions_2', 'ffn1_norm_g_2', 'ffn1_w_gate_2', 'ffn1_w_up_2', 'ffn1_w_down_2',
        'mix_norm_g_2', 'mem_norm_g_2', 'w_mem_kv_2', 'mem_q_norm_g_2', 'mem_k_norm_g_2', 'w_o_2', 'ffn2_norm_g_2',
        'ffn2_w_gate_2', 'ffn2_w_up_2', 'ffn2_w_down_2', 'a_w_in_2', 'a_dw_kernel_2', 'a_dw_bias_2', 'a_ln_g_2',
        'a_ln_b_2', 'kv_norm_g_2', 'w_kv_2', 'k_norm_g_2', 'b_w_in_2', 'b_q_norm_g_2']
_OUT = ((1, TOK, D), 'float32')


def kernel(**inputs):
    import concourse.bacc as _bacc
    from concourse.bass_utils import run_bass_kernel_spmd as _run

    nc = _bacc.Bacc("TRN2", target_bir_lowering=False, num_devices=1)
    arrays, ins = {}, {}
    for name in _INS:
        a = np.ascontiguousarray(inputs[name])
        arrays[f"in_{name}_dram"] = a
        ins[name] = nc.dram_tensor(f"in_{name}_dram", a.shape, mybir.dt.from_np(a.dtype), kind="ExternalInput").ap()
    arrays["shape_constants"] = shape_constants()
    consts = nc.dram_tensor("shape_constants", (P, C_END), F32, kind="ExternalInput").ap()
    out = nc.dram_tensor("out_0_dram", _OUT[0], F32, kind="ExternalOutput").ap()
    build(nc, ins, consts, out)
    r = _run(nc, [arrays], core_ids=[0])
    return r.results[0]["out_0_dram"]
```
